# Optimizing a Trainium2 kernel written in Bass

```python
import jax, jax.numpy as jnp
from jax import lax
import numpy as np

D_MODEL = 1024
BATCH = 1
SEQ = 256
DEPTH = 2

D_NSA = 512
D_LRU = 512
D_CONV = 512
D_MIX = D_NSA + D_LRU + D_CONV
HEAD_DIM = 64
N_HEADS = D_NSA // HEAD_DIM
N_KV = 2
N_REP = N_HEADS // N_KV
KV_W = N_KV * HEAD_DIM
L_CMP = 32
S_CMP = 16
CMP_HIDDEN = 256
L_SLC = 64
K_SEL = 16
WINDOW = 512
Q_BLOCK = 128
N_BRANCH = 3
ROPE_THETA = 10000.0
LRU_BLOCKS = 8
LRU_BLOCK_W = D_LRU // LRU_BLOCKS
LRU_CONV = 4
LRU_C = 8.0
CONV_K = 31
EPS = 1e-6
NEG = -1e30
FORCE = 1e4
COL_SIZES = (D_NSA, KV_W, KV_W, KV_W, KV_W, KV_W, KV_W, N_HEADS * N_BRANCH,
             D_NSA, D_LRU, D_LRU, D_CONV, D_CONV, D_CONV)
N_IN = D_NSA * 2 + KV_W * 6 + N_HEADS * N_BRANCH + D_LRU * 2 + D_CONV * 3


def split_points():
    return [int(v) for v in np.cumsum(COL_SIZES)[:-1]]

def rms_norm(x, g):
    xf = x.astype(jnp.float32)
    y = xf * lax.rsqrt(jnp.mean(xf * xf, axis=-1, keepdims=True) + EPS)
    return (y * g.astype(jnp.float32)).astype(x.dtype)

def rope_tables(positions):
    inv_freq = ROPE_THETA ** (-jnp.arange(0, HEAD_DIM, 2, dtype=jnp.float32) / HEAD_DIM)
    ang = positions.astype(jnp.float32)[..., None] * inv_freq
    return jnp.cos(ang)[:, :, None, :], jnp.sin(ang)[:, :, None, :]

def apply_rope(u, cos, sin):
    uf = u.astype(jnp.float32)
    u1, u2 = jnp.split(uf, 2, axis=-1)
    out = jnp.concatenate([u1 * cos - u2 * sin, u2 * cos + u1 * sin], axis=-1)
    return out.astype(u.dtype)

def causal_dwconv(u, w, b):
    k = w.shape[0]
    c = u.shape[-1]
    y = lax.conv_general_dilated(u, w[:, None, :].astype(u.dtype), window_strides=(1,),
                                 padding=[(k - 1, 0)], dimension_numbers=('NWC', 'WIO', 'NWC'),
                                 feature_group_count=c)
    return y + b

def nsa_attention(q, k_c, v_c, k_s, v_s, k_w, v_w, gates, cmp_pos, cmp_w1, cmp_w2):
    B, T = q.shape[0], q.shape[1]
    qg = q.reshape(B, T, N_KV, N_REP, HEAD_DIM).transpose(0, 2, 3, 1, 4)
    tr = lambda a: a.transpose(0, 2, 1, 3)
    k_c, v_c, k_s, v_s, k_w, v_w = tr(k_c), tr(v_c), tr(k_s), tr(v_s), tr(k_w), tr(v_w)

    n_cmp = (T - L_CMP) // S_CMP + 1
    cmp_start = jnp.arange(n_cmp) * S_CMP
    idx = cmp_start[:, None] + jnp.arange(L_CMP)[None, :]

    def compress(kv, pos, w1, w2):
        blk = (kv[:, :, idx] + pos).reshape(B, N_KV, n_cmp, L_CMP * HEAD_DIM)
        return jax.nn.silu(blk @ w1) @ w2

    kc = compress(k_c, cmp_pos[0], cmp_w1[0], cmp_w2[0])
    vc = compress(v_c, cmp_pos[1], cmp_w1[1], cmp_w2[1])
    cmp_end = cmp_start + L_CMP - 1

    n_sel = T // L_SLC
    k_sel = min(K_SEL, n_sel)
    sel_start = jnp.arange(n_sel) * L_SLC
    overlap = ((cmp_start[:, None] < sel_start[None, :] + L_SLC) &
               (cmp_start[:, None] + L_CMP > sel_start[None, :])).astype(jnp.float32)
    ks_blk = k_s.reshape(B, N_KV, n_sel, L_SLC, HEAD_DIM)
    vs_blk = v_s.reshape(B, N_KV, n_sel, L_SLC, HEAD_DIM)
    bi = jnp.arange(B)[:, None, None, None]
    gi = jnp.arange(N_KV)[None, :, None, None]
    sel_j = jnp.arange(n_sel)

    pad = ((0, 0), (0, 0), (WINDOW, 0), (0, 0))
    kw_pad = jnp.pad(k_w, pad)
    vw_pad = jnp.pad(v_w, pad)
    scale = HEAD_DIM ** -0.5

    def block(i):
        s = i * Q_BLOCK
        qb = lax.dynamic_slice_in_dim(qg, s, Q_BLOCK, axis=3)
        t = s + jnp.arange(Q_BLOCK)
        sc = jnp.einsum('bgrqd,bgnd->bgrqn', qb, kc).astype(jnp.float32) * scale
        mc = cmp_end[None, :] <= t[:, None]
        pc = jnp.where(mc, jax.nn.softmax(jnp.where(mc, sc, NEG), axis=-1), 0.0)
        o_c = jnp.einsum('bgrqn,bgnd->bgrqd', pc.astype(vc.dtype), vc)
        imp = jnp.einsum('bgrqn,ns->bgqs', pc, overlap)
        cur = t // L_SLC
        forced = ((sel_j[None, :] == 0) | (sel_j[None, :] == cur[:, None]) |
                  (sel_j[None, :] == cur[:, None] - 1))
        valid = sel_start[None, :] <= t[:, None]
        score = jnp.where(forced, FORCE, jnp.where(valid, imp, -1.0))
        top_v, top_i = lax.top_k(score, k_sel)
        ok = top_v >= 0.0
        kg = ks_blk[bi, gi, top_i]
        vg = vs_blk[bi, gi, top_i]
        ss = jnp.einsum('bgrqd,bgqkld->bgrqkl', qb, kg).astype(jnp.float32) * scale
        tok = top_i[..., None] * L_SLC + jnp.arange(L_SLC)
        ms = (ok[..., None] & (tok <= t[None, None, :, None, None]))[:, :, None]
        ss = jnp.where(ms, ss, NEG).reshape(B, N_KV, N_REP, Q_BLOCK, k_sel * L_SLC)
        ps = jax.nn.softmax(ss, axis=-1).reshape(B, N_KV, N_REP, Q_BLOCK, k_sel, L_SLC)
        o_s = jnp.einsum('bgrqkl,bgqkld->bgrqd', ps.astype(vg.dtype), vg)
        kw = lax.dynamic_slice_in_dim(kw_pad, s, WINDOW + Q_BLOCK, axis=2)
        vw = lax.dynamic_slice_in_dim(vw_pad, s, WINDOW + Q_BLOCK, axis=2)
        pos = s - WINDOW + jnp.arange(WINDOW + Q_BLOCK)
        mw = ((pos[None, :] <= t[:, None]) & (pos[None, :] > t[:, None] - WINDOW) &
              (pos[None, :] >= 0))
        sw = jnp.einsum('bgrqd,bgkd->bgrqk', qb, kw).astype(jnp.float32) * scale
        pw = jax.nn.softmax(jnp.where(mw, sw, NEG), axis=-1)
        o_w = jnp.einsum('bgrqk,bgkd->bgrqd', pw.astype(vw.dtype), vw)
        return o_c, o_s, o_w

    o_c, o_s, o_w = lax.map(block, jnp.arange(T // Q_BLOCK))

    def unblock(o):
        return o.transpose(1, 0, 4, 2, 3, 5).reshape(B, T, N_KV, N_REP, HEAD_DIM)

    g = gates.reshape(B, T, N_KV, N_REP, N_BRANCH)
    out = g[..., 0:1] * unblock(o_c) + g[..., 1:2] * unblock(o_s) + g[..., 2:3] * unblock(o_w)
    return out.reshape(B, T, D_NSA)

def rg_lru(u, conv_w, conv_b, w_a, b_a, w_i, b_i, lam):
    B, T, C = u.shape
    xc = causal_dwconv(u, conv_w, conv_b)
    xh = xc.reshape(B, T, LRU_BLOCKS, LRU_BLOCK_W)
    r = jax.nn.sigmoid(jnp.einsum('bthi,hij->bthj', xh, w_a).reshape(B, T, C) + b_a)
    ig = jax.nn.sigmoid(jnp.einsum('bthi,hij->bthj', xh, w_i).reshape(B, T, C) + b_i)
    log_a = -LRU_C * r.astype(jnp.float32) * jax.nn.softplus(-lam.astype(jnp.float32))
    a = jnp.exp(log_a)
    bterm = jnp.sqrt(-jnp.expm1(2.0 * log_a)) * (ig * xc).astype(jnp.float32)

    def combine(left, right):
        a1, b1 = left
        a2, b2 = right
        return a1 * a2, a2 * b1 + b2

    _, h = lax.associative_scan(combine, (a, bterm), axis=1)
    return h.astype(u.dtype)

def conformer_conv(ga, gb, dw_w, dw_b, ln_g, ln_b, w_pw2):
    u = ga * jax.nn.sigmoid(gb)
    u = causal_dwconv(u, dw_w, dw_b)
    uf = u.astype(jnp.float32)
    mu = jnp.mean(uf, axis=-1, keepdims=True)
    var = jnp.mean(jnp.square(uf - mu), axis=-1, keepdims=True)
    un = (uf - mu) * lax.rsqrt(var + EPS) * ln_g.astype(jnp.float32) + ln_b.astype(jnp.float32)
    return jax.nn.silu(un).astype(u.dtype) @ w_pw2

def first_inputs(seed: int = 0) -> dict:
    key = jax.random.key(seed)
    ks = jax.random.split(key, 24)
    f32 = jnp.float32
    nrm = lambda k, shape, s: jax.random.normal(k, shape, f32) * s
    u = jax.random.uniform(ks[13], (DEPTH, D_LRU), f32, 0.9, 0.999)
    sg = u ** (1.0 / LRU_C)
    lam = jnp.log(sg / (1.0 - sg))
    return {
        "x": jax.random.normal(ks[0], (BATCH, SEQ, D_MODEL), f32),
        "positions": jnp.broadcast_to(jnp.arange(SEQ, dtype=jnp.int32), (BATCH, SEQ)),
        "norm_g": 1.0 + nrm(ks[1], (DEPTH, D_MODEL), 0.02),
        "w_in": nrm(ks[2], (DEPTH, D_MODEL, N_IN), D_MODEL ** -0.5),
        "b_gate": nrm(ks[3], (DEPTH, N_HEADS * N_BRANCH), 0.02),
        "cmp_pos": nrm(ks[4], (DEPTH, 2, L_CMP, HEAD_DIM), 0.02),
        "cmp_w1": nrm(ks[5], (DEPTH, 2, L_CMP * HEAD_DIM, CMP_HIDDEN), (L_CMP * HEAD_DIM) ** -0.5),
        "cmp_w2": nrm(ks[6], (DEPTH, 2, CMP_HIDDEN, HEAD_DIM), CMP_HIDDEN ** -0.5),
        "lru_conv_w": nrm(ks[7], (DEPTH, LRU_CONV, D_LRU), LRU_CONV ** -0.5),
        "lru_conv_b": nrm(ks[8], (DEPTH, D_LRU), 0.02),
        "lru_w_a": nrm(ks[9], (DEPTH, LRU_BLOCKS, LRU_BLOCK_W, LRU_BLOCK_W), LRU_BLOCK_W ** -0.5),
        "lru_b_a": nrm(ks[10], (DEPTH, D_LRU), 0.02),
        "lru_w_i": nrm(ks[11], (DEPTH, LRU_BLOCKS, LRU_BLOCK_W, LRU_BLOCK_W), LRU_BLOCK_W ** -0.5),
        "lru_b_i": nrm(ks[12], (DEPTH, D_LRU), 0.02),
        "lru_lam": lam,
        "conv_dw_w": nrm(ks[14], (DEPTH, CONV_K, D_CONV), CONV_K ** -0.5),
        "conv_dw_b": nrm(ks[15], (DEPTH, D_CONV), 0.02),
        "conv_ln_g": 1.0 + nrm(ks[16], (DEPTH, D_CONV), 0.02),
        "conv_ln_b": nrm(ks[17], (DEPTH, D_CONV), 0.02),
        "conv_w_pw2": nrm(ks[18], (DEPTH, D_CONV, D_CONV), D_CONV ** -0.5),
        "w_out": nrm(ks[19], (DEPTH, D_MIX, D_MODEL), D_MIX ** -0.5),
        "final_g": 1.0 + nrm(ks[20], (D_MODEL,), 0.02),
    }

def first_block(x, positions, norm_g, w_in, b_gate, cmp_pos, cmp_w1, cmp_w2, lru_conv_w, lru_conv_b,
              lru_w_a, lru_b_a, lru_w_i, lru_b_i, lru_lam, conv_dw_w, conv_dw_b, conv_ln_g, conv_ln_b,
              conv_w_pw2, w_out, final_g):
    B, T = x.shape[0], x.shape[1]
    cos, sin = rope_tables(positions)
    for l in range(DEPTH):
        h = rms_norm(x, norm_g[l])
        proj = h @ w_in[l]
        (q, k_c, v_c, k_s, v_s, k_w, v_w, g_lin, z_nsa, u_lru, z_lru, glu_a, glu_b,
         z_conv) = jnp.split(proj, split_points(), axis=-1)
        kvr = lambda a: a.reshape(B, T, N_KV, HEAD_DIM)
        q = apply_rope(q.reshape(B, T, N_HEADS, HEAD_DIM), cos, sin)
        k_c = apply_rope(kvr(k_c), cos, sin)
        k_s = apply_rope(kvr(k_s), cos, sin)
        k_w = apply_rope(kvr(k_w), cos, sin)
        gates = jax.nn.sigmoid(g_lin + b_gate[l]).reshape(B, T, N_HEADS, N_BRANCH)
        y_nsa = nsa_attention(q, k_c, kvr(v_c), k_s, kvr(v_s), k_w, kvr(v_w), gates,
                              cmp_pos[l], cmp_w1[l], cmp_w2[l])
        y_lru = rg_lru(u_lru, lru_conv_w[l], lru_conv_b[l], lru_w_a[l], lru_b_a[l],
                       lru_w_i[l], lru_b_i[l], lru_lam[l])
        y_conv = conformer_conv(glu_a, glu_b, conv_dw_w[l], conv_dw_b[l], conv_ln_g[l],
                                conv_ln_b[l], conv_w_pw2[l])
        mixed = jnp.concatenate([y_nsa * jax.nn.silu(z_nsa), y_lru * jax.nn.silu(z_lru),
                                 y_conv * jax.nn.silu(z_conv)], axis=-1)
        x = x + mixed @ w_out[l]
    return rms_norm(x, final_g)


DEPTH_2 = 1

GRID_W = 64
CTX_LEN = 256
N_MOD = 6
MLA_HEADS = 4
MLA_Q_RANK = 256
MLA_KV_RANK = 128
MLA_NOPE = 128
MLA_ROPE = 64
MLA_V = 128
MLA_QK = MLA_NOPE + MLA_ROPE
ROPE_AXIS = MLA_ROPE // 2
ROPE_BASE = 10000.0
ML_HEADS = 4
ML_QK = 64
ML_V = 128
ML_CHUNK = 64
CONV_W = 3
FGATE_BIAS_LO = 3.0
FGATE_BIAS_HI = 6.0
MLA_COLS = MLA_Q_RANK + MLA_KV_RANK + MLA_ROPE
ML_COLS = 2 * ML_HEADS * ML_QK + 2 * ML_HEADS * ML_V + 4 * ML_HEADS
IN_COLS = MLA_COLS + ML_COLS
MIX_WIDTH = MLA_HEADS * MLA_V + ML_HEADS * ML_V
PEER_HEADS = 8
N_KEYS = 128
N_EXPERTS = N_KEYS * N_KEYS
PEER_DK = 256
PEER_DKH = PEER_DK // 2
PEER_TOPK = 16
PEER_BLOCK = 128


def rmsnorm(x, g):
    xf = x.astype(jnp.float32)
    y = xf * lax.rsqrt(jnp.mean(xf * xf, axis=-1, keepdims=True) + EPS)
    return (y * g.astype(jnp.float32)).astype(x.dtype)

def rope_tables_2(rows):
    row = jnp.repeat(jnp.arange(rows, dtype=jnp.float32), GRID_W)
    col = jnp.tile(jnp.arange(GRID_W, dtype=jnp.float32), rows)
    inv = ROPE_BASE ** (-jnp.arange(ROPE_AXIS // 2, dtype=jnp.float32) * (2.0 / ROPE_AXIS))
    ang_r = row[:, None] * inv
    ang_c = col[:, None] * inv
    return (jnp.cos(ang_r), jnp.sin(ang_r), jnp.cos(ang_c), jnp.sin(ang_c))

def rotate(t, cos, sin):
    half = t.shape[-1] // 2
    t1, t2 = t[..., :half], t[..., half:]
    cos = cos.astype(t.dtype)
    sin = sin.astype(t.dtype)
    return jnp.concatenate([t1 * cos - t2 * sin, t2 * cos + t1 * sin], axis=-1)

def apply_rope2d(t, rope):
    cos_r, sin_r, cos_c, sin_c = rope
    t_row = rotate(t[..., MLA_NOPE:MLA_NOPE + ROPE_AXIS], cos_r, sin_r)
    t_col = rotate(t[..., MLA_NOPE + ROPE_AXIS:], cos_c, sin_c)
    return jnp.concatenate([t[..., :MLA_NOPE], t_row, t_col], axis=-1)

def split_heads(t, n_heads):
    b, n, _ = t.shape
    return t.reshape(b, n, n_heads, -1).transpose(0, 2, 1, 3)

def merge_heads(t):
    b, h, n, d = t.shape
    return t.transpose(0, 2, 1, 3).reshape(b, n, h * d)

def mla_prep(cols, g_cq, w_uq, g_ckv, w_ukv, g_qn, g_kn, rope):
    b, n, _ = cols.shape
    c_q = cols[..., :MLA_Q_RANK]
    c_kv = cols[..., MLA_Q_RANK:MLA_Q_RANK + MLA_KV_RANK]
    k_rope = cols[..., MLA_Q_RANK + MLA_KV_RANK:]
    q = (rmsnorm(c_q, g_cq) @ w_uq).reshape(b, n, MLA_HEADS, MLA_QK)
    kv = (rmsnorm(c_kv, g_ckv) @ w_ukv).reshape(b, n, MLA_HEADS, MLA_NOPE + MLA_V)
    k = jnp.concatenate([kv[..., :MLA_NOPE],
                         jnp.broadcast_to(k_rope[:, :, None, :], (b, n, MLA_HEADS, MLA_ROPE))], axis=-1)
    v = kv[..., MLA_NOPE:].transpose(0, 2, 1, 3)
    q = rmsnorm(q, g_qn).transpose(0, 2, 1, 3)
    k = rmsnorm(k, g_kn).transpose(0, 2, 1, 3)
    if rope is not None:
        q = apply_rope2d(q, rope)
        k = apply_rope2d(k, rope)
    return q, k, v

def attend(q, k, v):
    s = jnp.einsum('bhqd,bhkd->bhqk', q, k).astype(jnp.float32) * (MLA_QK ** -0.5)
    p = jax.nn.softmax(s, axis=-1).astype(v.dtype)
    return jnp.einsum('bhqk,bhkd->bhqd', p, v)

def attend_blocked(q, k, v):
    b, h, n, dk = q.shape
    nb = n // Q_BLOCK
    qb = jnp.moveaxis(q.reshape(b, h, nb, Q_BLOCK, dk), 2, 0)
    ob = lax.map(lambda q_blk: attend(q_blk, k, v), qb)
    return jnp.moveaxis(ob, 0, 2).reshape(b, h, n, -1)

def mla_mixer(cols_lat, cols_ctx, g_cq, w_uq, g_ckv, w_ukv, g_qn, g_kn, rope, need_ctx_out):
    q_l, k_l, v_l = mla_prep(cols_lat, g_cq, w_uq, g_ckv, w_ukv, g_qn, g_kn, rope)
    q_c, k_c, v_c = mla_prep(cols_ctx, g_cq, w_uq, g_ckv, w_ukv, g_qn, g_kn, None)
    k_all = jnp.concatenate([k_c, k_l], axis=2)
    v_all = jnp.concatenate([v_c, v_l], axis=2)
    out_lat = merge_heads(attend_blocked(q_l, k_all, v_all))
    out_ctx = merge_heads(attend(q_c, k_c, v_c)) if need_ctx_out else None
    return out_lat, out_ctx

def centred_conv(u, w):
    k = w.shape[0]
    p = k // 2
    n = u.shape[1]
    up = jnp.pad(u, ((0, 0), (p, p), (0, 0)))
    return sum(up[:, j:j + n] * w[j] for j in range(k))

def mlstm_prep(cols, conv_w, b_i, b_f):
    b, n, _ = cols.shape
    n_qk = ML_HEADS * ML_QK
    n_v = ML_HEADS * ML_V
    qk = jax.nn.silu(centred_conv(cols[..., :2 * n_qk], conv_w))
    q = split_heads(qk[..., :n_qk], ML_HEADS).astype(jnp.float32) * (ML_QK ** -0.5)
    k = split_heads(qk[..., n_qk:], ML_HEADS).astype(jnp.float32)
    v = split_heads(cols[..., 2 * n_qk:2 * n_qk + n_v], ML_HEADS).astype(jnp.float32)
    o = cols[..., 2 * n_qk + n_v:2 * n_qk + 2 * n_v]
    gates = cols[..., 2 * n_qk + 2 * n_v:].astype(jnp.float32).reshape(b, n, 2, 2, ML_HEADS)
    ig = (gates[:, :, 0] + b_i.astype(jnp.float32)).transpose(2, 0, 3, 1)
    lf = jax.nn.log_sigmoid(gates[:, :, 1] + b_f.astype(jnp.float32)).transpose(2, 0, 3, 1)
    return q, k, v, o, ig, lf

def mlstm_scan(q, k, v, ig, lf, state, need_out):
    b, h, n_tok, _ = q.shape
    nc = n_tok // ML_CHUNK

    def chunks(a):
        return jnp.moveaxis(a.reshape(a.shape[:2] + (nc, ML_CHUNK) + a.shape[3:]), 2, 0)

    tri = jnp.tril(jnp.ones((ML_CHUNK, ML_CHUNK), dtype=bool))

    def body(carry, inp):
        c_mat, n_vec, m_prev = carry
        qc, kc, vc, ic, fc = inp
        cum_f = jnp.cumsum(fc, axis=-1)
        dmat = jnp.where(tri, cum_f[..., :, None] - cum_f[..., None, :] + ic[..., None, :], -jnp.inf)
        inter = cum_f + m_prev[..., None]
        m_t = jnp.maximum(inter, jnp.max(dmat, axis=-1))
        m_new = m_t[..., -1]
        w_s = jnp.exp(dmat[..., -1, :] - m_new[..., None])
        decay = jnp.exp(inter[..., -1] - m_new)
        c_new = decay[..., None, None] * c_mat + jnp.einsum('bhs,bhsv,bhsd->bhvd', w_s, vc, kc)
        n_new = decay[..., None] * n_vec + jnp.einsum('bhs,bhsd->bhd', w_s, kc)
        if not need_out:
            return (c_new, n_new, m_new), None
        wmat = jnp.exp(dmat - m_t[..., None]) * jnp.einsum('bhtd,bhsd->bhts', qc, kc)
        scale_inter = jnp.exp(inter - m_t)
        num = jnp.einsum('bhts,bhsv->bhtv', wmat, vc) + scale_inter[..., None] * jnp.einsum('bhvd,bhtd->bhtv', c_mat, qc)
        den = jnp.sum(wmat, axis=-1) + scale_inter * jnp.einsum('bhd,bhtd->bht', n_vec, qc)
        h_out = num / jnp.maximum(jnp.abs(den), jnp.exp(-m_t))[..., None]
        return (c_new, n_new, m_new), h_out

    state, hs = lax.scan(body, state, (chunks(q), chunks(k), chunks(v), chunks(ig), chunks(lf)))
    h_seq = jnp.moveaxis(hs, 0, 2).reshape(b, h, n_tok, -1) if need_out else None
    return state, h_seq

def mlstm_output(h_sum, o, g_out):
    b, h, n, dv = h_sum.shape
    hn = rmsnorm(h_sum.transpose(0, 2, 1, 3), g_out.reshape(h, dv)).reshape(b, n, h * dv)
    return (jax.nn.sigmoid(o.astype(jnp.float32)) * hn).astype(o.dtype)

def mlstm_mixer(cols_lat, cols_ctx, conv_w, b_i, b_f, g_out, need_ctx_out):
    q_l, k_l, v_l, o_l, ig_l, lf_l = mlstm_prep(cols_lat, conv_w, b_i, b_f)
    q_c, k_c, v_c, o_c, ig_c, lf_c = mlstm_prep(cols_ctx, conv_w, b_i, b_f)
    b = q_l.shape[0]
    outs_lat, outs_ctx = [], []
    for d in range(2):
        rev = d == 1

        def fl(a):
            return jnp.flip(a, axis=2) if rev else a

        state0 = (jnp.zeros((b, ML_HEADS, ML_V, ML_QK), jnp.float32),
                  jnp.zeros((b, ML_HEADS, ML_QK), jnp.float32),
                  jnp.zeros((b, ML_HEADS), jnp.float32))
        st_ctx, h_c = mlstm_scan(fl(q_c), fl(k_c), fl(v_c), fl(ig_c[d]), fl(lf_c[d]), state0, need_ctx_out)
        _, h_l = mlstm_scan(fl(q_l), fl(k_l), fl(v_l), fl(ig_l[d]), fl(lf_l[d]), st_ctx, True)
        outs_lat.append(fl(h_l))
        if need_ctx_out:
            outs_ctx.append(fl(h_c))
    out_lat = mlstm_output(outs_lat[0] + outs_lat[1], o_l, g_out)
    out_ctx = mlstm_output(outs_ctx[0] + outs_ctx[1], o_c, g_out) if need_ctx_out else None
    return out_lat, out_ctx

def peer(h, w_pq, sub_keys, expert_u, expert_v):
    b, n, d = h.shape
    xb_all = h.reshape(-1, PEER_BLOCK, d)

    def one(xb):
        q = (xb @ w_pq).reshape(PEER_BLOCK, PEER_HEADS, 2, PEER_DKH)
        s = jnp.einsum('thpd,hpkd->thpk', q, sub_keys).astype(jnp.float32)
        sv, si = lax.top_k(s, PEER_TOPK)
        cand = (sv[:, :, 0, :, None] + sv[:, :, 1, None, :]).reshape(PEER_BLOCK, PEER_HEADS, -1)
        cidx = (si[:, :, 0, :, None] * N_KEYS + si[:, :, 1, None, :]).reshape(PEER_BLOCK, PEER_HEADS, -1)
        best, pos = lax.top_k(cand, PEER_TOPK)
        eidx = jnp.take_along_axis(cidx, pos, axis=-1)
        g = jax.nn.softmax(best, axis=-1)
        act = jax.nn.gelu(jnp.einsum('thkd,td->thk', expert_u[eidx], xb).astype(jnp.float32), approximate=False)
        return jnp.einsum('thk,thkd->td', (g * act).astype(xb.dtype), expert_v[eidx])

    return lax.map(one, xb_all).reshape(b, n, d)

def second_inputs(seed: int = 0) -> dict:
    key = jax.random.key(seed)
    ks = jax.random.split(key, 24)

    def nrm(k, shape, s):
        return jax.random.normal(k, shape, jnp.float32) * s

    def gain(k, shape):
        return 1.0 + nrm(k, shape, 0.01)

    D, L = D_MODEL, DEPTH_2
    fgate = jnp.linspace(FGATE_BIAS_LO, FGATE_BIAS_HI, ML_HEADS, dtype=jnp.float32)
    return {
        'x': nrm(ks[0], (BATCH, SEQ, D), 1.0),
        'c': nrm(ks[1], (BATCH, D), 1.0),
        'ctx': nrm(ks[2], (BATCH, CTX_LEN, D), 1.0),
        'c_ctx': nrm(ks[3], (D,), 1.0),
        'w_ada': nrm(ks[4], (L, D, N_MOD * D), 0.5 * D ** -0.5),
        'b_ada': nrm(ks[5], (L, N_MOD * D), 0.01),
        'g_norm1': gain(ks[6], (L, D)),
        'w_in': nrm(ks[7], (L, D, IN_COLS), D ** -0.5),
        'g_cq': gain(ks[8], (L, MLA_Q_RANK)),
        'w_uq': nrm(ks[9], (L, MLA_Q_RANK, MLA_HEADS * MLA_QK), MLA_Q_RANK ** -0.5),
        'g_ckv': gain(ks[10], (L, MLA_KV_RANK)),
        'w_ukv': nrm(ks[11], (L, MLA_KV_RANK, MLA_HEADS * (MLA_NOPE + MLA_V)), MLA_KV_RANK ** -0.5),
        'g_qn': gain(ks[12], (L, MLA_QK)),
        'g_kn': gain(ks[13], (L, MLA_QK)),
        'conv_qk': nrm(ks[14], (L, CONV_W, 2 * ML_HEADS * ML_QK), CONV_W ** -0.5),
        'b_igate': nrm(ks[15], (L, 2, ML_HEADS), 0.01),
        'b_fgate': fgate[None, None, :] + nrm(ks[16], (L, 2, ML_HEADS), 0.01),
        'g_mlstm': gain(ks[17], (L, ML_HEADS * ML_V)),
        'w_out': nrm(ks[18], (L, MIX_WIDTH, D), MIX_WIDTH ** -0.5),
        'g_norm2': gain(ks[19], (L, D)),
        'w_pq': nrm(ks[20], (L, D, PEER_HEADS * PEER_DK), D ** -0.5),
        'sub_keys': nrm(ks[21], (L, PEER_HEADS, 2, N_KEYS, PEER_DKH), PEER_DKH ** -0.5),
        'expert_u': nrm(ks[22], (L, N_EXPERTS, D), D ** -0.5),
        'expert_v': nrm(ks[23], (L, N_EXPERTS, D), PEER_HEADS ** -0.5),
    }

def second_block(x, c, ctx, c_ctx, w_ada, b_ada, g_norm1, w_in, g_cq, w_uq, g_ckv, w_ukv, g_qn, g_kn,
              conv_qk, b_igate, b_fgate, g_mlstm, w_out, g_norm2, w_pq, sub_keys, expert_u, expert_v):
    n_lat = x.shape[1]
    ROWS = n_lat // GRID_W
    rope = rope_tables_2(ROWS)
    s_c = jax.nn.silu(c)
    s_cc = jax.nn.silu(c_ctx)
    for l in range(DEPTH_2):
        last = l == DEPTH_2 - 1
        mod_lat = (s_c @ w_ada[l] + b_ada[l])[:, None, :]
        mod_ctx = s_cc @ w_ada[l] + b_ada[l]
        sh1, sc1, gt1, sh2, sc2, gt2 = jnp.split(mod_lat, N_MOD, axis=-1)
        csh1, csc1, cgt1, csh2, csc2, cgt2 = jnp.split(mod_ctx, N_MOD, axis=-1)
        h_lat = rmsnorm(x, g_norm1[l]) * (1.0 + sc1) + sh1
        h_ctx = rmsnorm(ctx, g_norm1[l]) * (1.0 + csc1) + csh1
        cols_lat = h_lat @ w_in[l]
        cols_ctx = h_ctx @ w_in[l]
        mla_lat, mla_ctx = mla_mixer(cols_lat[..., :MLA_COLS], cols_ctx[..., :MLA_COLS],
                                     g_cq[l], w_uq[l], g_ckv[l], w_ukv[l], g_qn[l], g_kn[l], rope, not last)
        ml_lat, ml_ctx = mlstm_mixer(cols_lat[..., MLA_COLS:], cols_ctx[..., MLA_COLS:],
                                     conv_qk[l], b_igate[l], b_fgate[l], g_mlstm[l], not last)
        x = x + gt1 * (jnp.concatenate([mla_lat, ml_lat], axis=-1) @ w_out[l])
        h2 = rmsnorm(x, g_norm2[l]) * (1.0 + sc2) + sh2
        x = x + gt2 * peer(h2, w_pq[l], sub_keys[l], expert_u[l], expert_v[l])
        if not last:
            ctx = ctx + cgt1 * (jnp.concatenate([mla_ctx, ml_ctx], axis=-1) @ w_out[l])
            hc2 = rmsnorm(ctx, g_norm2[l]) * (1.0 + csc2) + csh2
            ctx = ctx + cgt2 * peer(hc2, w_pq[l], sub_keys[l], expert_u[l], expert_v[l])
    return x


def setup_inputs(seed=0):
    out = dict(first_inputs(seed))
    for name, value in second_inputs(seed + 1).items():
        if name != "x":
            out[name + "_2"] = value
    return out


def reference(
    x, positions, norm_g, w_in, b_gate, cmp_pos, cmp_w1, cmp_w2, lru_conv_w, lru_conv_b,
    lru_w_a, lru_b_a, lru_w_i, lru_b_i, lru_lam, conv_dw_w, conv_dw_b, conv_ln_g, conv_ln_b,
    conv_w_pw2, w_out, final_g, c_2, ctx_2, c_ctx_2, w_ada_2, b_ada_2, g_norm1_2, w_in_2,
    g_cq_2, w_uq_2, g_ckv_2, w_ukv_2, g_qn_2, g_kn_2, conv_qk_2, b_igate_2, b_fgate_2,
    g_mlstm_2, w_out_2, g_norm2_2, w_pq_2, sub_keys_2, expert_u_2, expert_v_2,
):
    x = first_block(
        x, positions, norm_g, w_in, b_gate, cmp_pos, cmp_w1, cmp_w2, lru_conv_w, lru_conv_b,
        lru_w_a, lru_b_a, lru_w_i, lru_b_i, lru_lam, conv_dw_w, conv_dw_b, conv_ln_g, conv_ln_b,
        conv_w_pw2, w_out, final_g,
    )
    return second_block(
        x, c_2, ctx_2, c_ctx_2, w_ada_2, b_ada_2, g_norm1_2, w_in_2, g_cq_2, w_uq_2, g_ckv_2,
        w_ukv_2, g_qn_2, g_kn_2, conv_qk_2, b_igate_2, b_fgate_2, g_mlstm_2, w_out_2, g_norm2_2,
        w_pq_2, sub_keys_2, expert_u_2, expert_v_2,
    )


_drawn_inputs = setup_inputs


def setup_inputs(seed=0):
    import zlib

    import numpy as np

    out = dict(_drawn_inputs(seed))
    spreads = {}
    factors = {'norm_g': 3.872,
     'b_gate': 8.0,
     'cmp_pos': 8.0,
     'lru_b_a': 8.0,
     'lru_b_i': 8.0,
     'conv_dw_b': 3.957,
     'conv_ln_g': 6.725,
     'conv_ln_b': 7.409,
     'final_g': 2.676,
     'b_ada_2': 5.685,
     'g_norm1_2': 8.0,
     'g_cq_2': 8.0,
     'g_ckv_2': 8.0,
     'g_qn_2': 8.0,
     'g_kn_2': 8.0,
     'b_igate_2': 64.0,
     'g_mlstm_2': 64.0,
     'g_norm2_2': 29.051}
    for name, (base, spread) in spreads.items():
        noise = np.random.default_rng([zlib.crc32(name.encode()), seed]).standard_normal(out[name].shape)
        drawn = base * np.exp(spread * noise) if base else spread * noise
        out[name] = __import__('jax').numpy.asarray(drawn.astype(out[name].dtype))
    for name, factor in factors.items():
        out[name] = (out[name] * factor).astype(out[name].dtype)
    return out
```

```python
from contextlib import ExitStack

import numpy as np
import concourse.bass as bass
from concourse import mybir

F32 = mybir.dt.float32
I32 = mybir.dt.int32
U32 = mybir.dt.uint32
ALU = mybir.AluOpType
ACT = mybir.ActivationFunctionType
AX = mybir.AxisListType
MUL, ADD, SUB, MAX, MIN = ALU.mult, ALU.add, ALU.subtract, ALU.max, ALU.min

P = 128
T = 256
NT = T // P
D = 1024
KT = D // P
DEPTH = 2
EPS = 1e-6
NEG = -1e30

HEADS, KV, HD = 8, 2, 64
REP = HEADS // KV
WIDE = 512
FT = WIDE // P
NCMP, CMP_PAD, L_CMP, S_CMP, CMP_HID = 15, 16, 32, 16, 256
LRU_C = 8.0
LRU_TAPS, DW_TAPS = 4, 31
BRANCHES = 3
C_Q, C_KVC, C_KVW, C_ZN = 0, 512, 1024, 1304
C_ULRU, C_ZLRU, C_GA, C_GB, C_ZC = 1816, 2328, 2840, 3352, 3864

MLA_H, NOPE, ROPE2, MLA_V = 4, 128, 64, 128
QK = NOPE + ROPE2
Q_RANK, KV_RANK = 256, 128
ML_H, ML_QK, ML_V = 4, 64, 128
MLA_COLS = Q_RANK + KV_RANK + ROPE2
B_QK = MLA_COLS
B_V = B_QK + 2 * ML_H * ML_QK
B_O = B_V + ML_H * ML_V
B_G = B_O + ML_H * ML_V
PEER_H, N_KEYS, TOPK = 8, 128, 16
SLOTS = PEER_H * TOPK

ROW_DW, ROW_LC, ROW_LCB, ROW_BA, ROW_BI, ROW_LAM, ROW_DWB, ROW_LNG, ROW_LNB, N_ROWS = (
    0, 31, 35, 36, 37, 38, 39, 40, 41, 42)


def constants():
    p, f = np.arange(P)[:, None], np.arange(P)[None, :]
    t = np.arange(T).reshape(NT, P)
    n = np.arange(CMP_PAD)
    parts = {}
    parts["ident"] = np.eye(P)
    parts["zeros"] = np.zeros((P, P))
    parts["lower"] = np.where(f <= p, 0.0, NEG)
    parts["upper"] = np.where(f >= p, 0.0, NEG)
    ok = (n[None, None] < NCMP) & (n[None, None] * S_CMP + L_CMP - 1 <= t.T[:, :, None])
    parts["cmp_neg"] = np.where(ok, 0.0, NEG).reshape(P, -1)
    parts["cmp_one"] = ok.astype(float).reshape(P, -1)
    parts["blocks"] = (np.arange(P)[:, None] // CMP_PAD == np.arange(HEADS)[None]).astype(float)
    inv = (np.float32(10000.0) ** (-np.arange(0, HD, 2, dtype=np.float32) / np.float32(HD)))
    parts["inv_freq"] = np.broadcast_to(inv, (P, HD // 2))
    half = ROPE2 // 4
    inv2 = np.float32(10000.0) ** (-np.arange(half, dtype=np.float32) * np.float32(2.0 / (2 * half)))
    ang = np.stack([(t // 64).T, (t % 64).T], -1).astype(np.float32)[..., None] * inv2
    parts["cos2"] = np.cos(ang).reshape(P, -1)
    parts["sin2"] = np.sin(ang).reshape(P, -1)
    sel = np.zeros((P, ML_H, P))
    sel[np.arange(ML_H), np.arange(ML_H)] = 1.0
    parts["select"] = sel.reshape(P, -1)
    parts["iota"] = np.broadcast_to(np.arange(TOPK), (P, TOPK))
    parts["ones"] = np.ones((P, P))
    at, where = 0, {}
    for name, a in parts.items():
        where[name] = (at, at + a.shape[1])
        at += a.shape[1]
    return np.concatenate(list(parts.values()), 1).astype(np.float32), where


class Lane:

    def __init__(self, nc, engine, name, chained):
        self.engine, self.sem, self.chained = engine, nc.alloc_semaphore(name), chained
        self.count, self.seen = 0, {}

    def wait(self, *tokens):
        for token in tokens:
            if isinstance(token, list):
                self.wait(*token)
            elif token is not None and self.seen.get(token[0].name, 0) < token[1]:
                self.engine.wait_ge(token[0], token[1])
                self.seen[token[0].name] = token[1]

    @property
    def last(self):
        return (self.sem, self.count) if self.count else None

    def __call__(self, tokens, issue, *args, mark=True, **kw):
        self.wait(*tokens)
        if self.chained:
            self.wait(self.last)
        ins = issue(*args, **kw)
        if mark:
            ins.then_inc(self.sem, 1)
            self.count += 1
        return self.last

    def clear(self):
        self.count, self.seen = 0, {}


class Arrivals:

    def __init__(self, nc, name):
        self.nc, self.sem, self.count = nc, nc.alloc_semaphore(name), 0

    def load(self, lane, tokens, out, in_, **kw):
        lane.wait(*tokens)
        lane.engine.dma_start(out, in_, **kw).then_inc(self.sem, 16)
        self.count += 16
        return (self.sem, self.count)

    def clear(self):
        self.count = 0


class Ring:

    def __init__(self, items):
        self.items = items
        self.clear()

    def take(self):
        self.at = (self.at + 1) % len(self.items)
        assert not self.taken[self.at], "a buffer is taken again before its release"
        self.taken[self.at] = True
        return self.at, self.items[self.at], self.free[self.at]

    def release(self, slot, token):
        self.free[slot], self.taken[slot] = token, False

    def clear(self):
        n = len(self.items)
        self.free, self.taken, self.at = [None] * n, [False] * n, -1


class WeightStream:

    def __init__(self, core, ring, plan):
        self.core, self.ring, self.plan, self.ready = core, ring, list(plan), []
        for _ in ring.items:
            self.fetch()

    def fetch(self):
        if self.plan:
            src, k, n = self.plan.pop(0)
            slot, buf, free = self.ring.take()
            view = buf[:, 0:k * n].rearrange("p (k n) -> p k n", k=k)
            self.ready.append((slot, view, self.core.load(f"weights{slot}", view, src, [free])))

    def next(self):
        return self.ready[0][1:]

    def done(self, token):
        self.ring.release(self.ready.pop(0)[0], token)
        self.fetch()


class Core:

    def __init__(self, nc):
        self.nc = nc
        self.dve = Lane(nc, nc.vector, "dve_done", True)
        self.act = Lane(nc, nc.scalar, "act_done", True)
        self.pool = Lane(nc, nc.gpsimd, "pool_done", True)
        self.pe = Lane(nc, nc.tensor, "pe_done", False)
        self.sp = Lane(nc, nc.sync, "sp_done", False)
        self.lanes = [self.dve, self.act, self.pool, self.pe, self.sp]
        self.streams, self.rings = {}, []
        self.flip = 0
        banks = [nc.alloc_psum_tensor(f"bank{i}", [P, 512], F32)[:] for i in range(8)]
        self.banks = self.ring([b for b in banks[:4]])
        self.held = banks[4:]

    def ring(self, items):
        r = Ring(items)
        self.rings.append(r)
        return r

    def stream(self, name):
        if name not in self.streams:
            self.streams[name] = Arrivals(self.nc, "in_" + name)
        return self.streams[name]

    def load(self, name, out, in_, tokens=(), lane=None, **kw):
        return self.stream(name).load(lane or self.sp, tokens, out, in_, **kw)

    def meet(self):
        done = [lane.last for lane in self.lanes]
        for lane in self.lanes:
            lane.wait(*done)

    def restart(self):
        for s in self.streams.values():
            self.sp.wait((s.sem, s.count) if s.count else None)
        self.nc.all_engine_barrier()
        for s in [*self.lanes, *self.streams.values()]:
            self.nc.gpsimd.sem_clear(s.sem)
        self.nc.all_engine_barrier()
        for s in [*self.lanes, *self.streams.values(), *self.rings]:
            s.clear()

    def matmul(self, tokens, out, lhsT, rhs, start=True, stop=True, mark=None, **kw):
        return self.pe(tokens, self.nc.tensor.matmul, out, lhsT, rhs, start=start, stop=stop,
                       mark=stop if mark is None else mark, **kw)

    def copy(self, tokens, out, in_):
        self.flip ^= 1
        if self.flip:
            return self.dve(tokens, self.nc.vector.tensor_copy, out, in_)
        return self.act(tokens, self.nc.scalar.copy, out, in_)

    def tt(self, tokens, out, a, b, op):
        return self.dve(tokens, self.nc.vector.tensor_tensor, out, a, b, op)

    def ts(self, tokens, out, a, s1, op0, s2=None, op1=None):
        if s2 is None:
            return self.dve(tokens, self.nc.vector.tensor_scalar, out, a, s1, None, op0)
        return self.dve(tokens, self.nc.vector.tensor_scalar, out, a, s1, s2, op0, op1)

    def stt(self, tokens, out, a, s, b, op0, op1):
        return self.dve(tokens, self.nc.vector.scalar_tensor_tensor, out, a, s, b, op0, op1)

    def f(self, tokens, out, a, func, **kw):
        return self.act(tokens, self.nc.scalar.activation, out, a, func, **kw)


def wide(ap, shape):
    return ap.to_broadcast(shape)


def sb(core, stack, name, shape, dt=F32):
    return stack.enter_context(core.nc.sbuf_tensor(name, shape, dt))[:]


def inv_rms(core, tokens, out, sums, width, scratch):
    core.ts(tokens, scratch, sums, 1.0 / width, MUL, EPS, ADD)
    t = core.dve([], core.nc.vector.reciprocal, scratch, scratch)
    return core.f([t], out, scratch, ACT.Sqrt)


def norm_transposed(core, ready, x, xn, hT, col, scale, shift, sq, small, ident):
    nc = core.nc
    for tt in range(NT):
        s = core.f(ready, sq, x[:, tt, :], ACT.Square, accum_out=small[:, tt:tt + 1])
    s = inv_rms(core, [s], small[:, 4:6], small[:, 0:2], D, small[:, 2:4])
    for tt in range(NT):
        s = core.ts([s], xn[:, tt, :], x[:, tt, :], small[:, 4 + tt:5 + tt], MUL)
    done = []
    for k in range(KT):
        slot, bank, free = core.banks.take()
        for tt in range(NT):
            t = core.pe([s, free], nc.tensor.transpose, bank[:, tt * P:tt * P + P],
                        xn[:, tt, k * P:k * P + P], ident)
        if shift is None:
            t = core.ts([t], hT[:, k, col:col + T], bank[:, 0:T], scale[:, k:k + 1], MUL)
        else:
            t = core.ts([t], hT[:, k, col:col + T], bank[:, 0:T], scale[:, k:k + 1], MUL,
                        shift[:, k:k + 1], ADD)
        core.banks.release(slot, t)
    return t


def log1p_unit(core, tokens, out, z, s, s2, acc):
    core.ts(tokens, s, z, 2.0, ADD)
    core.dve([], core.nc.vector.reciprocal, s, s)
    core.tt([], s, s, z, MUL)
    core.tt([], s2, s, s, MUL)
    core.ts([], acc, s2, 1.0 / 17, MUL, 1.0 / 15, ADD)
    for odd in (13, 11, 9, 7, 5, 3, 1):
        core.tt([], acc, acc, s2, MUL)
        core.ts([], acc, acc, 1.0 / odd, ADD)
    core.tt([], acc, acc, s, MUL)
    return core.ts([], out, acc, 2.0, MUL)


def rope_angles(core, ready, pos, inv_freq, cos, sin, ang, turns):
    two_pi, magic = 2 * np.pi, 1.5 * 2.0**23
    part1 = 6.28125
    part2 = float(np.float32(np.round((two_pi - part1) * 2**21) / 2**21))
    part3 = two_pi - part1 - part2
    edge = 3.1415925
    for tt in range(NT):
        core.ts(ready, ang[:, tt, :], inv_freq, pos[:, tt:tt + 1], MUL)
    core.ts([], turns, ang, 1.0 / two_pi, MUL)
    core.ts([], turns, turns, magic, ADD)
    core.ts([], turns, turns, magic, SUB)
    for part in (part1, part2, part3):
        core.stt([], ang, turns, -part, ang, MUL, ADD)
    s = core.ts([], ang, ang, edge, MIN, -edge, MAX)
    core.f([s], sin, ang, ACT.Sin)
    core.stt([], turns, ang, -1.0, ang, MUL, MAX)
    s = core.ts([], turns, turns, -1.0, MUL, np.pi / 2, ADD)
    return core.f([s], cos, turns, ACT.Sin)


def first_block(core, A, K, x):
    nc = core.nc
    with ExitStack() as stack:
        def tile(name, shape, dt=F32):
            return sb(core, stack, name, shape, dt)

        w = core.ring([tile(f"weights{i}", [P, 4096]) for i in range(4)])
        tiles = {}
        for name, shape in (
                ("hT", [P, KT, T]), ("xn", [P, NT, D]), ("sq", [P, D]), ("small", [P, 8]),
                ("rows", [N_ROWS, WIDE]), ("vec", [P, FT, N_ROWS]), ("sp8", [P, FT]),
                ("grows", [KT, P]), ("gT", [P, KT]), ("b_gate", [P, 24]),
                ("cos", [P, NT, 32]), ("sin", [P, NT, 32]), ("ang", [P, NT, 32]), ("turns", [P, NT, 32]),
                ("posf", [P, NT]),
                ("ubuf", [P, FT, DW_TAPS - 1 + T]), ("conv", [P, FT, T]), ("fa", [P, FT, T]),
                ("fb", [P, FT, T]), ("fc", [P, FT, T]), ("fd", [P, FT, T]), ("lbuf", [P, FT, LRU_TAPS - 1 + T]), ("xc", [P, FT, T]),
                ("qr", [P, NT, WIDE]), ("kr", [P, 3, NT, P]), ("vr", [P, 3, NT, P]),
                ("r1", [P, WIDE // 2]), ("r2", [P, WIDE // 2]),
                ("qT", [P, FT, T]), ("kT", [P, 2, T]), ("pair", [P, 2, KV, T]), ("cT", [P, 2, T]),
                ("pos_rows", [16, 2, P]), ("posT", [P, 2, 16]), ("blk", [P, 2, 16, KV * CMP_PAD]),
                ("hidT", [P, 2, 2, KV * CMP_PAD]), ("hid_rep", [P, 2, HEADS, CMP_PAD]), ("sig32", [P, 32]),
                ("w2", [P, 2, 2, HD]), ("kcT", [P, CMP_PAD]), ("vcb", [P, HEADS, HD]),
                ("gates", [P, NT, 24]), ("zn", [P, NT, WIDE]), ("mixT", [P, 12, T]),
                ("S", [P, 4, T]), ("mx", [P, 4]), ("sums", [P, 3, HEADS]),
                ("pc", [P, HEADS, CMP_PAD]), ("mc", [P, HEADS]), ("PT", [P, 3, 512]),
                ("y", [P, WIDE]), ("yt", [P, WIDE]), ("coef", [P, 3, HEADS]), ("bd", [P, 2, FT, P])):
            tiles[name] = tile(name, shape)
        posi = tile("posi", [P, NT], I32)
        core.dve([], nc.vector.memset, tiles["bd"][:], 0.0)
        core.dve([], nc.vector.memset, tiles["ubuf"][:], 0.0)
        core.dve([], nc.vector.memset, tiles["lbuf"][:], 0.0)
        core.dve([], nc.vector.memset, tiles["blk"][:], 0.0)
        s = core.load("pos", posi[:], A["positions"].rearrange("b (t p) -> p (b t)", p=P),
                      allow_slow_non_contiguous=True)
        s = core.dve([s, K["ready"]], nc.vector.tensor_copy, tiles["posf"][:], posi[:])
        rope_angles(core, [s], tiles["posf"], K["inv_freq"], tiles["cos"][:], tiles["sin"][:],
                    tiles["ang"], tiles["turns"][:])
        core.restart()
        with nc.Fori(0, DEPTH) as layer:
            first_layer(core, A, K, x, w, tiles, layer)
            core.restart()
        core.rings.remove(w)


def first_layer(core, A, K, x, w, tl, layer):
    nc = core.nc
    V = nc.vector
    one = bass.ds(layer, 1)
    ident = K["ident"]
    hT, vec, mixT = tl["hT"], tl["vec"], tl["mixT"]

    def rows_of(ap):
        return ap.rearrange("o (k p) n -> p (o k) n", p=P)

    stream = WeightStream(core, w, [
        *((rows_of(A["w_in"][one, :, c0:c0 + n]), KT, n) for c0, n in (
            (C_GB, WIDE), (C_GA, WIDE), (C_ULRU, WIDE), (C_Q, WIDE), (C_KVC, WIDE),
            (C_KVW, C_ZN - C_KVW), (C_ZN, WIDE), (C_ZLRU, WIDE), (C_ZC, WIDE))),
        *((rows_of(A["cmp_w1"][one, b]), 16, CMP_HID) for b in range(2)),
        (rows_of(A["conv_w_pw2"][one]), FT, WIDE),
        *((rows_of(A["w_out"][one, i * 512:i * 512 + 512, :]), 4, D) for i in range(3))])

    rows = tl["rows"]
    core.load("rows", tl["grows"][:], A["norm_g"][one, :].rearrange("o (k p) -> (o k) p", p=P))
    core.load("rows", rows[ROW_DW:ROW_LC, :], A["conv_dw_w"][one].rearrange("o k c -> (o k) c"))
    core.load("rows", rows[ROW_LC:ROW_LCB, :], A["lru_conv_w"][one].rearrange("o k c -> (o k) c"))
    for r, name in ((ROW_LCB, "lru_conv_b"), (ROW_BA, "lru_b_a"), (ROW_BI, "lru_b_i"),
                    (ROW_LAM, "lru_lam"), (ROW_DWB, "conv_dw_b"), (ROW_LNG, "conv_ln_g"),
                    (ROW_LNB, "conv_ln_b")):
        rows_in = core.load("rows", rows[r:r + 1, :], A[name][one, :])
    bd = tl["bd"]
    for i, name in enumerate(("lru_w_a", "lru_w_i")):
        for par in range(2):
            bd_in = core.load("bd", bd[par * HD:par * HD + HD, i, :, par * HD:par * HD + HD],
                              A[name][one, par:HEADS:2].rearrange("o h i j -> i (o h) j"))
    core.load("misc", tl["b_gate"][:], A["b_gate"][one, :].to_broadcast([P, 24]))
    core.load("misc", tl["pos_rows"][:], A["cmp_pos"][one].rearrange("o b (j e) d -> j (o b) (e d)", e=2))
    misc_in = core.load("misc", tl["w2"][:], A["cmp_w2"][one].rearrange("o b (k p) d -> p (o b) k d", p=P))

    slot, bank, free = core.banks.take()
    for c in range(FT):
        t = core.pe([rows_in, free], nc.tensor.transpose, bank[:, c * N_ROWS:(c + 1) * N_ROWS],
                    rows[:, c * P:c * P + P], ident[0:N_ROWS, 0:N_ROWS])
    t = core.pe([], nc.tensor.transpose, bank[:, 256:256 + KT], tl["grows"][:], ident[0:KT, 0:KT])
    core.dve([t], V.tensor_copy, vec[:], bank[:, 0:FT * N_ROWS].rearrange("p (c r) -> p c r", c=FT))
    vec_ready = core.dve([], V.tensor_copy, tl["gT"][:], bank[:, 256:256 + KT])
    core.banks.release(slot, vec_ready)
    slot, bank, free = core.banks.take()
    for b in range(2):
        t = core.pe([misc_in, free], nc.tensor.transpose, bank[:, b * 16:b * 16 + 16],
                    tl["pos_rows"][:, b, :], ident[0:16, 0:16])
    s = core.dve([t], V.tensor_copy, tl["posT"][:], bank[:, 0:32].rearrange("p (b j) -> p b j", b=2))
    core.banks.release(slot, s)

    h_ready = norm_transposed(core, [vec_ready], x, tl["xn"], hT, 0, tl["gT"], None, tl["sq"][:],
                              tl["small"], ident)

    def by_feature(use):
        view, landed = stream.next()
        for c in range(0, FT, 2):
            slot, bank, free = core.banks.take()
            for e in range(2):
                for k in range(KT):
                    t = core.matmul([landed, h_ready, free], bank[:, e * T:e * T + T],
                                    view[:, k, (c + e) * P:(c + e) * P + P], hT[:, k, :],
                                    start=k == 0, stop=k == KT - 1)
            core.banks.release(slot, use(c, bank[:, :].rearrange("p (e t) -> p e t", e=2), t))
        stream.done(t)

    def by_token(n, use):
        view, landed = stream.next()
        for tt in range(NT):
            slot, bank, free = core.banks.take()
            for k in range(KT):
                t = core.matmul([landed, h_ready, free], bank[:, 0:n], hT[:, k, tt * P:tt * P + P],
                                view[:, k, :], start=k == 0, stop=k == KT - 1)
            core.banks.release(slot, use(tt, bank, t))
        stream.done(t)

    fa, fb, fc, fd, conv, xc = tl["fa"], tl["fb"], tl["fc"], tl["fd"], tl["conv"], tl["xc"]
    ubuf, lbuf = tl["ubuf"], tl["lbuf"]

    by_feature(lambda c, b, t: core.f([t], fb[:, c:c + 2, :], b, ACT.Sigmoid))
    sig_ready = core.act.last
    by_feature(lambda c, b, t: core.tt([t, sig_ready], ubuf[:, c:c + 2, DW_TAPS - 1:], b,
                                                fb[:, c:c + 2, :], MUL))
    by_feature(lambda c, b, t: core.f([t], lbuf[:, c:c + 2, LRU_TAPS - 1:], b, ACT.Copy))
    u_ready = core.act.last

    def depthwise(tokens, out, src, row_w, row_b, taps):
        for c in range(FT):
            core.ts(tokens, out[:, c, :], src[:, c, 0:T], vec[:, c, row_w:row_w + 1], MUL,
                    vec[:, c, row_b:row_b + 1], ADD)
            for j in range(1, taps):
                s = core.stt([], out[:, c, :], src[:, c, j:j + T], vec[:, c, row_w + j:row_w + j + 1],
                             out[:, c, :], MUL, ADD)
        return s

    xc_ready = depthwise([u_ready], xc, lbuf, ROW_LC, ROW_LCB, LRU_TAPS)
    lam = vec[:, :, ROW_LAM]
    sp8, st = tl["sp8"], tl["small"]
    sc = tl["r1"]
    s = core.stt([], sc[:, 0:4], lam, -1.0, lam, MUL, MAX)
    s = core.f([s], sc[:, 4:8], sc[:, 0:4], ACT.Exp, scale=-1.0)
    log1p_unit(core, [s], sc[:, 8:12], sc[:, 4:8], sc[:, 12:16], sc[:, 16:20], sc[:, 20:24])
    core.ts([], sc[:, 0:4], lam, -1.0, MUL, 0.0, MAX)
    core.tt([], sp8[:], sc[:, 0:4], sc[:, 8:12], ADD)
    sp_ready = core.ts([], sp8[:], sp8[:], LRU_C, MUL)

    for i, (dst, row) in enumerate(((fa, ROW_BA), (fc, ROW_BI))):
        for c in range(0, FT, 2):
            slot, bank, free = core.banks.take()
            for e in range(2):
                t = core.matmul([xc_ready, bd_in, free], bank[:, e * T:e * T + T], bd[:, i, c + e, :],
                                xc[:, c + e, :])
            for e in range(2):
                s = core.f([t], dst[:, c + e, :], bank[:, e * T:e * T + T], ACT.Sigmoid,
                           bias=vec[:, c + e, row:row + 1])
            core.banks.release(slot, s)

    for c in range(FT):
        core.f([sp_ready], fd[:, c, :], fa[:, c, :], ACT.Tanh, scale=sp8[:, c:c + 1])
    s = core.act.last
    core.ts([s], fb[:], fd[:], 1.0, ADD)
    core.dve([], V.reciprocal, fb[:], fb[:])
    s = core.tt([], fd[:], fd[:], fb[:], MUL)
    core.tt([s], fc[:], fc[:], xc[:], MUL)
    neg = core.ts([], tl["small"][:, 0:4], sp8[:], -1.0, MUL)
    for c in range(FT):
        core.f([neg], fa[:, c, :], fa[:, c, :], ACT.Exp, scale=tl["small"][:, c:c + 1])
    s = core.f([s], fd[:], fd[:], ACT.Sqrt, scale=2.0)
    core.tt([s], fd[:], fd[:], fc[:], MUL)
    for c in range(FT):
        core.dve([], V.tensor_tensor_scan, fc[:, c, :], fa[:, c, :], fd[:, c, :], 0.0, MUL, ADD)
    lru_ready = core.dve.last

    cos, sin, r1, r2, qr, kr, vr = (tl[n] for n in ("cos", "sin", "r1", "r2", "qr", "kr", "vr"))

    def rotate(tt, t, out, src, g, i):
        n = g * i * 32
        shape = [P, g, i, 32]
        c4 = wide(cos[:, tt, :].unsqueeze(1).unsqueeze(1), shape)
        s4 = wide(sin[:, tt, :].unsqueeze(1).unsqueeze(1), shape)
        v1 = r1[:, 0:n].rearrange("p (g i d) -> p g i d", g=g, i=i)
        v2 = r2[:, 0:n].rearrange("p (g i d) -> p g i d", g=g, i=i)
        a, b = src[:, :, :, 0:32], src[:, :, :, 32:64]
        core.tt([t], v1, a, c4, MUL)
        core.tt([], v2, b, s4, MUL)
        core.tt([], out[:, :, :, 0:32], v1, v2, SUB)
        core.tt([], v1, b, c4, MUL)
        core.tt([], v2, a, s4, MUL)
        return core.tt([], out[:, :, :, 32:64], v1, v2, ADD)

    def use_q(tt, bank, t):
        return rotate(tt, t, qr[:, tt, :].rearrange("p (i g d) -> p g i d", g=KV, d=HD),
                      bank[:, :].rearrange("p (g i d) -> p g i d", g=KV, d=HD), KV, REP)

    def use_k(tt, bank, t):
        s = []
        for i, (kc, b) in enumerate(((0, 0), (256, 1))):
            s.append(rotate(tt, t, kr[:, b, tt, :].rearrange("p (g i d) -> p g i d", g=KV, d=HD),
                            bank[:, kc:kc + P].rearrange("p (g i d) -> p g i d", g=KV, d=HD), KV, 1))
            s.append(core.dve([t], V.tensor_copy, vr[:, b, tt, :], bank[:, kc + P:kc + 2 * P]))
        return s

    gates = tl["gates"]

    def use_w(tt, bank, t):
        s1 = rotate(tt, t, kr[:, 2, tt, :].rearrange("p (g i d) -> p g i d", g=KV, d=HD),
                    bank[:, 0:P].rearrange("p (g i d) -> p g i d", g=KV, d=HD), KV, 1)
        s2 = core.dve([t], V.tensor_copy, vr[:, 2, tt, :], bank[:, P:2 * P])
        s1 = core.tt([t, misc_in], gates[:, tt, :], bank[:, 256:280], tl["b_gate"][:], ADD)
        return [s1, s2]

    by_token(WIDE, use_q)
    by_token(WIDE, use_k)
    by_token(C_ZN - C_KVW, use_w)
    s = core.f([core.dve.last], gates[:], gates[:], ACT.Sigmoid)
    qkv_ready = [s, core.dve.last]
    zn = tl["zn"]

    def use_z(tt, bank, t):
        s = core.f([t], zn[:, tt, :], bank[:, :], ACT.Sigmoid)
        return core.tt([s], zn[:, tt, :], zn[:, tt, :], bank[:, :], MUL)

    by_token(WIDE, use_z)

    qT, kT, cT, pair = tl["qT"], tl["kT"], tl["cT"], tl["pair"]
    for c in range(0, FT, 2):
        slot, bank, free = core.banks.take()
        for e in range(2):
            for tt in range(NT):
                t = core.pe([qkv_ready, free], nc.tensor.transpose,
                            bank[:, e * T + tt * P:e * T + tt * P + P],
                            qr[:, tt, (c + e) * P:(c + e) * P + P], ident)
        s = core.copy([t], qT[:, c:c + 2, :], bank[:, :].rearrange("p (e t) -> p e t", e=2))
        core.banks.release(slot, s)
    q_ready = [core.dve.last, core.act.last]
    for dst, srcs in ((kT, (kr[:, 1], kr[:, 2])), (cT, (kr[:, 0], vr[:, 0]))):
        slot, bank, free = core.banks.take()
        for e, src in enumerate(srcs):
            for tt in range(NT):
                t = core.pe([free], nc.tensor.transpose, bank[:, e * T + tt * P:e * T + tt * P + P],
                            src[:, tt, :], ident)
        s = core.copy([t], dst[:], bank[:, :].rearrange("p (e t) -> p e t", e=2))
        core.banks.release(slot, s)
    k_ready = [core.dve.last, core.act.last]
    for g in range(KV):
        src = cT[g * HD:g * HD + HD, :, :]
        core.load("pair", pair[0:HD, :, g, :], src, [k_ready])
        pair_in = core.load("pair", pair[HD:P, :, g, 0:T - 1], src[:, :, 1:T])

    conv_ready = depthwise([], conv, ubuf, ROW_DW, ROW_DWB, DW_TAPS)

    def gate_lru(c, b, t):
        s = core.f([t], fb[:, c:c + 2, :], b, ACT.Sigmoid)
        core.tt([s], fb[:, c:c + 2, :], fb[:, c:c + 2, :], b, MUL)
        return core.tt([lru_ready], mixT[:, 4 + c:6 + c, :], fb[:, c:c + 2, :], fc[:, c:c + 2, :], MUL)

    by_feature(gate_lru)
    zc = tl["xc"]

    def gate_conv(c, b, t):
        s = core.f([t, core.pe.last, lru_ready], zc[:, c:c + 2, :], b, ACT.Sigmoid)
        return core.tt([s], zc[:, c:c + 2, :], zc[:, c:c + 2, :], b, MUL)

    by_feature(gate_conv)

    blk, posT, hidT, w2 = tl["blk"], tl["posT"], tl["hidT"], tl["w2"]
    for b in range(2):
        for g in range(KV):
            ap = pair[:, b, g, :]
            src = bass.AP(ap.tensor, ap.offset, [ap.ap[0], [2, 8], [S_CMP, NCMP]])
            src2 = bass.AP(ap.tensor, ap.offset + 16, [ap.ap[0], [2, 8], [S_CMP, NCMP]])
            for half, sr in ((0, src), (1, src2)):
                dst = blk[:, b, half * 8:half * 8 + 8, g * CMP_PAD:g * CMP_PAD + NCMP]
                s = core.tt([pair_in, misc_in], dst, sr,
                            wide(posT[:, b, half * 8:half * 8 + 8].unsqueeze(2), [P, 8, NCMP]), ADD)
        view, landed = stream.next()
        slot, bank, free = core.banks.take()
        for m in range(2):
            for k in range(16):
                t = core.matmul([s, landed, free], bank[:, m * 32:m * 32 + 32],
                                view[:, k, m * P:m * P + P], blk[:, b, k, :], start=k == 0, stop=k == 15)
        stream.done(t)
        for m in range(2):
            s = core.f([t], tl["sig32"][:], bank[:, m * 32:m * 32 + 32], ACT.Sigmoid)
            s = core.tt([s], hidT[:, b, m, :], bank[:, m * 32:m * 32 + 32], tl["sig32"][:], MUL)
            core.act.wait(s)
        core.banks.release(slot, s)
    slot, bank, free = core.banks.take()
    for g in range(KV):
        for m in range(2):
            t = core.matmul([s, free], bank[g * HD:g * HD + HD, 0:CMP_PAD], w2[:, 0, m, :],
                            hidT[:, 0, m, g * CMP_PAD:g * CMP_PAD + CMP_PAD], start=m == 0, stop=m == 1)
    s = core.dve([t], V.tensor_copy, tl["kcT"][:], bank[:, 0:CMP_PAD])
    core.banks.release(slot, s)
    rep = tl["hid_rep"]
    for m in range(2):
        for g in range(KV):
            s = core.dve([], V.tensor_copy, rep[:, m, g * REP:g * REP + REP, :],
                         wide(hidT[:, 1, m, g * CMP_PAD:g * CMP_PAD + CMP_PAD].unsqueeze(1), [P, REP, CMP_PAD]))
    slot, bank, free = core.banks.take()
    for m in range(2):
        t = core.matmul([s, free], bank[:, 0:HD], rep[:, m, :, :].rearrange("p h n -> p (h n)"),
                        w2[:, 1, m, :], start=m == 0, stop=m == 1)
    cmp_ready = core.tt([t], tl["vcb"][:], wide(bank[:, 0:HD].unsqueeze(1), [P, HEADS, HD]),
                        wide(K["blocks"].unsqueeze(2), [P, HEADS, HD]), MUL)
    core.banks.release(slot, cmp_ready)

    pw2, pw_in = stream.next()
    ones = K["ones"]
    slot, bank, free = core.banks.take()
    for c in range(FT):
        t = core.matmul([conv_ready, free], bank[:, 0:T], ones, conv[:, c, :], start=c == 0, stop=c == FT - 1)
    mean, var = fa[:, 0, :], fa[:, 1, :]
    core.ts([t], mean, bank[:, 0:T], 1.0 / WIDE, MUL)
    core.banks.release(slot, core.dve.last)
    s = core.tt([], conv[:], conv[:], wide(mean.unsqueeze(1), [P, FT, T]), SUB)
    s = core.f([s], fd[:], conv[:], ACT.Square)
    slot, bank, free = core.banks.take()
    for c in range(FT):
        t = core.matmul([s, free], bank[:, 0:T], ones, fd[:, c, :], start=c == 0, stop=c == FT - 1)
    s = inv_rms(core, [t], var, bank[:, 0:T], WIDE, fa[:, 2, :])
    core.banks.release(slot, s)
    core.tt([s], conv[:], conv[:], wide(var.unsqueeze(1), [P, FT, T]), MUL)
    for c in range(FT):
        s = core.ts([], conv[:, c, :], conv[:, c, :], vec[:, c, ROW_LNG:ROW_LNG + 1], MUL,
                    vec[:, c, ROW_LNB:ROW_LNB + 1], ADD)
    s = core.f([s], fd[:], conv[:], ACT.Sigmoid)
    act_ready = core.tt([s], fd[:], fd[:], conv[:], MUL)
    for c in range(0, FT, 2):
        slot, bank, free = core.banks.take()
        for e in range(2):
            for k in range(FT):
                t = core.matmul([act_ready, pw_in, free], bank[:, e * T:e * T + T],
                                pw2[:, k, (c + e) * P:(c + e) * P + P], fd[:, k, :],
                                start=k == 0, stop=k == FT - 1)
        s = core.tt([t], mixT[:, 8 + c:10 + c, :], bank[:, :].rearrange("p (e t) -> p e t", e=2),
                    zc[:, c:c + 2, :], MUL)
        core.banks.release(slot, s)
    stream.done(t)

    S, mx, PT, sums, coef = tl["S"], tl["mx"], tl["PT"], tl["sums"], tl["coef"]
    O = core.held
    pc, mc, y, yt = tl["pc"], tl["mc"], tl["y"], tl["yt"]
    pt_free, o_free, s_free = [None] * 3, None, [None] * 2
    n_pt = 0
    for qt in range(NT):
        nk = (qt + 1) * P
        mask = K["mask2"][:, (NT - 1 - qt) * P:NT * P]
        parts = []
        for g in range(KV):
            slot, bank, free = core.banks.take()
            for i in range(REP):
                t = core.matmul([q_ready, cmp_ready, free], bank[:, i * CMP_PAD:(i + 1) * CMP_PAD],
                                qT[g * HD:g * HD + HD, i, qt * P:qt * P + P], tl["kcT"][g * HD:g * HD + HD, :])
            s = core.stt([t], pc[:, g * REP:g * REP + REP, :], bank[:, 0:REP * CMP_PAD].rearrange("p (h n) -> p h n", h=REP),
                         HD ** -0.5, wide(K["cmp_neg"][:, qt * CMP_PAD:qt * CMP_PAD + CMP_PAD].unsqueeze(1),
                                          [P, REP, CMP_PAD]), MUL, ADD)
            core.banks.release(slot, s)
        core.dve([], V.tensor_reduce, mc[:], pc[:], AX.X, MAX)
        s = core.tt([], pc[:], pc[:], wide(mc[:].unsqueeze(2), [P, HEADS, CMP_PAD]), SUB)
        s = core.f([s], pc[:], pc[:], ACT.Exp)
        core.dve([s], V.tensor_reduce, sums[:, 0, :], pc[:], AX.X, ADD)
        s = core.tt([], pc[:], pc[:], wide(K["cmp_one"][:, qt * CMP_PAD:qt * CMP_PAD + CMP_PAD].unsqueeze(1),
                                           [P, HEADS, CMP_PAD]), MUL)
        slot, bank, free = core.banks.take()
        t = core.pe([s, free], nc.tensor.transpose, bank[:, 0:P], pc[:].rearrange("p h n -> p (h n)"), ident)
        b = n_pt % 3
        n_pt += 1
        s = core.dve([t, pt_free[b]], V.tensor_copy, PT[:, b, 0:P], bank[:, 0:P])
        core.banks.release(slot, s)
        t = core.matmul([s, o_free], O[0][:, :], PT[:, b, 0:P], tl["vcb"][:].rearrange("p h d -> p (h d)"))
        pt_free[b] = t
        for i in range(REP):
            scores = []
            for g in range(KV):
                slot, bank, free = core.banks.take()
                for b in range(2):
                    t = core.matmul([k_ready, free], bank[:, b * T:b * T + nk],
                                    qT[g * HD:g * HD + HD, i, qt * P:qt * P + P], kT[g * HD:g * HD + HD, b, 0:nk])
                scores.append((slot, bank, t))
            for g, (slot, bank, t) in enumerate(scores):
                h = g * REP + i
                for b in range(2):
                    s = core.dve([t, s_free[g]], V.tensor_tensor_reduce, S[:, 2 * g + b, 0:nk], bank[:, b * T:b * T + nk],
                                 mask, -(HD ** -0.5), 3e38, ADD, MIN, mx[:, 2 * g + b:2 * g + b + 1])
                core.banks.release(slot, s)
                for b in range(2):
                    s = core.f([s], S[:, 2 * g + b, 0:nk], S[:, 2 * g + b, 0:nk], ACT.Exp,
                               bias=mx[:, 2 * g + b:2 * g + b + 1], scale=-1.0, accum_out=sums[:, 1 + b, h:h + 1])
                slot, bank, free = core.banks.take()
                for b in range(2):
                    for kt in range(qt + 1):
                        t = core.pe([s, free], nc.tensor.transpose, bank[:, (b * (qt + 1) + kt) * P:(b * (qt + 1) + kt + 1) * P],
                                    S[:, 2 * g + b, kt * P:kt * P + P], ident)
                s_free[g] = t
                z = n_pt % 3
                n_pt += 1
                n = 2 * nk
                s = core.copy([t, pt_free[z]], PT[:, z, 0:n], bank[:, 0:n])
                core.banks.release(slot, s)
                for b in range(2):
                    for kt in range(qt + 1):
                        t = core.matmul([s, o_free], O[1 + b][:, h * HD:h * HD + HD],
                                        PT[:, z, (b * (qt + 1) + kt) * P:(b * (qt + 1) + kt + 1) * P],
                                        vr[:, 1 + b, kt, g * HD:g * HD + HD], start=kt == 0, stop=kt == qt)
                pt_free[z] = t
        core.dve([core.act.last], V.reciprocal, coef[:], sums[:])
        core.tt([], coef[:], coef[:], gates[:, qt, :].rearrange("p (h b) -> p b h", b=BRANCHES), MUL)
        for b in range(BRANCHES):
            dst = y if b == 0 else yt
            core.tt([t], dst[:, :].rearrange("p (h d) -> p h d", h=HEADS), O[b][:, :].rearrange("p (h d) -> p h d", h=HEADS),
                    wide(coef[:, b, :].unsqueeze(2), [P, HEADS, HD]), MUL)
            if b:
                core.tt([], y[:], y[:], yt[:], ADD)
        o_free = core.dve.last
        s = core.tt([], y[:], y[:], zn[:, qt, :], MUL)
        slot, bank, free = core.banks.take()
        for c in range(FT):
            t = core.pe([s, free], nc.tensor.transpose, bank[:, c * P:c * P + P], y[:, c * P:c * P + P], ident)
        s = core.dve([t], V.tensor_copy, mixT[:, 0:FT, qt * P:qt * P + P], bank[:, :].rearrange("p (c t) -> p c t", c=FT))
        core.banks.release(slot, s)

    for i in range(3):
        view, landed = stream.next()
        for k in range(4):
            for tt in range(NT):
                for n in range(2):
                    t = core.matmul([s, landed], O[2 * tt + n][:, :], mixT[:, 4 * i + k, tt * P:tt * P + P],
                                    view[:, k, n * 512:n * 512 + 512], start=i + k == 0, stop=i == 2 and k == 3, mark=k == 3)
        stream.done(t)
    for tt in range(NT):
        for n in range(2):
            s = core.tt([t], x[:, tt, n * 512:n * 512 + 512], O[2 * tt + n][:, :], x[:, tt, n * 512:n * 512 + 512], ADD)
    return s


def matmul_groups(core, w_stream, tokens, n_out, width, lhs, rhs, use, k_tiles):
    view, landed = w_stream.next()
    for o in range(n_out):
        slot, bank, free = core.banks.take()
        for k in range(k_tiles):
            t = core.matmul([landed, free, *tokens], bank[:, 0:width], lhs(view, o, k), rhs(view, o, k),
                            start=k == 0, stop=k == k_tiles - 1)
        core.banks.release(slot, use(o, bank, t))
    w_stream.done(t)


def turned(core, tokens, srcs, ident, rows=P):
    slot, bank, free = core.banks.take()
    for i, src in enumerate(srcs):
        n = src.shape[-1]
        t = core.pe([*tokens, free], core.nc.tensor.transpose, bank[0:n, i * P:i * P + rows], src,
                    ident[0:rows, 0:rows])
    return slot, bank, t


def second_block(core, A, K, x, out):
    nc = core.nc
    V = nc.vector
    ident = K["ident"]
    with ExitStack() as outer:
        def keep(name, shape, dt=F32):
            return sb(core, outer, "second_" + name, shape, dt)

        gt2, h2 = keep("gt2", [P, D]), keep("h2", [P, NT, D])
        hT = keep("hT", [P, KT, 2 * T])
        with ExitStack() as stack:
            mixers(core, A, K, x, gt2, h2, hT, stack)
            core.restart()
        with ExitStack() as stack:
            experts(core, A, K, x, gt2, h2, hT, out, stack)


def mixers(core, A, K, x, gt2, h2, hT, stack):
    nc = core.nc
    V = nc.vector
    ident = K["ident"]

    def tile(name, shape, dt=F32):
        return sb(core, stack, "m_" + name, shape, dt)

    def rows_of(ap):
        return ap.rearrange("o (k p) n -> p (o k) n", p=P)

    ring = core.ring([tile(f"w{i}", [P, 4096]) for i in range(3)])
    ada = lambda c: (rows_of(A["w_ada_2"][:, :, c * 512:c * 512 + 512]), KT, 512)
    w_in = lambda a, b: (rows_of(A["w_in_2"][:, :, a:b]), KT, b - a)
    stream = WeightStream(core, ring, [
        *(ada(c) for c in (0, 1, 2, 3)), w_in(0, B_QK), w_in(B_QK, B_V), w_in(B_V, B_O),
        w_in(B_O, B_G), w_in(B_G, B_G + 16),
        (rows_of(A["w_uq_2"]), 2, MLA_H * QK), (rows_of(A["w_ukv_2"]), 1, MLA_H * (NOPE + MLA_V)),
        *(ada(c) for c in (4, 5, 6, 7, 8, 9, 10, 11)),
        *((rows_of(A["w_out_2"][:, i * 512:i * 512 + 512, :]), 4, D) for i in range(2))])

    R_C, R_CC, R_G1, R_G2, R_ADA, R_GCQ, R_GKV, R_GML, R_END = 0, 8, 16, 24, 32, 80, 82, 83, 87
    rows = tile("rows", [R_END, P])
    for r, name, k in ((R_C, "c_2", 8), (R_G1, "g_norm1_2", 8), (R_G2, "g_norm2_2", 8),
                       (R_ADA, "b_ada_2", 48), (R_GCQ, "g_cq_2", 2), (R_GKV, "g_ckv_2", 1),
                       (R_GML, "g_mlstm_2", 4)):
        core.load("m_rows", rows[r:r + k, :], A[name].rearrange("o (k p) -> (o k) p", p=P))
    core.load("m_rows", rows[R_CC:R_G1, :], A["c_ctx_2"].rearrange("(k p) -> k p", p=P))
    conv_rows = tile("conv_rows", [3, 512])
    rows_in = core.load("m_rows", conv_rows, A["conv_qk_2"].rearrange("o k c -> (o k) c"))
    gt1, fin_g = tile("gt1", [P, D]), tile("fin_g", [P, D])
    fin_in = core.load("fin_g", fin_g, A["final_g"].rearrange("(o n) -> o n", o=1).to_broadcast([P, D]))
    ctx = tile("ctx", [P, NT, D])
    ctx_in = core.load("ctx", ctx, A["ctx_2"].rearrange("b (t p) d -> p (b t) d", p=P))
    b_if = tile("b_if", [P, 16])
    g_q, g_k = tile("g_q", [P, QK]), tile("g_k", [P, QK])
    core.load("m_small", b_if[:, 0:8], A["b_igate_2"].rearrange("o a b -> o (a b)").to_broadcast([P, 8]))
    core.load("m_small", b_if[:, 8:16], A["b_fgate_2"].rearrange("o a b -> o (a b)").to_broadcast([P, 8]))
    core.load("m_small", g_q, A["g_qn_2"].to_broadcast([P, QK]))
    core.load("m_small", g_k, A["g_kn_2"].to_broadcast([P, QK]))
    for dst, col in ((gt1, 2 * D), (gt2, 5 * D)):
        small_in = core.load("m_small", dst, A["b_ada_2"][:, col:col + D].to_broadcast([P, D]))

    vec = tile("vec", [P, R_END])
    convw = tile("convw", [P, 4, 3])
    slot, bank, t = turned(core, [rows_in], [rows], ident, R_END)
    core.banks.release(slot, core.dve([t], V.tensor_copy, vec, bank[:, 0:R_END]))
    slot, bank, t = turned(core, [rows_in], [conv_rows[:, c * P:c * P + P] for c in range(4)], ident, 3)
    vec_ready = core.dve([t], V.tensor_copy, convw, bank[:, :].rearrange("p (c r) -> p c r", c=4)[:, :, 0:3])
    core.banks.release(slot, vec_ready)

    small, sq = tile("small", [P, 64]), tile("sq", [P, D])
    for tt in range(NT):
        s = core.f([], sq, x[:, tt, :], ACT.Square, accum_out=small[:, tt:tt + 1])
    s = inv_rms(core, [s], small[:, 4:6], small[:, 0:2], D, small[:, 2:4])
    for tt in range(NT):
        x_ready = core.stt([s, fin_in], x[:, tt, :], x[:, tt, :], small[:, 4 + tt:5 + tt], fin_g, MUL, MUL)

    sT, cond = tile("sT", [P, KT, 2]), vec[:, 0:16].rearrange("p (a k) -> p k a", a=2)
    s = core.f([vec_ready], sT, cond, ACT.Sigmoid)
    core.tt([s], sT, sT, cond, MUL)
    s_wide = tile("s_wide", [P, KT, P])
    s_ready = core.dve([], V.tensor_copy, s_wide, wide(sT[:, :, 0:1], [P, KT, P]))

    mod = tile("mod", [P, 48, 2])

    def modulation(c):
        view, landed = stream.next()
        slot, bank, free = core.banks.take()
        for n in range(4):
            for k in range(KT):
                t = core.matmul([landed, s_ready, free], bank[:, 2 * n:2 * n + 2], view[:, k, n * P:n * P + P],
                                sT[:, k, :], start=k == 0, stop=k == KT - 1)
        stream.done(t)
        s = core.tt([t], mod[:, 4 * c:4 * c + 4, :], bank[:, 0:8].rearrange("p (n a) -> p n a", a=2),
                    wide(vec[:, R_ADA + 4 * c:R_ADA + 4 * c + 4].unsqueeze(2), [P, 4, 2]), ADD)
        core.banks.release(slot, s)
        return s

    def gate_row(dst, half):
        matmul_groups(core, stream, [s_ready, small_in], 1, 512, lambda v, o, k: s_wide[:, k, :],
                      lambda v, o, k: v[:, k, :],
                      lambda o, bank, t: core.tt([t], dst[:, half * 512:half * 512 + 512], bank[:, :],
                                                 dst[:, half * 512:half * 512 + 512], ADD), KT)

    for c in range(4):
        mod_ready = modulation(c)
    scale1, scale2 = tile("scale1", [P, 2, KT]), tile("scale2", [P, KT])
    for a in range(2):
        core.ts([], scale1[:, a, :], mod[:, 8:16, a], 1.0, ADD)
        s = core.tt([], scale1[:, a, :], scale1[:, a, :], vec[:, R_G1:R_G1 + 8], MUL)

    xn = h2
    norm_transposed(core, [s, ctx_in], ctx, xn, hT, 0, scale1[:, 1, :], mod[:, 0:8, 1], sq, small, ident)
    core.act.wait(core.dve.last)
    core.dve.wait(core.pe.last)
    h_ready = norm_transposed(core, [s, x_ready], x, xn, hT, T, scale1[:, 0, :], mod[:, 0:8, 0], sq,
                              small, ident)
    TILES = 2 * NT

    cq, ckv = tile("cq", [P, NT, Q_RANK]), tile("ckv", [P, TILES, KV_RANK + ROPE2])
    v_ext = tile("v_ext", [P, TILES, ML_H, ML_V + 1])
    o_gate = tile("o_gate", [P, NT, ML_H * ML_V])
    gates = tile("gates", [P, TILES, 16])
    core.dve([], V.memset, v_ext[:, :, :, ML_V:ML_V + 1], 1.0)

    def token(tile_at):
        return lambda v, o, k: hT[:, k, (tile_at + o) * P:(tile_at + o) * P + P]

    def use_mla(o, bank, t):
        if o >= NT:
            core.dve([t], V.tensor_copy, cq[:, o - NT, :], bank[:, 0:Q_RANK])
        return core.dve([t], V.tensor_copy, ckv[:, o, :], bank[:, Q_RANK:B_QK])

    matmul_groups(core, stream, [h_ready], TILES, B_QK, token(0), lambda v, o, k: v[:, k, :], use_mla, KT)

    qk_lat, k_ctx = tile("qk_lat", [P, 4, T + 2]), tile("k_ctx", [P, 2, T + 2])
    core.dve([], V.memset, qk_lat, 0.0)
    pads = core.dve([], V.memset, k_ctx, 0.0)

    def use_qk(o, bank, t):
        if o < 4:
            return core.dve([t], V.tensor_copy, qk_lat[:, o, 1:T + 1], bank[:, 0:T])
        return core.dve([t], V.tensor_copy, k_ctx[:, o - 4, 1:T + 1], bank[:, 0:T])

    matmul_groups(core, stream, [h_ready], 6, T,
                  lambda v, o, k: v[:, k, (o if o < 4 else o - 2) * P:(o if o < 4 else o - 2) * P + P],
                  lambda v, o, k: hT[:, k, T:2 * T] if o < 4 else hT[:, k, 0:T], use_qk, KT)
    matmul_groups(core, stream, [h_ready], TILES, 512, token(0), lambda v, o, k: v[:, k, :],
                  lambda o, bank, t: core.f([t], v_ext[:, o, :, 0:ML_V],
                                            bank[:, :].rearrange("p (h d) -> p h d", h=ML_H), ACT.Copy), KT)
    matmul_groups(core, stream, [h_ready], NT, 512, token(NT), lambda v, o, k: v[:, k, :],
                  lambda o, bank, t: core.f([t], o_gate[:, o, :], bank[:, :], ACT.Sigmoid), KT)
    matmul_groups(core, stream, [h_ready], TILES, 16, token(0), lambda v, o, k: v[:, k, :],
                  lambda o, bank, t: core.tt([t, small_in], gates[:, o, :], bank[:, 0:16], b_if, ADD), KT)

    mixT = tile("mixT", [P, KT, T])
    whole, mla = tile, ExitStack()

    def tile(name, shape, dt=F32):
        return sb(core, mla, "mla_" + name, shape, dt)

    qnT, qrT = tile("qnT", [P, MLA_H, T]), tile("qrT", [ROPE2, MLA_H, T])
    knT, krT = tile("knT", [P, MLA_H, 2 * T]), tile("krT", [ROPE2, MLA_H, 2 * T])
    vm = tile("vm", [P, TILES, MLA_H, MLA_V])
    cqT, ckvT = tile("cqT", [P, 2, T]), tile("ckvT", [P, 2 * T])
    heads, sq4 = tile("heads", [P, MLA_H, QK]), tile("sq4", [P, MLA_H, QK])
    r1, r2 = tile("r1", [P, MLA_H, 2, 16]), tile("r2", [P, MLA_H, 2, 16])

    def low_rank(src, n_tiles, width, dst_of, g_row):
        for i in range(n_tiles):
            s = core.f([core.dve.last], sq[:, 0:width], src[:, i, 0:width], ACT.Square, accum_out=small[:, i:i + 1])
        s = inv_rms(core, [s], small[:, 16:16 + n_tiles], small[:, 0:n_tiles], width, small[:, 8:8 + n_tiles])
        for i in range(n_tiles):
            s = core.ts([s], src[:, i, 0:width], src[:, i, 0:width], small[:, 16 + i:17 + i], MUL)
        for i in range(n_tiles):
            slot, bank, t = turned(core, [s], [src[:, i, k * P:k * P + P] for k in range(width // P)], ident)
            for k in range(width // P):
                s2 = core.ts([t], dst_of(k, i), bank[:, k * P:k * P + P], vec[:, g_row + k:g_row + k + 1], MUL)
            core.banks.release(slot, s2)
        return s2

    s = low_rank(cq, NT, Q_RANK, lambda k, i: cqT[:, k, i * P:i * P + P], R_GCQ)
    cq_ready = low_rank(ckv, TILES, KV_RANK, lambda k, i: ckvT[:, i * P:i * P + P], R_GKV)

    def head_norm(tokens, g, rope_tile, dstn, dstr, col):
        core.tt(tokens, sq4, heads, heads, MUL)
        core.dve([], V.tensor_reduce, small[:, 24:28], sq4, AX.X, ADD)
        s = inv_rms(core, [], small[:, 32:36], small[:, 24:28], QK, small[:, 28:32])
        core.tt([s, small_in], heads, heads, wide(small[:, 32:36].unsqueeze(2), [P, MLA_H, QK]), MUL)
        core.tt([], heads, heads, wide(g.unsqueeze(1), [P, MLA_H, QK]), MUL)
        if rope_tile is not None:
            r = heads[:, :, NOPE:QK].rearrange("p h (a e d) -> p h a e d", a=2, e=2)
            a, b = r[:, :, :, 0, :], r[:, :, :, 1, :]
            shape = [P, MLA_H, 2, 16]
            c, n = (wide(K[name][:, rope_tile * 32:rope_tile * 32 + 32].rearrange("p (a d) -> p a d", a=2)
                         .unsqueeze(1), shape) for name in ("cos2", "sin2"))
            core.tt([], r1, a, n, MUL)
            core.tt([], r2, b, n, MUL)
            core.tt([], a, a, c, MUL)
            core.tt([], a, a, r2, SUB)
            core.tt([], b, b, c, MUL)
            core.tt([], b, b, r1, ADD)
        s = core.dve.last
        slot, bank, t = turned(core, [s], [heads[:, h, 0:NOPE] for h in range(MLA_H)], ident)
        s = core.copy([t], dstn[:, :, col:col + P], bank[:, :].rearrange("p (h t) -> p h t", h=MLA_H))
        core.banks.release(slot, s)
        slot, bank, t = turned(core, [], [heads[:, h, NOPE:QK] for h in range(MLA_H)], ident)
        s = core.copy([t], dstr[:, :, col:col + P], bank[0:ROPE2, :].rearrange("p (h t) -> p h t", h=MLA_H))
        core.banks.release(slot, s)
        return t

    view, landed = stream.next()
    free_heads = None
    for i in range(NT):
        for half in range(2):
            slot, bank, free = core.banks.take()
            for k in range(2):
                t = core.matmul([landed, s, cq_ready, free], bank[:, 0:2 * QK], cqT[:, k, i * P:i * P + P],
                                view[:, k, half * 2 * QK:half * 2 * QK + 2 * QK], start=k == 0, stop=k == 1)
            s2 = core.dve([t, free_heads], V.tensor_copy, heads[:, 2 * half:2 * half + 2, :],
                          bank[:, 0:2 * QK].rearrange("p (h d) -> p h d", h=2))
            core.banks.release(slot, s2)
        free_heads = head_norm([], g_q, i, qnT, qrT, i * P)
    stream.done(t)
    view, landed = stream.next()
    for i in range(TILES):
        for half in range(2):
            slot, bank, free = core.banks.take()
            t = core.matmul([landed, cq_ready, free], bank[:, :], ckvT[:, i * P:i * P + P],
                            view[:, 0, half * 512:half * 512 + 512])
            b4 = bank[:, :].rearrange("p (h e d) -> p h e d", h=2, e=2)
            core.dve([t, free_heads], V.tensor_copy, heads[:, 2 * half:2 * half + 2, 0:NOPE], b4[:, :, 0, :])
            s2 = core.dve([], V.tensor_copy, vm[:, i, 2 * half:2 * half + 2, :], b4[:, :, 1, :])
            core.banks.release(slot, s2)
        core.dve([], V.tensor_copy, heads[:, :, NOPE:QK],
                 wide(ckv[:, i, KV_RANK:KV_RANK + ROPE2].unsqueeze(1), [P, MLA_H, ROPE2]))
        free_heads = head_norm([], g_k, i - NT if i >= NT else None, knT, krT, i * P)
    stream.done(t)
    k_ready = [core.dve.last, core.act.last]

    gate_row(gt1, 0)
    gate_row(gt1, 1)

    p_sb, PT = (ctx[:, i, :].rearrange("p (b c) -> p b c", b=2) for i in range(2))
    att, den = tile("att", [P, NT, 512]), tile("den", [P, NT, MLA_H])
    scale = QK ** -0.5
    p_free, pt_free, n = [None] * 2, [None] * 2, 0
    for tt in range(NT):
        q = slice(tt * P, tt * P + P)
        for h in range(MLA_H):
            slot, bank, free = core.banks.take()
            core.matmul([k_ready, free], bank[:, :], qnT[:, h, q], knT[:, h, :], start=True, stop=False)
            t = core.matmul([], bank[:, :], qrT[:, h, q], krT[:, h, :], start=False, stop=True)
            m = small[:, 40 + 2 * (n % 2):42 + 2 * (n % 2)]
            core.dve([t, core.act.last], V.tensor_reduce, m[:, 0:1], bank[:, :], AX.X, MAX)
            s = core.ts([], m[:, 1:2], m[:, 0:1], -scale, MUL)
            s = core.f([s, p_free[n % 2]], p_sb[:, n % 2, :], bank[:, :], ACT.Exp, bias=m[:, 1:2], scale=scale,
                       accum_out=den[:, tt, h:h + 1])
            core.banks.release(slot, s)
            slot, bank, t = turned(core, [s], [p_sb[:, n % 2, c * P:c * P + P] for c in range(TILES)], ident)
            p_free[n % 2] = t
            s = core.copy([t, pt_free[n % 2]], PT[:, n % 2, :], bank[:, :])
            core.banks.release(slot, s)
            for c in range(TILES):
                t = core.matmul([s], core.held[tt][:, h * P:h * P + P], PT[:, n % 2, c * P:c * P + P], vm[:, c, h, :],
                                start=c == 0, stop=c == TILES - 1)
            pt_free[n % 2] = t
            n += 1
        core.dve([core.act.last], V.reciprocal, den[:, tt, :], den[:, tt, :])
        s = core.tt([t], att[:, tt, :].rearrange("p (h d) -> p h d", h=MLA_H),
                    core.held[tt][:, :].rearrange("p (h d) -> p h d", h=MLA_H),
                    wide(den[:, tt, :].unsqueeze(2), [P, MLA_H, MLA_V]), MUL)
        slot, bank, t = turned(core, [s], [att[:, tt, c * P:c * P + P] for c in range(4)], ident)
        s = core.dve([t], V.tensor_copy, mixT[:, 0:4, q], bank[:, :].rearrange("p (c t) -> p c t", c=4))
        core.banks.release(slot, s)
    mla.close()
    core.meet()
    with ExitStack() as own:
        mlstm(core, A, K, lambda n, shape, dt=F32: sb(core, own, n, shape, dt), vec, R_GML, convw, qk_lat, k_ctx, pads, v_ext, o_gate, gates, mixT,
              small, ident)
    core.meet()
    tile = whole

    for c in (6, 7, 8, 9):
        modulation(c)
    gate_row(gt2, 0)
    gate_row(gt2, 1)
    core.ts([], scale2, mod[:, 32:40, 0], 1.0, ADD)
    core.tt([], scale2, scale2, vec[:, R_G2:R_G2 + 8], MUL)

    s = [core.dve.last, core.act.last]
    for i in range(2):
        view, landed = stream.next()
        for k in range(4):
            for tt in range(NT):
                for h in range(2):
                    t = core.matmul([s, landed], core.held[2 * tt + h][:, :], mixT[:, 4 * i + k, tt * P:tt * P + P],
                                    view[:, k, h * 512:h * 512 + 512], start=i + k == 0, stop=i == 1 and k == 3, mark=k == 3)
        stream.done(t)
    for tt in range(NT):
        for h in range(2):
            c = slice(h * 512, h * 512 + 512)
            core.tt([t], sq[:, c], core.held[2 * tt + h][:, :], gt1[:, c], MUL)
            s = core.tt([], x[:, tt, c], x[:, tt, c], sq[:, c], ADD)
    core.act.wait(s)
    h2_ready = norm_transposed(core, [s], x, xn, hT, 0, scale2, mod[:, 24:32, 0], sq, small, ident)
    for tt in range(NT):
        for half in range(2):
            slot, bank, t = turned(core, [h2_ready], [hT[:, 4 * half + k, tt * P:tt * P + P] for k in range(4)], ident)
            s = core.copy([t], h2[:, tt, half * 512:half * 512 + 512], bank[:, :])
            core.banks.release(slot, s)
    core.rings.remove(ring)


def mlstm(core, A, K, tile, vec, g_row, convw, qk_lat, k_ctx, pads, v_ext, o_gate, gates, mixT, small, ident):
    nc = core.nc
    V = nc.vector
    ST = 2 * NT
    qT, kT = tile("ml_qT", [P, 2, T]), tile("ml_kT", [P, 2, 2 * T])
    raw, sig = tile("ml_raw", [P, T]), tile("ml_sig", [P, T])
    for c in range(6):
        src = qk_lat[:, c, :] if c < 4 else k_ctx[:, c - 4, :]
        wc = c if c < 4 else c - 2
        core.ts([pads, core.act.last], raw, src[:, 0:T], convw[:, wc, 0:1], MUL)
        core.stt([], raw, src[:, 1:T + 1], convw[:, wc, 1:2], raw, MUL, ADD)
        s = core.stt([], raw, src[:, 2:T + 2], convw[:, wc, 2:3], raw, MUL, ADD)
        s = core.f([s], sig, raw, ACT.Sigmoid)
        if c < 2:
            core.stt([s], qT[:, c, :], raw, ML_QK ** -0.5, sig, MUL, MUL)
        else:
            at = T if c < 4 else 0
            core.tt([s], kT[:, c - 2 if c < 4 else c - 4, at:at + T], raw, sig, MUL)
    qk_ready = core.dve.last

    f = gates[:, :, 8:16]
    tmp = tile("ml_tmp", [P, 6, ST, 8])
    core.stt([], tmp[:, 0], f, -1.0, f, MUL, MAX)
    s = core.f([core.dve.last], tmp[:, 1], tmp[:, 0], ACT.Exp, scale=-1.0)
    log1p_unit(core, [s], tmp[:, 2], tmp[:, 1], tmp[:, 3], tmp[:, 4], tmp[:, 5])
    core.ts([], f, f, 0.0, MIN)
    s = core.tt([], f, f, tmp[:, 2], SUB)

    rows = tile("ml_rows", [ML_H, 4, 2 * T])
    for td in range(4):
        slot, bank, t = turned(core, [s], [gates[:, i, td * 4:td * 4 + 4] for i in range(ST)], ident)
        core.banks.release(slot, core.dve([t], V.tensor_copy, rows[:, td, :], bank[0:ML_H, :]))
    F, G, M = (tile("ml_" + n, [ML_H, 2, 2 * T]) for n in ("F", "G", "M"))
    E = rows[:, 2:4, :]
    ones = K["ones"]
    one = wide(ones[0:ML_H, 0:1], [ML_H, T])
    for d in range(2):
        def order(ap, part):
            a, b = part * T, part * T + T
            if d == 0:
                return ap[:, a:b]
            return ap[:, a:b][:, ::-1]

        def last(ap, part):
            at = part * T + (T - 1 if d == 0 else 0)
            return ap[:, at:at + 1]

        fd, idd = rows[:, 2 + d, :], rows[:, d, :]
        core.dve([], V.tensor_tensor_scan, order(F[:, d, :], 0), one, order(fd, 0), 0.0, MUL, ADD)
        core.dve([], V.tensor_tensor_scan, order(F[:, d, :], 1), one, order(fd, 1), last(F[:, d, :], 0), MUL, ADD)
        core.tt([], G[:, d, :], idd, F[:, d, :], SUB)
        g = G[:, d, :]
        core.dve([], V.tensor_tensor_scan, order(M[:, d, :], 0), order(g, 0), order(g, 0), 0.0, MAX, MAX)
        core.dve([], V.tensor_tensor_scan, order(M[:, d, :], 1), order(g, 1), order(g, 1), last(M[:, d, :], 0), MAX, MAX)
    s = core.tt([], E, F, M, ADD)
    rows_ready = core.f([s], E, E, ACT.Exp, scale=-1.0)
    gcol, ecol = tile("ml_gcol", [P, 2, ST, ML_H]), tile("ml_ecol", [P, NT, ML_H, 2])
    for d in range(2):
        slot, bank, free = core.banks.take()
        for i in range(ST):
            t = core.pe([rows_ready, free], nc.tensor.transpose, bank[:, i * 4:i * 4 + 4],
                        G[:, d, i * P:i * P + P], ident[0:ML_H, 0:ML_H])
        for i in range(NT):
            t = core.pe([], nc.tensor.transpose, bank[:, 16 + i * 4:20 + i * 4],
                        E[:, d, T + i * P:T + i * P + P], ident[0:ML_H, 0:ML_H])
        core.dve([t], V.tensor_copy, gcol[:, d], bank[:, 0:16].rearrange("p (i h) -> p i h", h=ML_H))
        s = core.dve([], V.tensor_copy, ecol[:, :, :, d], bank[:, 16:24].rearrange("p (i h) -> p i h", h=ML_H))
        core.banks.release(slot, s)
    cols_ready = s

    nm, nmm = tile("ml_nm", [P, 2, NT, P]), tile("ml_nmm", [P, 2, NT, P])
    W = tile("ml_W", [P, 2, ST, T])
    hn = tile("ml_hn", [P, NT, ML_H, 2, ML_V + 1])
    w_free, score_free, n = [None] * 2, [None] * 2, 0
    for h in range(ML_H):
        half = slice((h % 2) * ML_QK, (h % 2) * ML_QK + ML_QK)
        score = []
        for part in range(2):
            bank = core.held[2 * (h % 2) + part]
            for e in range(2):
                st = 2 * part + e
                t = core.matmul([qk_ready, score_free[h % 2]], bank[:, e * T:e * T + T], kT[half, h // 2, st * P:st * P + P],
                                qT[half, h // 2, :])
            score.append(bank)
        t_score = t
        for d in range(2):
            b = n % 2
            n += 1
            slot, bank, free = core.banks.take()
            t = core.matmul([rows_ready, free], bank[:, 0:T], K["select"][0:ML_H, h * P:h * P + P], M[:, d, T:2 * T])
            core.ts([t, w_free[b]], nm[:, b], bank[:, 0:T].rearrange("p (i t) -> p i t", i=NT), -1.0, MUL)
            core.banks.release(slot, core.dve.last)
            mask = K["upper"] if d == 0 else K["lower"]
            s = core.tt([], nmm[:, b], nm[:, b], wide(mask.unsqueeze(1), [P, NT, P]), ADD)
            flat = nm[:, b].rearrange("p i t -> p (i t)")
            for st in range(2):
                core.f([s, cols_ready, w_free[b]], W[:, b, st, :], flat, ACT.Exp, bias=gcol[:, d, st, h:h + 1])
            for i in range(NT):
                e = core.f([], W[:, b, 2 + i, i * P:i * P + P], nmm[:, b, i, :], ACT.Exp,
                           bias=gcol[:, d, 2 + i, h:h + 1])
            src_t, dst_t = (2, 1) if d == 0 else (3, 0)
            e = core.f([], W[:, b, src_t, dst_t * P:dst_t * P + P], nm[:, b, dst_t, :], ACT.Exp,
                       bias=gcol[:, d, src_t, h:h + 1])
            pairs = [(2, 0), (3, 1), (src_t, dst_t)]
            core.tt([e, t_score], W[:, b, 0:2, :], W[:, b, 0:2, :], score[0][:, :].rearrange("p (e t) -> p e t", e=2), MUL)
            for st, i in pairs:
                c = slice(i * P, i * P + P)
                s = core.tt([], W[:, b, st, c], W[:, b, st, c],
                            score[1][:, (st - 2) * T + i * P:(st - 2) * T + i * P + P], MUL)
            slot, bank, free = core.banks.take()
            for i in range(NT):
                use = [0, 1] + [st for st, j in sorted(pairs) if j == i]
                for st in use:
                    t = core.matmul([s, free], bank[:, i * (ML_V + 1):(i + 1) * (ML_V + 1)], W[:, b, st, i * P:i * P + P],
                                    v_ext[:, st, h, :], start=st == use[0], stop=st == use[-1])
            w_free[b] = t
            s = core.act([t], nc.scalar.copy, hn[:, :, h, d, :], bank[:, 0:NT * (ML_V + 1)].rearrange("p (i v) -> p i v", i=NT))
            core.banks.release(slot, s)
        score_free[h % 2] = core.dve.last

    den = tile("ml_den", [P, NT * ML_H, 2])
    num = hn.rearrange("p i h d v -> p (i h) d v")
    raw_den = num[:, :, :, ML_V]
    core.ts([core.act.last], den, raw_den, -1.0, MUL)
    core.tt([], den, den, raw_den, MAX)
    core.tt([], den, den, ecol.rearrange("p i h d -> p (i h) d"), MAX)
    core.dve([], V.reciprocal, den, den)
    hs, ht = (W[:, b].rearrange("p s t -> p (s t)").rearrange("p (i v) -> p i v", v=ML_V) for b in range(2))
    shape = [P, NT * ML_H, ML_V]
    core.tt([core.pe.last], hs, num[:, :, 0, 0:ML_V], wide(den[:, :, 0:1], shape), MUL)
    core.tt([], ht, num[:, :, 1, 0:ML_V], wide(den[:, :, 1:2], shape), MUL)
    core.tt([], hs, hs, ht, ADD)
    core.tt([], ht, hs, hs, MUL)
    core.dve([], V.tensor_reduce, small[:, 0:8], ht, AX.X, ADD)
    s = inv_rms(core, [], small[:, 16:24], small[:, 0:8], ML_V, small[:, 8:16])
    core.tt([s], hs, hs, wide(small[:, 16:24].unsqueeze(2), shape), MUL)
    s = core.tt([], hs, hs, o_gate.rearrange("p i (h v) -> p (i h) v", h=ML_H), MUL)
    for i in range(NT):
        slot, bank, t = turned(core, [s], [hs[:, i * ML_H + h, :] for h in range(ML_H)], ident)
        for h in range(ML_H):
            s2 = core.ts([t], mixT[:, 4 + h, i * P:i * P + P], bank[:, h * P:h * P + P],
                         vec[:, g_row + h:g_row + h + 1], MUL)
        core.banks.release(slot, s2)


def experts(core, A, K, x, gt2, h2, hT, out, stack):
    nc = core.nc
    V = nc.vector
    ident = K["ident"]
    BUFS, BATCH = TOPK, 4
    BATCHES = NT * TOPK // BATCH

    def tile(name, shape, dt=F32):
        return sb(core, stack, "e_" + name, shape, dt)

    rows_uv = [tile(f"uv{j}", [P, 2 * D]) for j in range(BUFS)]
    idx = [tile(f"idx{j}", [P, 1], U32) for j in range(BUFS)]
    diag = [tile(f"diag{j}", [P, P]) for j in range(BUFS)]
    dot, act, w = tile("dot", [P, BUFS]), tile("act", [P, BUFS]), tile("w", [P, BUFS])
    chosen, weight = tile("chosen", [P, NT, SLOTS], U32), tile("weight", [P, NT, SLOTS])
    w_pq, keys, keysT = tile("w_pq", [P, KT, 2 * P]), tile("keys", [P, 2, P]), tile("keysT", [P, 2, P])
    qT, scores = tile("qT", [P, 2, T]), tile("scores", [P, NT, 2, N_KEYS])
    rest = tile("rest", [P, TOPK * TOPK])
    sv, si, sif = tile("sv", [P, NT, 2, TOPK]), tile("si", [P, NT, 2, TOPK], U32), tile("sif", [P, NT, 2, TOPK])
    cand, hot = tile("cand", [P, NT, TOPK * TOPK]), tile("hot", [P, NT, TOPK, TOPK])
    best, pos = tile("best", [P, NT, TOPK]), tile("pos", [P, NT, TOPK], U32)
    part, partf, e01 = tile("part", [P, NT, TOPK], U32), tile("partf", [P, NT, TOPK]), tile("e01", [P, 2, NT, TOPK])
    gap, norm = tile("gap", [P, NT, TOPK]), tile("norm", [P, NT])

    sem = nc.alloc_semaphore
    landed, free = ([sem(f"{name}{j}") for j in range(BUFS)] for name in ("uv_in", "uv_free"))
    idx_set = [sem(f"idx_set{j}") for j in range(BUFS)]
    seen, dots_done, gelu_done, diags_done = (
        sem(n) for n in ("indices_seen", "dots_done", "gelu_done", "diags_done"))
    w_in, keys_in, keys_turned, queries_done, scores_done, keysT_set, qT_set, scores_set, scores_seen, best_set, exp_set, routed = (
        sem(n) for n in ("w_pq_in", "keys_in", "keys_turned", "queries_done", "scores_done", "keysT_set",
                         "qT_set", "scores_set", "scores_seen", "best_set", "exp_set", "routed"))
    steps = Lane(nc, nc.vector, "steps", True)
    acc = [core.held[0:2], core.held[2:4]]
    bank_k, bank_q, bank_s = core.banks.items[0:3]
    table = A["experts"]

    def after(engine, sem, heads):
        if not isinstance(heads, int) or heads > 0:
            engine.wait_ge(sem, heads)

    def load_head(head):
        w_cols = A["w_pq_2"][:, :, bass.ds(head * 2 * P, 2 * P)]
        after(nc.sync, keys_turned, head)
        nc.sync.dma_start(keys, A["sub_keys_2"][:, bass.ds(head, 1)].rearrange("o h a k d -> k (o h a) d")).then_inc(keys_in, 16)
        after(nc.sync, queries_done, head)
        nc.sync.dma_start(w_pq, w_cols.rearrange("o (k p) n -> p (o k) n", p=P)).then_inc(w_in, 16)

    def product_keys(head):
        def keys_step():
            nc.tensor.wait_ge(keys_in, head * 16 + 16)
            for a in range(2):
                t = nc.tensor.transpose(bank_k[:, a * P:a * P + P], keys[:, a, :], ident)
            t.then_inc(keys_turned, 1)
            nc.scalar.wait_ge(keys_turned, head + 1)
            nc.scalar.copy(keysT, bank_k[:, 0:2 * P].rearrange("p (a k) -> p a k", a=2)).then_inc(keysT_set, 1)
            nc.tensor.wait_ge(w_in, head * 16 + 16)
            queries(0)

        def queries(a):
            for k in range(KT):
                t = nc.tensor.matmul(bank_q[:, a * T:a * T + T], w_pq[:, k, a * P:a * P + P], hT[:, k, 0:T],
                                     start=k == 0, stop=k == KT - 1)
            return t

        def queries_step():
            queries(1).then_inc(queries_done, 1)
            nc.scalar.wait_ge(queries_done, head + 1)
            nc.scalar.copy(qT, bank_q[:, :].rearrange("p (a t) -> p a t", a=2)).then_inc(qT_set, 1)

        def scores_step():
            nc.tensor.wait_ge(keysT_set, head + 1)
            nc.tensor.wait_ge(qT_set, head + 1)
            for tt in range(NT):
                for a in range(2):
                    t = nc.tensor.matmul(bank_s[:, (2 * tt + a) * P:(2 * tt + a) * P + P],
                                         qT[:, a, tt * P:tt * P + P], keysT[:, a, :], start=True, stop=True)
            t.then_inc(scores_done, 1)
            nc.scalar.wait_ge(scores_done, head + 1)
            after(nc.scalar, routed, head)
            nc.scalar.copy(scores, bank_s[:, :].rearrange("p (t a k) -> p t a k", t=NT, a=2)).then_inc(scores_set, 1)

        return [keys_step, queries_step, scores_step]

    def top16(values, scratch, out_v, out_i):
        steps([], V.max, out_v[:, 0:8], values)
        steps([], V.max_index, out_i[:, 0:8], out_v[:, 0:8], values)
        steps([], V.match_replace, scratch, out_v[:, 0:8], values, -3e38)
        steps([], V.max, out_v[:, 8:16], scratch)
        steps([], V.max_index, out_i[:, 8:16], out_v[:, 8:16], scratch)

    def route(head):
        shape = [P, NT, TOPK, TOPK]
        col = bass.ds(head * TOPK, TOPK)

        def halves(tt):
            if tt == 0:
                nc.vector.wait_ge(scores_set, head + 1)
                nc.vector.sem_inc(scores_seen, 1)
            for a in range(2):
                top16(scores[:, tt, a, :], rest[:, 0:N_KEYS], sv[:, tt, a, :], si[:, tt, a, :])

        def candidates():
            steps([], V.tensor_copy, sif, si)
            steps([], V.tensor_tensor, cand.rearrange("p t (i j) -> p t i j", i=TOPK),
                  wide(sv[:, :, 0, :].unsqueeze(3), shape), wide(sv[:, :, 1, :].unsqueeze(2), shape), ADD)
            for tt in range(NT):
                top16(cand[:, tt, :], rest, best[:, tt, :], pos[:, tt, :])
            steps([], V.tensor_tensor, gap, best, wide(best[:, :, 0:1], [P, NT, TOPK]), SUB)
            nc.vector.wait_ge(*steps.last)
            nc.vector.sem_inc(best_set, 1)
            nc.scalar.wait_ge(best_set, head + 1)
            nc.scalar.activation(best, gap, ACT.Exp).then_inc(exp_set, 1)

        def places():
            iota = wide(K["iota"].unsqueeze(1).unsqueeze(1), shape)
            for a, (op, by) in enumerate(((ALU.logical_shift_right, 4), (ALU.bitwise_and, 15))):
                steps([], V.tensor_scalar, part, pos, by, None, op)
                steps([], V.tensor_copy, partf, part)
                steps([], V.tensor_tensor, hot, wide(partf.unsqueeze(3), shape), iota, ALU.is_equal)
                steps([], V.tensor_tensor, hot, hot, wide(sif[:, :, a, :].unsqueeze(2), shape), MUL)
                steps([], V.tensor_reduce, e01[:, a], hot, AX.X, ADD)

        def weights():
            steps([], V.scalar_tensor_tensor, e01[:, 0], e01[:, 0], float(N_KEYS), e01[:, 1], MUL, ADD)
            steps([], V.tensor_copy, chosen[:, :, col], e01[:, 0])
            nc.vector.wait_ge(exp_set, head + 1)
            steps([], V.tensor_reduce, norm, best, AX.X, ADD)
            steps([], V.reciprocal, norm, norm)
            steps([], V.tensor_tensor, weight[:, :, col], best, wide(norm.unsqueeze(2), [P, NT, TOPK]), MUL)
            nc.vector.wait_ge(*steps.last)
            nc.vector.sem_inc(routed, 1)

        return [lambda: halves(0), lambda: halves(1), candidates, places, weights]

    def rewind():
        nc.vector.wait_ge(*steps.last)
        nc.vector.sem_clear(steps.sem)
        steps.clear()

    def gather(turn):
        nc.gpsimd.wait_ge(routed, turn + 1)
        for n in range(NT * TOPK):
            tt, j = divmod(n, BUFS)
            use = turn * NT + tt
            nc.gpsimd.wait_ge(free[j], use + 1)
            nc.gpsimd.tensor_copy(idx[j], chosen[:, tt, bass.ds(turn * TOPK + j, 1)]).then_inc(idx_set[j], 1)
            nc.gpsimd.wait_ge(idx_set[j], use + 1)
            nc.gpsimd.sem_inc(seen, 1)
            nc.gpsimd.indirect_dma_start(out=rows_uv[j], out_offset=None, in_=table,
                                         in_offset=bass.IndirectOffsetOnAxis(ap=idx[j], axis=0)).then_inc(landed[j], 16)

    def dots(turn, b):
        tt, j0 = divmod(b * BATCH, BUFS)
        for j in range(j0, j0 + BATCH):
            nc.vector.wait_ge(landed[j], turn * 32 + (tt * 16 + 16))
            u = rows_uv[j][:, 0:D]
            ins = nc.vector.tensor_tensor_reduce(u, u, h2[:, tt, :], 1.0, 0.0, MUL, ADD, dot[:, j:j + 1])
        ins.then_inc(dots_done, 1)
        nc.scalar.wait_ge(dots_done, turn * BATCHES + (b + 1))
        nc.scalar.activation(act[:, j0:j0 + BATCH], dot[:, j0:j0 + BATCH], ACT.Gelu).then_inc(gelu_done, 1)

    def add(turn, b):
        tt, j0 = divmod(b * BATCH, BUFS)
        cols = slice(j0, j0 + BATCH)
        nc.vector.wait_ge(gelu_done, turn * BATCHES + (b + 1))
        steps([], V.tensor_tensor, w[:, cols], act[:, cols], weight[:, tt, bass.ds(turn * TOPK + j0, BATCH)], MUL)
        nc.vector.wait_ge(*steps.last)
        for j in range(j0, j0 + BATCH):
            ins = nc.vector.tensor_scalar(diag[j], ident, w[:, j:j + 1], None, MUL)
        ins.then_inc(diags_done, 1)
        nc.tensor.wait_ge(diags_done, turn * BATCHES + (b + 1))
        for j in range(j0, j0 + BATCH):
            for h in range(2):
                ins = nc.tensor.matmul(acc[tt][h], diag[j], rows_uv[j][:, D + h * 512:D + h * 512 + 512],
                                       start=False, stop=False, skip_group_check=True)
            ins.then_inc(free[j], 1)

    def experts_of(turn, between):
        for b in range(BATCHES):
            dots(turn, b)
            for step in between[b]:
                step()
            if b:
                add(turn, b - 1)
        add(turn, BATCHES - 1)
        rewind()

    for tt in range(NT):
        for h in range(2):
            core.matmul([], acc[tt][h], K["zeros"], h2[:, tt, h * 512:h * 512 + 512], start=True, stop=False,
                        mark=False)
    for j in range(BUFS):
        nc.tensor.sem_inc(free[j], 1)
    for head in range(2):
        load_head(head)
        for step in product_keys(head) + route(head):
            step()
        rewind()
    with nc.Fori(0, PEER_H - 2) as turn:
        head = turn + 2
        load_head(head)
        gather(turn)
        pk, rt = product_keys(head), route(head)
        experts_of(turn, [pk[0:1], pk[1:2], pk[2:3], rt[0:1], rt[1:2], rt[2:3], rt[3:4], rt[4:5]])
    with nc.Fori(PEER_H - 2, PEER_H) as turn:
        gather(turn)
        experts_of(turn, [[]] * BATCHES)
    stored = nc.alloc_semaphore("stored")
    for tt in range(NT):
        for h in range(2):
            t = core.matmul([], acc[tt][h], K["zeros"], h2[:, tt, h * 512:h * 512 + 512], start=False, stop=True)
    for tt in range(NT):
        for h in range(2):
            c = slice(h * 512, h * 512 + 512)
            core.tt([t], h2[:, tt, c], acc[tt][h], gt2[:, c], MUL)
            s = core.tt([], x[:, tt, c], x[:, tt, c], h2[:, tt, c], ADD)
        core.sp.wait(s)
        nc.sync.dma_start(out[tt * P:tt * P + P, :], x[:, tt, :]).then_inc(stored, 16)
    nc.sync.wait_ge(stored, 16 * NT)


def program(nc, A, out):
    core = Core(nc)
    _, where = constants()
    x = nc.alloc_sbuf_tensor("x_sb", [P, NT, D], F32)[:]
    table = nc.alloc_sbuf_tensor("constants", [P, max(b for _, b in where.values())], F32)[:]
    K = {name: table[:, a:b] for name, (a, b) in where.items()}
    zeros = where["zeros"][0]
    K["mask2"] = table[:, zeros:zeros + 2 * P]
    K["ready"] = core.load("constants", table, A["constants"])
    x_in = core.load("x", x, A["x"].rearrange("b (t p) d -> p (b t) d", p=P))
    core.sp.wait(x_in, K["ready"])
    first_block(core, A, K, x)
    second_block(core, A, K, x, out)


_USED = ["x", "positions", "norm_g", "w_in", "b_gate", "cmp_pos", "cmp_w1", "cmp_w2", "lru_conv_w",
         "lru_conv_b", "lru_w_a", "lru_b_a", "lru_w_i", "lru_b_i", "lru_lam", "conv_dw_w",
         "conv_dw_b", "conv_ln_g", "conv_ln_b", "conv_w_pw2", "w_out", "final_g", "c_2", "ctx_2",
         "c_ctx_2", "w_ada_2", "b_ada_2", "g_norm1_2", "w_in_2", "g_cq_2", "w_uq_2", "g_ckv_2",
         "w_ukv_2", "g_qn_2", "g_kn_2", "conv_qk_2", "b_igate_2", "b_fgate_2", "g_mlstm_2",
         "w_out_2", "g_norm2_2", "w_pq_2", "sub_keys_2", "expert_u_2", "expert_v_2"]


def kernel(**inputs):
    import concourse.bacc as bacc
    from concourse.bass_utils import run_bass_kernel_spmd

    nc = bacc.Bacc("TRN2", target_bir_lowering=False, num_devices=1)
    arrays, A = {}, {}
    rows = np.concatenate([inputs["expert_u_2"][0], inputs["expert_v_2"][0]], axis=1)
    for name, a in [("constants", constants()[0]), ("experts", rows)] + [(n, inputs[n]) for n in _USED]:
        a = np.ascontiguousarray(a)
        arrays[f"in_{name}_dram"] = a
        A[name] = nc.dram_tensor(f"in_{name}_dram", a.shape, mybir.dt.from_np(a.dtype), kind="ExternalInput").ap()
    out = nc.dram_tensor("out_0_dram", (T, D), F32, kind="ExternalOutput").ap()
    program(nc, A, out)
    r = run_bass_kernel_spmd(nc, [arrays], core_ids=[0])
    return r.results[0]["out_0_dram"].reshape(1, T, D)
```

```python
from contextlib import ExitStack

import numpy as np
import concourse.bass as bass
from concourse import mybir

F32 = mybir.dt.float32
I32 = mybir.dt.int32
U32 = mybir.dt.uint32
ALU = mybir.AluOpType
ACT = mybir.ActivationFunctionType
AX = mybir.AxisListType
MUL, ADD, SUB, MAX, MIN = ALU.mult, ALU.add, ALU.subtract, ALU.max, ALU.min

P = 128
T = 256
NT = T // P
D = 1024
KT = D // P
DEPTH = 2
EPS = 1e-6
NEG = -1e30

HEADS, KV, HD = 8, 2, 64
REP = HEADS // KV
WIDE = 512
FT = WIDE // P
NCMP, CMP_PAD, L_CMP, S_CMP, CMP_HID = 15, 16, 32, 16, 256
LRU_C = 8.0
LRU_TAPS, DW_TAPS = 4, 31
BRANCHES = 3
TAPS_AT_ONCE = 5
C_Q, C_KVC, C_KVW, C_ZN = 0, 512, 1024, 1304
C_ULRU, C_ZLRU, C_GA, C_GB, C_ZC = 1816, 2328, 2840, 3352, 3864

MLA_H, NOPE, ROPE2, MLA_V = 4, 128, 64, 128
QK = NOPE + ROPE2
Q_RANK, KV_RANK = 256, 128
ML_H, ML_QK, ML_V = 4, 64, 128
MLA_COLS = Q_RANK + KV_RANK + ROPE2
B_QK = MLA_COLS
B_V = B_QK + 2 * ML_H * ML_QK
B_O = B_V + ML_H * ML_V
B_G = B_O + ML_H * ML_V
PEER_H, N_KEYS, TOPK = 8, 128, 16
SLOTS = PEER_H * TOPK

ROW_DW, ROW_LC, ROW_LCB, ROW_BA, ROW_BI, ROW_LAM, ROW_DWB, ROW_LNG, ROW_LNB, N_ROWS = (
    0, 31, 35, 36, 37, 38, 39, 40, 41, 42)


def constants():
    p, f = np.arange(P)[:, None], np.arange(P)[None, :]
    t = np.arange(T).reshape(NT, P)
    n = np.arange(CMP_PAD)
    parts = {}
    parts["ident"] = np.eye(P)
    parts["zeros"] = np.zeros((P, P))
    parts["lower"] = np.where(f <= p, 0.0, NEG)
    parts["upper"] = np.where(f >= p, 0.0, NEG)
    ok = (n[None, None] < NCMP) & (n[None, None] * S_CMP + L_CMP - 1 <= t.T[:, :, None])
    parts["cmp_neg"] = np.where(ok, 0.0, NEG).reshape(P, -1)
    parts["cmp_one"] = ok.astype(float).reshape(P, -1)
    parts["blocks"] = (np.arange(P)[:, None] // CMP_PAD == np.arange(HEADS)[None]).astype(float)
    inv = (np.float32(10000.0) ** (-np.arange(0, HD, 2, dtype=np.float32) / np.float32(HD)))
    parts["inv_freq"] = np.broadcast_to(inv, (P, HD // 2))
    half = ROPE2 // 4
    inv2 = np.float32(10000.0) ** (-np.arange(half, dtype=np.float32) * np.float32(2.0 / (2 * half)))
    ang = np.stack([(t // 64).T, (t % 64).T], -1).astype(np.float32)[..., None] * inv2
    parts["cos2"] = np.cos(ang).reshape(P, -1)
    parts["sin2"] = np.sin(ang).reshape(P, -1)
    sel = np.zeros((P, ML_H, P))
    sel[np.arange(ML_H), np.arange(ML_H)] = 1.0
    parts["select"] = sel.reshape(P, -1)
    parts["iota"] = np.broadcast_to(np.arange(TOPK), (P, TOPK))
    parts["ones"] = np.ones((P, P))
    at, where = 0, {}
    for name, a in parts.items():
        where[name] = (at, at + a.shape[1])
        at += a.shape[1]
    return np.concatenate(list(parts.values()), 1).astype(np.float32), where


class Lane:

    def __init__(self, nc, engine, name, chained):
        self.engine, self.sem, self.chained = engine, nc.alloc_semaphore(name), chained
        self.count, self.seen = 0, {}

    def wait(self, *tokens):
        for token in tokens:
            if isinstance(token, list):
                self.wait(*token)
            elif token is not None and self.seen.get(token[0].name, 0) < token[1]:
                self.engine.wait_ge(token[0], token[1])
                self.seen[token[0].name] = token[1]

    @property
    def last(self):
        return (self.sem, self.count) if self.count else None

    def __call__(self, tokens, issue, *args, mark=True, behind=None, **kw):
        self.wait(*tokens)
        if self.chained:
            self.wait(behind or self.last)
        ins = issue(*args, **kw)
        if mark:
            ins.then_inc(self.sem, 1)
            self.count += 1
        return self.last

    def clear(self):
        self.count, self.seen = 0, {}


class Arrivals:

    def __init__(self, nc, name):
        self.nc, self.sem, self.count = nc, nc.alloc_semaphore(name), 0

    def load(self, lane, tokens, out, in_, **kw):
        lane.wait(*tokens)
        lane.engine.dma_start(out, in_, **kw).then_inc(self.sem, 16)
        self.count += 16
        return (self.sem, self.count)

    def clear(self):
        self.count = 0


class Ring:

    def __init__(self, items):
        self.items = items
        self.clear()

    def take(self):
        n = len(self.items)
        self.at = next(i % n for i in range(self.at + 1, self.at + 1 + n) if not self.taken[i % n])
        self.taken[self.at] = True
        return self.at, self.items[self.at], self.free[self.at]

    def release(self, slot, token):
        self.free[slot], self.taken[slot] = token, False

    def clear(self):
        n = len(self.items)
        self.free, self.taken, self.at = [None] * n, [False] * n, -1


class WeightStream:

    def __init__(self, core, ring, plan):
        self.core, self.ring, self.plan, self.ready = core, ring, list(plan), []
        for _ in ring.items:
            self.fetch()

    def fetch(self):
        if self.plan:
            src, k, n = self.plan.pop(0)
            slot, buf, free = self.ring.take()
            view = buf[:, 0:k * n].rearrange("p (k n) -> p k n", k=k)
            self.ready.append((slot, view, self.core.load(f"weights{slot}", view, src, [free])))

    def next(self):
        return self.ready[0][1:]

    def done(self, token):
        self.drop(self.hold(), token)

    def hold(self):
        return self.ready.pop(0)

    def drop(self, held, token):
        self.ring.release(held[0], token)
        self.fetch()


class Core:

    def __init__(self, nc):
        self.nc = nc
        self.dve = Lane(nc, nc.vector, "dve_done", True)
        self.act = Lane(nc, nc.scalar, "act_done", True)
        self.pool = Lane(nc, nc.gpsimd, "pool_done", True)
        self.pe = Lane(nc, nc.tensor, "pe_done", False)
        self.sp = Lane(nc, nc.sync, "sp_done", False)
        self.lanes = [self.dve, self.act, self.pool, self.pe, self.sp]
        self.streams, self.rings = {}, []
        self.flip = 0
        banks = [nc.alloc_psum_tensor(f"bank{i}", [P, 512], F32)[:] for i in range(8)]
        self.banks = self.ring([b for b in banks[:4]])
        self.held = banks[4:]

    def ring(self, items):
        r = Ring(items)
        self.rings.append(r)
        return r

    def stream(self, name):
        if name not in self.streams:
            self.streams[name] = Arrivals(self.nc, "in_" + name)
        return self.streams[name]

    def load(self, name, out, in_, tokens=(), lane=None, **kw):
        return self.stream(name).load(lane or self.sp, tokens, out, in_, **kw)

    def meet(self):
        done = [lane.last for lane in self.lanes]
        for lane in self.lanes:
            lane.wait(*done)

    def restart(self):
        for s in self.streams.values():
            self.sp.wait((s.sem, s.count) if s.count else None)
        self.nc.all_engine_barrier()
        for s in [*self.lanes, *self.streams.values()]:
            self.nc.gpsimd.sem_clear(s.sem)
        self.nc.all_engine_barrier()
        for s in [*self.lanes, *self.streams.values(), *self.rings]:
            s.clear()

    def matmul(self, tokens, out, lhsT, rhs, start=True, stop=True, mark=None, **kw):
        return self.pe(tokens, self.nc.tensor.matmul, out, lhsT, rhs, start=start, stop=stop,
                       mark=stop if mark is None else mark, **kw)

    def copy(self, tokens, out, in_):
        self.flip ^= 1
        if self.flip:
            return self.dve(tokens, self.nc.vector.tensor_copy, out, in_)
        return self.act(tokens, self.nc.scalar.copy, out, in_)

    def tt(self, tokens, out, a, b, op):
        return self.dve(tokens, self.nc.vector.tensor_tensor, out, a, b, op)

    def ts(self, tokens, out, a, s1, op0, s2=None, op1=None):
        if s2 is None:
            return self.dve(tokens, self.nc.vector.tensor_scalar, out, a, s1, None, op0)
        return self.dve(tokens, self.nc.vector.tensor_scalar, out, a, s1, s2, op0, op1)

    def stt(self, tokens, out, a, s, b, op0, op1, **kw):
        return self.dve(tokens, self.nc.vector.scalar_tensor_tensor, out, a, s, b, op0, op1, **kw)

    def f(self, tokens, out, a, func, **kw):
        return self.act(tokens, self.nc.scalar.activation, out, a, func, **kw)


def wide(ap, shape):
    return ap.to_broadcast(shape)


def sb(core, stack, name, shape, dt=F32):
    return stack.enter_context(core.nc.sbuf_tensor(name, shape, dt))[:]


def inv_rms(core, tokens, out, sums, width, scratch):
    core.ts(tokens, scratch, sums, 1.0 / width, MUL, EPS, ADD)
    t = core.dve([], core.nc.vector.reciprocal, scratch, scratch)
    return core.f([t], out, scratch, ACT.Sqrt)


def normed(core, ready, x, xn, sq, small):
    for tt in range(NT):
        s = core.f(ready, sq, x[:, tt, :], ACT.Square, accum_out=small[:, tt:tt + 1])
    s = inv_rms(core, [s], small[:, 4:6], small[:, 0:2], D, small[:, 2:4])
    for tt in range(NT):
        s = core.ts([s], xn[:, tt, :], x[:, tt, :], small[:, 4 + tt:5 + tt], MUL)
    return s


def scaled_transposed(core, ready, xn, hT, col, scale, shift, ident):
    for k in range(KT):
        slot, bank, free = core.banks.take()
        for tt in range(NT):
            t = core.pe([ready, free], core.nc.tensor.transpose, bank[:, tt * P:tt * P + P],
                        xn[:, tt, k * P:k * P + P], ident)
        if shift is None:
            t = core.ts([t], hT[:, k, col:col + T], bank[:, 0:T], scale[:, k:k + 1], MUL)
        else:
            t = core.ts([t], hT[:, k, col:col + T], bank[:, 0:T], scale[:, k:k + 1], MUL,
                        shift[:, k:k + 1], ADD)
        core.banks.release(slot, t)
    return t


def log1p_unit(core, tokens, out, z, s, s2, acc):
    core.ts(tokens, s, z, 2.0, ADD)
    core.dve([], core.nc.vector.reciprocal, s, s)
    core.tt([], s, s, z, MUL)
    core.tt([], s2, s, s, MUL)
    core.ts([], acc, s2, 1.0 / 17, MUL, 1.0 / 15, ADD)
    for odd in (13, 11, 9, 7, 5, 3, 1):
        core.tt([], acc, acc, s2, MUL)
        core.ts([], acc, acc, 1.0 / odd, ADD)
    core.tt([], acc, acc, s, MUL)
    return core.ts([], out, acc, 2.0, MUL)


def rope_angles(core, ready, pos, inv_freq, cos, sin, ang, turns):
    two_pi, magic = 2 * np.pi, 1.5 * 2.0**23
    part1 = 6.28125
    part2 = float(np.float32(np.round((two_pi - part1) * 2**21) / 2**21))
    part3 = two_pi - part1 - part2
    edge = 3.1415925
    for tt in range(NT):
        core.ts(ready, ang[:, tt, :], inv_freq, pos[:, tt:tt + 1], MUL)
    core.ts([], turns, ang, 1.0 / two_pi, MUL)
    core.ts([], turns, turns, magic, ADD)
    core.ts([], turns, turns, magic, SUB)
    for part in (part1, part2, part3):
        core.stt([], ang, turns, -part, ang, MUL, ADD)
    s = core.ts([], ang, ang, edge, MIN, -edge, MAX)
    core.f([s], sin, ang, ACT.Sin)
    core.stt([], turns, ang, -1.0, ang, MUL, MAX)
    s = core.ts([], turns, turns, -1.0, MUL, np.pi / 2, ADD)
    return core.f([s], cos, turns, ACT.Sin)


def first_block(core, A, K, x):
    nc = core.nc
    with ExitStack() as stack:
        def tile(name, shape, dt=F32):
            return sb(core, stack, name, shape, dt)

        w = core.ring([tile(f"weights{i}", [P, 4096]) for i in range(4)])
        tiles = {}
        for name, shape in (
                ("hT", [P, KT, T]), ("xn", [P, NT, D]), ("sq", [P, D]), ("small", [P, 8]),
                ("rows", [N_ROWS, WIDE]), ("vec", [P, FT, N_ROWS]), ("sp8", [P, FT]), ("sc", [P, 24]),
                ("grows", [KT, P]), ("gT", [P, KT]), ("b_gate", [P, 24]),
                ("cos", [P, NT, 32]), ("sin", [P, NT, 32]), ("ang", [P, NT, 32]), ("turns", [P, NT, 32]),
                ("posf", [P, NT]),
                ("ubuf", [P, FT, DW_TAPS - 1 + T]), ("conv", [P, FT, T]), ("fa", [P, FT, T]),
                ("fb", [P, FT, T]), ("fc", [P, FT, T]), ("fd", [P, FT, T]), ("lbuf", [P, FT, LRU_TAPS - 1 + T]), ("xc", [P, FT, T]),
                ("qr", [P, NT, WIDE]), ("kr", [P, 3, NT, P]), ("vr", [P, 3, NT, P]),
                ("r1", [P, WIDE // 2]), ("r2", [P, WIDE // 2]),
                ("qT", [P, FT, T]), ("kT", [P, 2, T]), ("pair", [P, 2, KV, T]), ("cT", [P, 2, T]),
                ("pos_rows", [16, 2, P]), ("posT", [P, 2, 16]), ("blk", [P, 2, 16, KV * CMP_PAD]),
                ("hidT", [P, 2, 2, KV * CMP_PAD]), ("hid_rep", [P, 2, HEADS, CMP_PAD]), ("sig32", [P, 32]),
                ("w2", [P, 2, 2, HD]), ("kcT", [P, CMP_PAD]), ("vcb", [P, HEADS, HD]),
                ("gates", [P, NT, 24]), ("zn", [P, NT, WIDE]), ("mixT", [P, 12, T]),
                ("S", [P, 4, T]), ("mx", [P, 4]), ("sums", [P, NT, 3, HEADS]),
                ("pc", [P, HEADS, CMP_PAD]), ("mc", [P, HEADS]), ("PT", [P, 3, 512]),
                ("y", [P, WIDE]), ("yt", [P, WIDE]), ("coef", [P, 3, HEADS]), ("bd", [P, 2, FT, P])):
            tiles[name] = tile(name, shape)
        posi = tile("posi", [P, NT], I32)
        core.dve([], nc.vector.memset, tiles["bd"][:], 0.0)
        core.dve([], nc.vector.memset, tiles["ubuf"][:], 0.0)
        core.dve([], nc.vector.memset, tiles["lbuf"][:], 0.0)
        core.dve([], nc.vector.memset, tiles["blk"][:], 0.0)
        s = core.load("pos", posi[:], A["positions"].rearrange("b (t p) -> p (b t)", p=P),
                      allow_slow_non_contiguous=True)
        s = core.dve([s, K["ready"]], nc.vector.tensor_copy, tiles["posf"][:], posi[:])
        rope_angles(core, [s], tiles["posf"], K["inv_freq"], tiles["cos"][:], tiles["sin"][:],
                    tiles["ang"], tiles["turns"][:])
        products = tiles["xn"].rearrange("p t (h c n) -> p (t h) c n", h=2, n=T)
        tap_ring = core.ring([products[:, i] for i in range(4)])
        core.restart()
        with nc.Fori(0, DEPTH) as layer:
            first_layer(core, A, K, x, w, tap_ring, tiles, layer)
            core.restart()
        core.rings.remove(w)
        core.rings.remove(tap_ring)


def first_layer(core, A, K, x, w, tap_ring, tl, layer):
    nc = core.nc
    V = nc.vector
    one = bass.ds(layer, 1)
    ident = K["ident"]
    hT, vec, mixT = tl["hT"], tl["vec"], tl["mixT"]

    def rows_of(ap):
        return ap.rearrange("o (k p) n -> p (o k) n", p=P)

    rows = tl["rows"]
    core.load("rows", tl["grows"][:], A["norm_g"][one, :].rearrange("o (k p) -> (o k) p", p=P))
    core.load("rows", rows[ROW_DW:ROW_LC, :], A["conv_dw_w"][one].rearrange("o k c -> (o k) c"))
    core.load("rows", rows[ROW_LC:ROW_LCB, :], A["lru_conv_w"][one].rearrange("o k c -> (o k) c"))
    for r, name in ((ROW_LCB, "lru_conv_b"), (ROW_BA, "lru_b_a"), (ROW_BI, "lru_b_i"),
                    (ROW_LAM, "lru_lam"), (ROW_DWB, "conv_dw_b"), (ROW_LNG, "conv_ln_g"),
                    (ROW_LNB, "conv_ln_b")):
        rows_in = core.load("rows", rows[r:r + 1, :], A[name][one, :])

    core.load("misc", tl["b_gate"][:], A["b_gate"][one, :].to_broadcast([P, 24]))
    core.load("misc", tl["pos_rows"][:], A["cmp_pos"][one].rearrange("o b (j e) d -> j (o b) (e d)", e=2))
    misc_in = core.load("misc", tl["w2"][:], A["cmp_w2"][one].rearrange("o b (k p) d -> p (o b) k d", p=P))

    stream = WeightStream(core, w, [
        *((rows_of(A["w_in"][one, :, c0:c0 + n]), KT, n) for c0, n in (
            (C_GB, WIDE), (C_GA, WIDE), (C_ULRU, WIDE), (C_Q, WIDE), (C_KVC, WIDE),
            (C_KVW, C_ZN - C_KVW), (C_ZN, WIDE), (C_ZLRU, WIDE), (C_ZC, WIDE))),
        *((rows_of(A["cmp_w1"][one, b]), 16, CMP_HID) for b in range(2)),
        (rows_of(A["conv_w_pw2"][one]), FT, WIDE),
        *((rows_of(A["w_out"][one, i * 512:i * 512 + 512, :]), 4, D) for i in (1, 2, 0))])

    bd = tl["bd"]
    for i, name in enumerate(("lru_w_a", "lru_w_i")):
        for par in range(2):
            bd_in = core.load("bd", bd[par * HD:par * HD + HD, i, :, par * HD:par * HD + HD],
                              A[name][one, par:HEADS:2].rearrange("o h i j -> i (o h) j"))
    slot, bank, free = core.banks.take()
    for c in range(FT):
        t = core.pe([rows_in, free], nc.tensor.transpose, bank[:, c * N_ROWS:(c + 1) * N_ROWS],
                    rows[:, c * P:c * P + P], ident[0:N_ROWS, 0:N_ROWS])
    t = core.pe([], nc.tensor.transpose, bank[:, 256:256 + KT], tl["grows"][:], ident[0:KT, 0:KT])
    core.dve([t], V.tensor_copy, vec[:], bank[:, 0:FT * N_ROWS].rearrange("p (c r) -> p c r", c=FT))
    vec_ready = core.dve([], V.tensor_copy, tl["gT"][:], bank[:, 256:256 + KT])
    core.banks.release(slot, vec_ready)

    xn_ready = normed(core, [], x, tl["xn"], tl["sq"][:], tl["small"])

    h_ready = scaled_transposed(core, [xn_ready, vec_ready], tl["xn"], hT, 0, tl["gT"], None, ident)

    lam = vec[:, :, ROW_LAM]
    sp8, sc = tl["sp8"], tl["sc"]
    s = core.stt([], sc[:, 0:4], lam, -1.0, lam, MUL, MAX)
    s = core.f([s], sc[:, 4:8], sc[:, 0:4], ACT.Exp, scale=-1.0)
    log1p_unit(core, [s], sc[:, 8:12], sc[:, 4:8], sc[:, 12:16], sc[:, 16:20], sc[:, 20:24])
    core.ts([], sc[:, 0:4], lam, -1.0, MUL, 0.0, MAX)
    core.tt([], sp8[:], sc[:, 0:4], sc[:, 8:12], ADD)
    half, neg = sc[:, 0:4], sc[:, 4:8]
    core.ts([], half, sp8[:], LRU_C / 2, MUL)
    sp_ready = core.ts([], neg, sp8[:], -LRU_C, MUL)

    def by_feature(use, pieces=0):
        view, landed = stream.next()
        for c in range(0, FT, 2):
            slot, bank, free = core.banks.take()
            for e in range(2):
                for k in range(KT):
                    t = core.matmul([landed, h_ready, free], bank[:, e * T:e * T + T],
                                    view[:, k, (c + e) * P:(c + e) * P + P], hT[:, k, :],
                                    start=k == 0, stop=k == KT - 1)
            core.banks.release(slot, use(c, bank[:, :].rearrange("p (e t) -> p e t", e=2), t))
            spare(pieces)
        stream.done(t)

    def by_token(n, use, pieces):
        view, landed = stream.next()
        for tt in range(NT):
            slot, bank, free = core.banks.take()
            for k in range(KT):
                t = core.matmul([landed, h_ready, free], bank[:, 0:n], hT[:, k, tt * P:tt * P + P],
                                view[:, k, :], start=k == 0, stop=k == KT - 1)
            core.banks.release(slot, use(tt, bank, t))
            spare(pieces)
        stream.done(t)

    fa, fb, fc, fd, conv, xc = tl["fa"], tl["fb"], tl["fc"], tl["fd"], tl["conv"], tl["xc"]
    ubuf, lbuf = tl["ubuf"], tl["lbuf"]

    later, tap_left = [], []

    def spare(pieces):
        for _ in range(min(pieces, len(later))):
            later.pop(0)()
        for _ in range(min(TAPS_AT_ONCE, len(tap_left))):
            tap(tap_left.pop(0))

    def taps(out, src, tiles, row_w, row_b, first, end):
        s = {c: core.dve.last for c in tiles}
        for j in range(first, end):
            for c in tiles:
                if j == 0:
                    s[c] = core.ts([], out[:, c, :], src[:, c, 0:T], vec[:, c, row_w:row_w + 1], MUL,
                                   vec[:, c, row_b:row_b + 1], ADD)
                else:
                    s[c] = core.stt([], out[:, c, :], src[:, c, j:j + T], vec[:, c, row_w + j:row_w + j + 1],
                                    out[:, c, :], MUL, ADD, behind=s[c])
        return core.dve.last

    def tap(j):
        slot, product, free = tap_ring.take()
        for c in range(FT // 2):
            row = ROW_DW + j
            if j == 0:
                s = core.f([free], product[:, c, :], ubuf[:, c, 0:T], ACT.Identity,
                           bias=vec[:, c, ROW_DWB:ROW_DWB + 1], scale=vec[:, c, row:row + 1])
            else:
                s = core.f([free], product[:, c, :], ubuf[:, c, j:j + T], ACT.Copy, scale=vec[:, c, row:row + 1])
        if j == 0:
            t = core.pool([s], nc.gpsimd.tensor_copy, conv[:, 0:2, :], product)
        else:
            t = core.pool([s], nc.gpsimd.tensor_tensor, conv[:, 0:2, :], conv[:, 0:2, :], product, ADD)
        tap_ring.release(slot, t)

    by_feature(lambda c, b, t: core.f([t], fb[:, c:c + 2, :], b, ACT.Sigmoid))
    sig_ready = core.act.last
    def use_a(c, b, t):
        s = core.tt([t, sig_ready], ubuf[:, c:c + 2, DW_TAPS - 1:], b, fb[:, c:c + 2, :], MUL)
        if c == 0:
            core.act.wait(s)
            tap_left.extend(range(DW_TAPS))
        return s

    by_feature(use_a)
    for first in range(0, DW_TAPS, 4):
        later.append(lambda first=first: taps(conv, ubuf, range(FT // 2, FT), ROW_DW, ROW_DWB, first,
                                              min(first + 4, DW_TAPS)))
    by_feature(lambda c, b, t: core.f([t], lbuf[:, c:c + 2, LRU_TAPS - 1:], b, ACT.Copy), 2)
    u_ready = core.act.last
    core.dve.wait(u_ready)
    xc_ready = taps(xc, lbuf, range(FT), ROW_LC, ROW_LCB, 0, LRU_TAPS)

    cos, sin, r1, r2, qr, kr, vr = (tl[n] for n in ("cos", "sin", "r1", "r2", "qr", "kr", "vr"))

    def rotate(tt, t, out, src, g, i):
        n = g * i * 32
        shape = [P, g, i, 32]
        c4 = wide(cos[:, tt, :].unsqueeze(1).unsqueeze(1), shape)
        s4 = wide(sin[:, tt, :].unsqueeze(1).unsqueeze(1), shape)
        v1 = r1[:, 0:n].rearrange("p (g i d) -> p g i d", g=g, i=i)
        v2 = r2[:, 0:n].rearrange("p (g i d) -> p g i d", g=g, i=i)
        a, b = src[:, :, :, 0:32], src[:, :, :, 32:64]
        core.tt([t], v1, a, c4, MUL)
        core.tt([], v2, b, s4, MUL)
        core.tt([], out[:, :, :, 0:32], v1, v2, SUB)
        core.tt([], v1, b, c4, MUL)
        core.tt([], v2, a, s4, MUL)
        return core.tt([], out[:, :, :, 32:64], v1, v2, ADD)

    def use_q(tt, bank, t):
        return rotate(tt, t, qr[:, tt, :].rearrange("p (i g d) -> p g i d", g=KV, d=HD),
                      bank[:, :].rearrange("p (g i d) -> p g i d", g=KV, d=HD), KV, REP)

    def use_k(tt, bank, t):
        s = []
        for i, (kc, b) in enumerate(((0, 0), (256, 1))):
            s.append(rotate(tt, t, kr[:, b, tt, :].rearrange("p (g i d) -> p g i d", g=KV, d=HD),
                            bank[:, kc:kc + P].rearrange("p (g i d) -> p g i d", g=KV, d=HD), KV, 1))
            s.append(core.dve([t], V.tensor_copy, vr[:, b, tt, :], bank[:, kc + P:kc + 2 * P]))
        return s

    gates = tl["gates"]

    def use_w(tt, bank, t):
        s1 = rotate(tt, t, kr[:, 2, tt, :].rearrange("p (g i d) -> p g i d", g=KV, d=HD),
                    bank[:, 0:P].rearrange("p (g i d) -> p g i d", g=KV, d=HD), KV, 1)
        s2 = core.dve([t], V.tensor_copy, vr[:, 2, tt, :], bank[:, P:2 * P])
        s1 = core.tt([t, misc_in], gates[:, tt, :], bank[:, 256:280], tl["b_gate"][:], ADD)
        return [s1, s2]

    by_token(WIDE, use_q, 0)
    slot, bank, free = core.banks.take()
    for b in range(2):
        t = core.pe([misc_in, free], nc.tensor.transpose, bank[:, b * 16:b * 16 + 16],
                    tl["pos_rows"][:, b, :], ident[0:16, 0:16])
    s = core.dve([t], V.tensor_copy, tl["posT"][:], bank[:, 0:32].rearrange("p (b j) -> p b j", b=2))
    core.banks.release(slot, s)
    for i, (dst, row) in enumerate(((fa, ROW_BA), (fc, ROW_BI))):
        for c in range(0, FT, 2):
            slot, bank, free = core.banks.take()
            for e in range(2):
                t = core.matmul([xc_ready, bd_in, free], bank[:, e * T:e * T + T], bd[:, i, c + e, :],
                                xc[:, c + e, :])
            for e in range(2):
                s = core.f([t], dst[:, c + e, :], bank[:, e * T:e * T + T], ACT.Sigmoid,
                           bias=vec[:, c + e, row:row + 1])
            core.banks.release(slot, s)

    for c in range(FT):
        core.f([sp_ready], fd[:, c, :], fa[:, c, :], ACT.Tanh, scale=half[:, c:c + 1])
    for c in range(FT):
        core.f([], fa[:, c, :], fa[:, c, :], ACT.Exp, scale=neg[:, c:c + 1])
    lru_in = core.f([], fd[:], fd[:], ACT.Sqrt)

    def lru_input():
        core.tt([lru_in], fc[:], fc[:], xc[:], MUL)
        core.stt([], fc[:], fa[:], 1.0, fc[:], ADD, MUL)
        core.tt([], fd[:], fd[:], fc[:], MUL)

    def lru_scan():
        for c in range(FT):
            core.dve([], V.tensor_tensor_scan, fc[:, c, :], fa[:, c, :], fd[:, c, :], 0.0, MUL, ADD)

    later[:0] = [lru_input, lru_scan]

    by_token(WIDE, use_k, 1)
    by_token(C_ZN - C_KVW, use_w, 1)
    s = core.f([core.dve.last], gates[:], gates[:], ACT.Sigmoid)
    qkv_ready = [s, core.dve.last]
    zn = tl["zn"]

    def use_z(tt, bank, t):
        s = core.f([t], zn[:, tt, :], bank[:, :], ACT.Sigmoid)
        return core.tt([s], zn[:, tt, :], zn[:, tt, :], bank[:, :], MUL)

    by_token(WIDE, use_z, 2)

    qT, kT, cT, pair = tl["qT"], tl["kT"], tl["cT"], tl["pair"]
    for c in range(0, FT, 2):
        slot, bank, free = core.banks.take()
        for e in range(2):
            for tt in range(NT):
                t = core.pe([qkv_ready, free], nc.tensor.transpose,
                            bank[:, e * T + tt * P:e * T + tt * P + P],
                            qr[:, tt, (c + e) * P:(c + e) * P + P], ident)
        s = core.act([t], nc.scalar.copy, qT[:, c:c + 2, :], bank[:, :].rearrange("p (e t) -> p e t", e=2))
        core.banks.release(slot, s)
    q_ready = [core.dve.last, core.act.last]
    for dst, srcs in ((kT, (kr[:, 1], kr[:, 2])), (cT, (kr[:, 0], vr[:, 0]))):
        slot, bank, free = core.banks.take()
        for e, src in enumerate(srcs):
            for tt in range(NT):
                t = core.pe([free], nc.tensor.transpose, bank[:, e * T + tt * P:e * T + tt * P + P],
                            src[:, tt, :], ident)
        s = core.act([t], nc.scalar.copy, dst[:], bank[:, :].rearrange("p (e t) -> p e t", e=2))
        core.banks.release(slot, s)
    k_ready = [core.dve.last, core.act.last]
    for g in range(KV):
        src = cT[g * HD:g * HD + HD, :, :]
        core.load("pair", pair[0:HD, :, g, :], src, [k_ready])
        pair_in = core.load("pair", pair[HD:P, :, g, 0:T - 1], src[:, :, 1:T])

    def gate_lru(c, b, t):
        s = core.f([t], fb[:, c:c + 2, :], b, ACT.Sigmoid)
        core.tt([s], fb[:, c:c + 2, :], fb[:, c:c + 2, :], b, MUL)
        return core.tt([], mixT[:, 4 + c:6 + c, :], fb[:, c:c + 2, :], fc[:, c:c + 2, :], MUL)

    by_feature(gate_lru, 3)
    blk, posT, hidT, w2 = tl["blk"], tl["posT"], tl["hidT"], tl["w2"]
    for b in range(2):
        for g in range(KV):
            ap = pair[:, b, g, :]
            src = bass.AP(ap.tensor, ap.offset, [ap.ap[0], [2, 8], [S_CMP, NCMP]])
            src2 = bass.AP(ap.tensor, ap.offset + 16, [ap.ap[0], [2, 8], [S_CMP, NCMP]])
            for half, sr in ((0, src), (1, src2)):
                dst = blk[:, b, half * 8:half * 8 + 8, g * CMP_PAD:g * CMP_PAD + NCMP]
                blk_ready = core.tt([pair_in, misc_in], dst, sr,
                            wide(posT[:, b, half * 8:half * 8 + 8].unsqueeze(2), [P, 8, NCMP]), ADD)

    def compress(b):
        view, landed = stream.next()
        slot, bank, free = core.banks.take()
        for m in range(2):
            for k in range(16):
                t = core.matmul([blk_ready, landed, free], bank[:, m * 32:m * 32 + 32],
                                view[:, k, m * P:m * P + P], blk[:, b, k, :], start=k == 0, stop=k == 15)
        stream.done(t)
        for m in range(2):
            s = core.f([t], tl["sig32"][:], bank[:, m * 32:m * 32 + 32], ACT.Sigmoid)
            s = core.tt([s], hidT[:, b, m, :], bank[:, m * 32:m * 32 + 32], tl["sig32"][:], MUL)
            core.act.wait(s)
        core.banks.release(slot, s)
        return s

    assert not later and not tap_left
    ones = K["ones"]
    mean, var = fa[:, 0, :], fa[:, 1, :]
    zc = tl["xc"]

    def gate_conv(c, b, t):
        s = core.f([t, core.dve.last], zc[:, c:c + 2, :], b, ACT.Sigmoid)
        s = core.tt([s], zc[:, c:c + 2, :], zc[:, c:c + 2, :], b, MUL)
        if c == 0:
            squares_ready.append(centred())
        else:
            layer_norm_end(squares_ready[0])
        return s

    squares_ready = []

    def centred():
        slot, bank, free = core.banks.take()
        for c in range(FT):
            t = core.matmul([core.dve.last, core.pool.last, free], bank[:, 0:T], ones, conv[:, c, :], start=c == 0, stop=c == FT - 1)
        core.ts([t], mean, bank[:, 0:T], 1.0 / WIDE, MUL)
        core.banks.release(slot, core.dve.last)
        s = core.tt([], conv[:], conv[:], wide(mean.unsqueeze(1), [P, FT, T]), SUB)
        s = core.f([s], fd[:], conv[:], ACT.Square)
        return s

    def layer_norm_end(squares_ready):
        slot, bank, free = core.banks.take()
        for c in range(FT):
            t = core.matmul([squares_ready, free], bank[:, 0:T], ones, fd[:, c, :], start=c == 0, stop=c == FT - 1)
        s = inv_rms(core, [t], var, bank[:, 0:T], WIDE, fa[:, 2, :])
        core.banks.release(slot, s)
        core.tt([s], conv[:], conv[:], wide(var.unsqueeze(1), [P, FT, T]), MUL)
        for c in range(FT):
            s = core.ts([], conv[:, c, :], conv[:, c, :], vec[:, c, ROW_LNG:ROW_LNG + 1], MUL,
                        vec[:, c, ROW_LNB:ROW_LNB + 1], ADD)
        s = core.f([s], fd[:], conv[:], ACT.Sigmoid)
        act_ready = core.tt([s], fd[:], fd[:], conv[:], MUL)

    by_feature(gate_conv)
    act_ready = core.dve.last
    compress(0)
    s = compress(1)
    pw2, pw_in = stream.next()
    for c in range(0, FT, 2):
        slot, bank, free = core.banks.take()
        for e in range(2):
            for k in range(FT):
                t = core.matmul([act_ready, pw_in, free], bank[:, e * T:e * T + T],
                                pw2[:, k, (c + e) * P:(c + e) * P + P], fd[:, k, :],
                                start=k == 0, stop=k == FT - 1)
        s = core.tt([t], mixT[:, 8 + c:10 + c, :], bank[:, :].rearrange("p (e t) -> p e t", e=2),
                    zc[:, c:c + 2, :], MUL)
        core.banks.release(slot, s)
    stream.done(t)

    slot, bank, free = core.banks.take()
    for g in range(KV):
        for m in range(2):
            t = core.matmul([s, free], bank[g * HD:g * HD + HD, 0:CMP_PAD], w2[:, 0, m, :],
                            hidT[:, 0, m, g * CMP_PAD:g * CMP_PAD + CMP_PAD], start=m == 0, stop=m == 1)
    s = core.dve([t], V.tensor_copy, tl["kcT"][:], bank[:, 0:CMP_PAD])
    core.banks.release(slot, s)
    rep = tl["hid_rep"]
    for m in range(2):
        for g in range(KV):
            s = core.dve([], V.tensor_copy, rep[:, m, g * REP:g * REP + REP, :],
                         wide(hidT[:, 1, m, g * CMP_PAD:g * CMP_PAD + CMP_PAD].unsqueeze(1), [P, REP, CMP_PAD]))
    slot, bank, free = core.banks.take()
    for m in range(2):
        t = core.matmul([s, free], bank[:, 0:HD], rep[:, m, :, :].rearrange("p h n -> p (h n)"),
                        w2[:, 1, m, :], start=m == 0, stop=m == 1)
    cmp_ready = core.tt([t], tl["vcb"][:], wide(bank[:, 0:HD].unsqueeze(1), [P, HEADS, HD]),
                        wide(K["blocks"].unsqueeze(2), [P, HEADS, HD]), MUL)
    core.banks.release(slot, cmp_ready)

    S, mx, PT, sums, coef = tl["S"], tl["mx"], tl["PT"], tl["sums"], tl["coef"]
    O = core.held
    pc, mc, y, yt = tl["pc"], tl["mc"], tl["y"], tl["yt"]
    free_of = {"y": None, "O": None, "S0": None, "S1": None, "PT0": None, "PT1": None, "PT2": None}

    def compressed_scores(qt, unit):
        at = slice(qt * CMP_PAD, qt * CMP_PAD + CMP_PAD)
        for g in range(KV):
            slot, bank, free = core.banks.take()
            for i in range(REP):
                t = core.matmul([q_ready, cmp_ready, free], bank[:, i * CMP_PAD:(i + 1) * CMP_PAD],
                                qT[g * HD:g * HD + HD, i, qt * P:qt * P + P], tl["kcT"][g * HD:g * HD + HD, :])
            s = core.stt([t], pc[:, g * REP:g * REP + REP, :],
                         bank[:, 0:REP * CMP_PAD].rearrange("p (h n) -> p h n", h=REP), HD ** -0.5,
                         wide(K["cmp_neg"][:, at].unsqueeze(1), [P, REP, CMP_PAD]), MUL, ADD)
            core.banks.release(slot, s)
        core.dve([], V.tensor_reduce, mc[:], pc[:], AX.X, MAX)
        s = core.tt([], pc[:], pc[:], wide(mc[:].unsqueeze(2), [P, HEADS, CMP_PAD]), SUB)
        s = core.f([s], pc[:], pc[:], ACT.Exp)
        core.dve([s], V.tensor_reduce, sums[:, qt, 0, :], pc[:], AX.X, ADD)
        return core.tt([], pc[:], pc[:], wide(K["cmp_one"][:, at].unsqueeze(1), [P, HEADS, CMP_PAD]), MUL)

    def compressed_turned(qt, unit, ready):
        slot, bank, free = core.banks.take()
        t = core.pe([ready, free], nc.tensor.transpose, bank[:, 0:P], pc[:].rearrange("p h n -> p (h n)"), ident)
        s = core.dve([t, free_of[f"PT{unit % 3}"]], V.tensor_copy, PT[:, unit % 3, 0:P], bank[:, 0:P])
        core.banks.release(slot, s)
        return s

    def compressed_values(qt, unit, ready):
        t = core.matmul([ready, free_of["O"]], O[0][:, :], PT[:, unit % 3, 0:P], tl["vcb"][:].rearrange("p h d -> p (h d)"))
        free_of[f"PT{unit % 3}"] = t
        return t

    def head_scores(qt, unit, i, g):
        nk, b0 = (qt + 1) * P, 2 * (unit % 2)
        mask = K["mask2"][:, (NT - 1 - qt) * P:NT * P]
        slot, bank, free = core.banks.take()
        for b in range(2):
            t = core.matmul([k_ready, free], bank[:, b * T:b * T + nk],
                            qT[g * HD:g * HD + HD, i, qt * P:qt * P + P], kT[g * HD:g * HD + HD, b, 0:nk])
        for b in range(2):
            s = core.dve([t, free_of[f"S{unit % 2}"]], V.tensor_tensor_reduce, S[:, b0 + b, 0:nk], bank[:, b * T:b * T + nk],
                         mask, -(HD ** -0.5), 3e38, ADD, MIN, mx[:, b0 + b:b0 + b + 1])
        core.banks.release(slot, s)
        for b in range(2):
            s = core.f([s], S[:, b0 + b, 0:nk], S[:, b0 + b, 0:nk], ACT.Exp, bias=mx[:, b0 + b:b0 + b + 1], scale=-1.0,
                       accum_out=sums[:, qt, 1 + b, g * REP + i:g * REP + i + 1])
        return s

    def head_turned(qt, unit, i, g, ready):
        slot, bank, free = core.banks.take()
        for b in range(2):
            for kt in range(qt + 1):
                at = (b * (qt + 1) + kt) * P
                t = core.pe([ready, free], nc.tensor.transpose, bank[:, at:at + P],
                            S[:, 2 * (unit % 2) + b, kt * P:kt * P + P], ident)
        free_of[f"S{unit % 2}"] = t
        n = 2 * (qt + 1) * P
        s = core.copy([t, free_of[f"PT{unit % 3}"]], PT[:, unit % 3, 0:n], bank[:, 0:n])
        core.banks.release(slot, s)
        return s

    def head_values(qt, unit, i, g, ready):
        h = g * REP + i
        for b in range(2):
            for kt in range(qt + 1):
                at = (b * (qt + 1) + kt) * P
                t = core.matmul([ready, free_of["O"]], O[1 + b][:, h * HD:h * HD + HD], PT[:, unit % 3, at:at + P],
                                vr[:, 1 + b, kt, g * HD:g * HD + HD], start=kt == 0, stop=kt == qt)
        free_of[f"PT{unit % 3}"] = t
        return t

    def gated(qt, t):
        core.dve([core.act.last], V.reciprocal, coef[:], sums[:, qt])
        core.tt([], coef[:], coef[:], gates[:, qt, :].rearrange("p (h b) -> p b h", b=BRANCHES), MUL)
        for b in range(BRANCHES):
            dst = y if b == 0 else yt
            core.tt([t, free_of["y"]], dst[:, :].rearrange("p (h d) -> p h d", h=HEADS), O[b][:, :].rearrange("p (h d) -> p h d", h=HEADS),
                    wide(coef[:, b, :].unsqueeze(2), [P, HEADS, HD]), MUL)
            if b:
                core.tt([], y[:], y[:], yt[:], ADD)
        free_of["O"] = core.dve.last
        return core.tt([], y[:], y[:], zn[:, qt, :], MUL)

    def mixed(qt, ready):
        slot, bank, free = core.banks.take()
        for c in range(FT):
            t = core.pe([ready, free], nc.tensor.transpose, bank[:, c * P:c * P + P], y[:, c * P:c * P + P], ident)
        free_of["y"] = t
        s = core.dve([t], V.tensor_copy, mixT[:, 0:FT, qt * P:qt * P + P], bank[:, :].rearrange("p (c t) -> p c t", c=FT))
        core.banks.release(slot, s)
        return s

    units = []
    for qt in range(NT):
        units += [(head_scores, head_turned, head_values, qt, i, g) for i in range(REP) for g in range(KV)]
        units.insert(len(units) - 2 * REP + 2, (compressed_scores, compressed_turned, compressed_values, qt))
    per_tile = len(units) // NT
    scored, copied = {}, {}
    for step in range(len(units) + 2):
        if step < len(units):
            first, _, _, qt, *head = units[step]
            scored[step] = first(qt, step, *head)
        if 1 <= step <= len(units):
            _, second, _, qt, *head = units[step - 1]
            copied[step - 1] = second(qt, step - 1, *head, scored[step - 1])
        if step >= 2:
            _, _, third, qt, *head = units[step - 2]
            t = third(qt, step - 2, *head, copied[step - 2])
        if step == per_tile + 1:
            y_ready = gated(0, t)
        if step == per_tile + 3:
            mixed(0, y_ready)
    y_ready = gated(1, t)
    taken = [core.banks.take() for _ in range(3)]
    sums_out = [bank for _, bank, _ in taken] + [core.held[3]]
    free = [token for _, _, token in taken]
    s = cmp_ready
    for i in (1, 2, 0):
        if i == 0:
            s = mixed(1, y_ready)
        view, landed = stream.next()
        for k in range(4):
            for tt in range(NT):
                for n in range(2):
                    t = core.matmul([s, landed, *free], sums_out[2 * tt + n][:, :], mixT[:, 4 * i + k, tt * P:tt * P + P],
                                    view[:, k, n * 512:n * 512 + 512], start=i == 1 and k == 0, stop=i == 0 and k == 3, mark=k == 3)
        stream.done(t)
    for tt in range(NT):
        for n in range(2):
            s = core.tt([t], x[:, tt, n * 512:n * 512 + 512], sums_out[2 * tt + n][:, :], x[:, tt, n * 512:n * 512 + 512], ADD)
    return s


def group_steps(core, w_stream, tokens, n_out, width, lhs, rhs, use, k_tiles):
    def step(o):
        view, landed = w_stream.next()
        slot, bank, free = core.banks.take()
        for k in range(k_tiles):
            a = lhs(view, o, k)
            t = core.matmul([landed, free, *tokens], bank[0:a.shape[-1], 0:width], a, rhs(view, o, k),
                            start=k == 0, stop=k == k_tiles - 1)
        core.banks.release(slot, use(o, bank, t))
        if o == n_out - 1:
            w_stream.done(t)

    return [lambda o=o: step(o) for o in range(n_out)]


def matmul_groups(*args):
    for step in group_steps(*args):
        step()


def turned(core, tokens, srcs, ident, rows=P):
    slot, bank, free = core.banks.take()
    for i, src in enumerate(srcs):
        n = src.shape[-1]
        t = core.pe([*tokens, free], core.nc.tensor.transpose, bank[0:n, i * P:i * P + rows], src,
                    ident[0:rows, 0:rows])
    return slot, bank, t


def second_block(core, A, K, x, out):
    nc = core.nc
    V = nc.vector
    ident = K["ident"]
    with ExitStack() as outer:
        def keep(name, shape, dt=F32):
            return sb(core, outer, "second_" + name, shape, dt)

        gt2, h2 = keep("gt2", [P, D]), keep("h2", [P, NT, D])
        hT = keep("hT", [P, KT, 2 * T])
        with ExitStack() as stack:
            mixers(core, A, K, x, gt2, h2, hT, stack)
            core.restart()
        with ExitStack() as stack:
            experts(core, A, K, x, gt2, h2, hT, out, stack)


def mixers(core, A, K, x, gt2, h2, hT, stack):
    nc = core.nc
    V = nc.vector
    ident = K["ident"]

    def tile(name, shape, dt=F32):
        return sb(core, stack, "m_" + name, shape, dt)

    def rows_of(ap):
        return ap.rearrange("o (k p) n -> p (o k) n", p=P)

    R_C, R_CC, R_G1, R_G2, R_ADA, R_GCQ, R_GKV, R_GML, R_END = 0, 8, 16, 24, 32, 80, 82, 83, 87
    rows = tile("rows", [R_END, P])
    for r, name, k in ((R_C, "c_2", 8), (R_G1, "g_norm1_2", 8), (R_G2, "g_norm2_2", 8),
                       (R_ADA, "b_ada_2", 48), (R_GCQ, "g_cq_2", 2), (R_GKV, "g_ckv_2", 1),
                       (R_GML, "g_mlstm_2", 4)):
        core.load("m_rows", rows[r:r + k, :], A[name].rearrange("o (k p) -> (o k) p", p=P))
    core.load("m_rows", rows[R_CC:R_G1, :], A["c_ctx_2"].rearrange("(k p) -> k p", p=P))
    conv_rows = tile("conv_rows", [3, 512])
    rows_in = core.load("m_rows", conv_rows, A["conv_qk_2"].rearrange("o k c -> (o k) c"))
    gt1, fin_g = tile("gt1", [P, D]), tile("fin_g", [P, D])
    fin_in = core.load("fin_g", fin_g, A["final_g"].rearrange("(o n) -> o n", o=1).to_broadcast([P, D]))
    ring = core.ring([tile(f"w{i}", [P, 4096]) for i in range(3)])
    ada = lambda c: (rows_of(A["w_ada_2"][:, :, c * 512:c * 512 + 512]), KT, 512)
    w_in = lambda a, b: (rows_of(A["w_in_2"][:, :, a:b]), KT, b - a)
    stream = WeightStream(core, ring, [
        *(ada(c) for c in (0, 1, 2, 3)), w_in(0, B_QK), w_in(B_QK, B_V), w_in(B_G, B_G + 16),
        (rows_of(A["w_uq_2"]), 2, MLA_H * QK), (rows_of(A["w_ukv_2"]), 1, MLA_H * (NOPE + MLA_V)),
        w_in(B_V, B_O), w_in(B_O, B_G), *(ada(c) for c in range(4, 12)),
        *((rows_of(A["w_out_2"][:, i * 512:i * 512 + 512, :]), 4, D) for i in range(2))])
    ctx = tile("ctx", [P, NT, D])
    ctx_in = core.load("ctx", ctx, A["ctx_2"].rearrange("b (t p) d -> p (b t) d", p=P))
    b_if = tile("b_if", [P, 16])
    g_q, g_k = tile("g_q", [P, QK]), tile("g_k", [P, QK])
    core.load("m_small", b_if[:, 0:8], A["b_igate_2"].rearrange("o a b -> o (a b)").to_broadcast([P, 8]))
    core.load("m_small", b_if[:, 8:16], A["b_fgate_2"].rearrange("o a b -> o (a b)").to_broadcast([P, 8]))
    core.load("m_small", g_q, A["g_qn_2"].to_broadcast([P, QK]))
    core.load("m_small", g_k, A["g_kn_2"].to_broadcast([P, QK]))
    for dst, col in ((gt1, 2 * D), (gt2, 5 * D)):
        small_in = core.load("m_small", dst, A["b_ada_2"][:, col:col + D].to_broadcast([P, D]))

    vec = tile("vec", [P, R_END])
    convw = tile("convw", [P, 4, 3])
    slot, bank, t = turned(core, [rows_in], [rows], ident, R_END)
    core.banks.release(slot, core.dve([t], V.tensor_copy, vec, bank[:, 0:R_END]))
    slot, bank, t = turned(core, [rows_in], [conv_rows[:, c * P:c * P + P] for c in range(4)], ident, 3)
    vec_ready = core.dve([t], V.tensor_copy, convw, bank[:, :].rearrange("p (c r) -> p c r", c=4)[:, :, 0:3])
    core.banks.release(slot, vec_ready)

    small, sq = tile("small", [P, 64]), tile("sq", [P, D])
    for tt in range(NT):
        s = core.f([], sq, x[:, tt, :], ACT.Square, accum_out=small[:, tt:tt + 1])
    s = inv_rms(core, [s], small[:, 4:6], small[:, 0:2], D, small[:, 2:4])
    for tt in range(NT):
        x_ready = core.stt([s, fin_in], x[:, tt, :], x[:, tt, :], small[:, 4 + tt:5 + tt], fin_g, MUL, MUL)

    sT, cond = tile("sT", [P, KT, 2]), vec[:, 0:16].rearrange("p (a k) -> p k a", a=2)
    s = core.f([vec_ready], sT, cond, ACT.Sigmoid)
    core.tt([s], sT, sT, cond, MUL)
    s_ready = core.dve.last
    sums = core.ring([tile(f"sum{i}", [P, 512]) for i in range(2)])

    mod, mod_rows, rows_free = tile("mod", [P, 48, 2]), tile("mod_rows", [2, 512]), None

    def modulation(c):
        def use(o, bank, t):
            nonlocal rows_free
            s = core.act([t, rows_free], nc.scalar.copy, mod_rows, bank[0:2, :])
            slot, turn, free = core.banks.take()
            for n in range(4):
                t = core.pe([s, free], nc.tensor.transpose, turn[:, 2 * n:2 * n + 2], mod_rows[:, n * P:n * P + P],
                            ident[0:2, 0:2])
            rows_free = t
            core.banks.release(slot, core.tt([t], mod[:, 4 * c:4 * c + 4, :], turn[:, 0:8].rearrange("p (n a) -> p n a", a=2),
                                             wide(vec[:, R_ADA + 4 * c:R_ADA + 4 * c + 4].unsqueeze(2), [P, 4, 2]), ADD))
            return s

        matmul_groups(core, stream, [s_ready], 1, 512, lambda v, o, k: sT[:, k, :], lambda v, o, k: v[:, k, :],
                      use, KT)
        return core.dve.last

    def weighted(o=None):
        view, landed = stream.next()
        slot, total, free = sums.take()
        add = lambda out, a, b: core.pool([], nc.gpsimd.tensor_tensor, out, a, b, ADD)
        core.pool([landed, s_ready], nc.gpsimd.tensor_tensor, view, view, wide(sT[:, :, 0:1], [P, KT, 512]), MUL)
        add(view[:, 0:4, :], view[:, 0:4, :], view[:, 4:8, :])
        add(view[:, 0:2, :], view[:, 0:2, :], view[:, 2:4, :])
        core.pool.wait(free)
        t = add(total, view[:, 0, :], view[:, 1, :])
        stream.done(t)
        totals.append((slot, total, t))

    totals = []

    def gate_row(dst, half):
        slot, total, ready = totals.pop(0)
        cols = slice(half * 512, half * 512 + 512)
        at, bank, free = core.banks.take()
        t = core.matmul([ready, free], bank[:, :], K["ones"], total)
        sums.release(slot, t)
        core.banks.release(at, core.tt([t, small_in], dst[:, cols], bank[:, :], dst[:, cols], ADD))

    def late_modulation(c):
        slot, total, ready = totals.pop(0)
        at, bank, free = core.banks.take()
        for n in range(4):
            t = core.matmul([ready, free], bank[:, n:n + 1], total[:, n * P:n * P + P], K["ones"][:, 0:1])
        sums.release(slot, t)
        core.banks.release(at, core.tt([t], mod[:, 4 * c:4 * c + 4, 0], bank[:, 0:4],
                                       vec[:, R_ADA + 4 * c:R_ADA + 4 * c + 4], ADD))

    late = [*(lambda h=h: gate_row(gt1, h) for h in range(2)), *(lambda c=c: late_modulation(c) for c in (6, 7, 8, 9)),
            *(lambda h=h: gate_row(gt2, h) for h in range(2))]

    def next_late():
        late.pop(0)()

    modulation(0)
    modulation(1)
    xn = h2
    normed(core, [ctx_in, core.dve.last], ctx, ctx, sq, small)
    core.act.wait(core.dve.last)
    normed(core, [x_ready], x, xn, sq, small)
    modulation(2)
    modulation(3)
    scale1, scale2 = tile("scale1", [P, 2, KT]), tile("scale2", [P, KT])
    for a in range(2):
        core.ts([], scale1[:, a, :], mod[:, 8:16, a], 1.0, ADD)
        s = core.tt([], scale1[:, a, :], scale1[:, a, :], vec[:, R_G1:R_G1 + 8], MUL)

    scaled_transposed(core, [s], ctx, hT, 0, scale1[:, 1, :], mod[:, 0:8, 1], ident)
    h_ready = scaled_transposed(core, [s], xn, hT, T, scale1[:, 0, :], mod[:, 0:8, 0], ident)
    TILES = 2 * NT

    cq, ckv = tile("cq", [P, NT, Q_RANK]), tile("ckv", [P, TILES, KV_RANK + ROPE2])
    v_ext = tile("v_ext", [P, TILES, ML_H, ML_V + 1])
    o_gate = tile("o_gate", [P, NT, ML_H * ML_V])
    gates = tile("gates", [P, TILES, 16])
    core.dve([], V.memset, v_ext[:, :, :, ML_V:ML_V + 1], 1.0)

    def token(tile_at):
        return lambda v, o, k: hT[:, k, (tile_at + o) * P:(tile_at + o) * P + P]

    def use_mla(o, bank, t):
        if o >= NT:
            core.dve([t], V.tensor_copy, cq[:, o - NT, :], bank[:, 0:Q_RANK])
        return core.dve([t], V.tensor_copy, ckv[:, o, :], bank[:, Q_RANK:B_QK])

    matmul_groups(core, stream, [h_ready], TILES, B_QK, token(0), lambda v, o, k: v[:, k, :], use_mla, KT)

    mixT = tile("mixT", [P, KT, T])
    whole, mla = tile, ExitStack()
    ml_tiles = {n: tile("ml_" + n, shape) for n, shape in (
        ("tmp", [P, 6, TILES, 8]), ("gcol", [P, 2, TILES, ML_H]), ("ecol", [P, NT, ML_H, 2]))}

    def tile(name, shape, dt=F32):
        return sb(core, mla, "mla_" + name, shape, dt)

    qnT, qrT = tile("qnT", [P, MLA_H, T]), tile("qrT", [ROPE2, MLA_H, T])
    knT, krT = tile("knT", [P, MLA_H, 2 * T]), tile("krT", [ROPE2, MLA_H, 2 * T])
    vm = tile("vm", [P, TILES, MLA_H, MLA_V])
    cqT, ckvT = tile("cqT", [P, 2, T]), tile("ckvT", [P, 2 * T])
    heads, sq4 = tile("heads", [P, MLA_H, QK]), tile("sq4", [P, MLA_H, QK])
    r1, r2 = tile("r1", [P, MLA_H, 2, 16]), tile("r2", [P, MLA_H, 2, 16])

    def rank_norm(src, n_tiles, width, at):
        sums, root, inv = (small[:, at + i * 4:at + i * 4 + n_tiles] for i in range(3))
        for i in range(n_tiles):
            s = core.f([core.dve.last], sq[:, 0:width], src[:, i, 0:width], ACT.Square, accum_out=sums[:, i:i + 1])
        s = inv_rms(core, [s], inv, sums, width, root)
        for i in range(n_tiles):
            s = core.ts([s], src[:, i, 0:width], src[:, i, 0:width], inv[:, i:i + 1], MUL)
        return s

    def rank_turned(ready, src, n_tiles, width, dst_of, g_row):
        for i in range(n_tiles):
            slot, bank, t = turned(core, [ready], [src[:, i, k * P:k * P + P] for k in range(width // P)], ident)
            for k in range(width // P):
                s = core.ts([t], dst_of(k, i), bank[:, k * P:k * P + P], vec[:, g_row + k:g_row + k + 1], MUL)
            core.banks.release(slot, s)
        return s

    rank_norm(cq, NT, Q_RANK, 0)
    ranks_ready = rank_norm(ckv, TILES, KV_RANK, 12)

    qk_lat, k_ctx = tile("qk_lat", [P, 4, T + 2]), tile("k_ctx", [P, 2, T + 2])
    core.dve([], V.memset, qk_lat, 0.0)
    pads = core.dve([], V.memset, k_ctx, 0.0)

    def use_qk(o, bank, t):
        if o < 4:
            return core.dve([t], V.tensor_copy, qk_lat[:, o, 1:T + 1], bank[:, 0:T])
        return core.dve([t], V.tensor_copy, k_ctx[:, o - 4, 1:T + 1], bank[:, 0:T])

    matmul_groups(core, stream, [h_ready], 6, T,
                  lambda v, o, k: v[:, k, (o if o < 4 else o - 2) * P:(o if o < 4 else o - 2) * P + P],
                  lambda v, o, k: hT[:, k, T:2 * T] if o < 4 else hT[:, k, 0:T], use_qk, KT)
    matmul_groups(core, stream, [h_ready], TILES, 16, token(0), lambda v, o, k: v[:, k, :],
                  lambda o, bank, t: core.tt([t, small_in], gates[:, o, :], bank[:, 0:16], b_if, ADD), KT)

    rank_turned(ranks_ready, cq, NT, Q_RANK, lambda k, i: cqT[:, k, i * P:i * P + P], R_GCQ)
    cq_ready = rank_turned(ranks_ready, ckv, TILES, KV_RANK, lambda k, i: ckvT[:, i * P:i * P + P], R_GKV)

    def head_norm(ready, heads, g, rope_tile):
        for h in range(MLA_H):
            s = core.f([ready], sq4[:, h, :], heads[:, h, :], ACT.Square, accum_out=small[:, 24 + h:25 + h])
        s = inv_rms(core, [s], small[:, 32:36], small[:, 24:28], QK, small[:, 28:32])
        core.tt([s, small_in], heads, heads, wide(small[:, 32:36].unsqueeze(2), [P, MLA_H, QK]), MUL)
        core.tt([], heads, heads, wide(g.unsqueeze(1), [P, MLA_H, QK]), MUL)
        if rope_tile is not None:
            r = heads[:, :, NOPE:QK].rearrange("p h (a e d) -> p h a e d", a=2, e=2)
            a, b = r[:, :, :, 0, :], r[:, :, :, 1, :]
            shape = [P, MLA_H, 2, 16]
            c, n = (wide(K[name][:, rope_tile * 32:rope_tile * 32 + 32].rearrange("p (a d) -> p a d", a=2)
                         .unsqueeze(1), shape) for name in ("cos2", "sin2"))
            core.tt([], r1, a, n, MUL)
            core.tt([], r2, b, n, MUL)
            core.tt([], a, a, c, MUL)
            core.tt([], a, a, r2, SUB)
            core.tt([], b, b, c, MUL)
            core.tt([], b, b, r1, ADD)
        return core.dve.last

    def heads_turned(ready, heads, dstn, dstr, col):
        slot, bank, t = turned(core, [ready], [heads[:, h, 0:NOPE] for h in range(MLA_H)], ident)
        s = core.copy([t], dstn[:, :, col:col + P], bank[:, :].rearrange("p (h t) -> p h t", h=MLA_H))
        core.banks.release(slot, s)
        slot, bank, t = turned(core, [], [heads[:, h, NOPE:QK] for h in range(MLA_H)], ident)
        s = core.copy([t], dstr[:, :, col:col + P], bank[0:ROPE2, :].rearrange("p (h t) -> p h t", h=MLA_H))
        core.banks.release(slot, s)
        return t

    w_uq, w_ukv = stream.hold(), stream.hold()
    fill = [
        *group_steps(core, stream, [h_ready], TILES, 512, token(0), lambda v, o, k: v[:, k, :],
                     lambda o, bank, t: core.f([t], v_ext[:, o, :, 0:ML_V],
                                               bank[:, :].rearrange("p (h d) -> p h d", h=ML_H), ACT.Copy), KT),
        *group_steps(core, stream, [h_ready], NT, 512, token(NT), lambda v, o, k: v[:, k, :],
                     lambda o, bank, t: core.f([t], o_gate[:, o, :], bank[:, :], ACT.Sigmoid), KT),
        weighted, weighted]
    def queries(i, heads, free_heads):
        _, view, landed = w_uq
        for half in range(2):
            slot, bank, free = core.banks.take()
            for k in range(2):
                t = core.matmul([landed, cq_ready, free], bank[:, 0:2 * QK], cqT[:, k, i * P:i * P + P],
                                view[:, k, half * 2 * QK:half * 2 * QK + 2 * QK], start=k == 0, stop=k == 1)
            s = core.act([t, free_heads], nc.scalar.copy, heads[:, 2 * half:2 * half + 2, :],
                         bank[:, 0:2 * QK].rearrange("p (h d) -> p h d", h=2))
            core.banks.release(slot, s)
        if i == NT - 1:
            stream.drop(w_uq, t)
        return s

    def keys_values(i, heads, free_heads):
        _, view, landed = w_ukv
        for half in range(2):
            slot, bank, free = core.banks.take()
            t = core.matmul([landed, cq_ready, free], bank[:, :], ckvT[:, i * P:i * P + P],
                            view[:, 0, half * 512:half * 512 + 512])
            b4 = bank[:, :].rearrange("p (h e d) -> p h e d", h=2, e=2)
            core.act([t, free_heads], nc.scalar.copy, heads[:, 2 * half:2 * half + 2, 0:NOPE], b4[:, :, 0, :])
            s = core.act([], nc.scalar.copy, vm[:, i, 2 * half:2 * half + 2, :], b4[:, :, 1, :])
            core.banks.release(slot, s)
        if i == TILES - 1:
            stream.drop(w_ukv, t)
        return core.act([core.dve.last], nc.scalar.copy, heads[:, :, NOPE:QK],
                        wide(ckv[:, i, KV_RANK:KV_RANK + ROPE2].unsqueeze(1), [P, MLA_H, ROPE2]))

    both = [heads, ctx[:, 0, 0:MLA_H * QK].rearrange("p (h d) -> p h d", h=MLA_H)]
    work = [(queries, g_q, i, qnT, qrT, i) for i in range(NT)] + [
        (keys_values, g_k, i - NT if i >= NT else None, knT, krT, i) for i in range(TILES)]
    heads_free, normed_at = [None, None], None
    for n in range(len(work) + 1):
        if n < len(work):
            product, g, rope_tile, _, _, i = work[n]
            ready = product(i, both[n % 2], heads_free[n % 2])
        if n:
            _, _, _, dstn, dstr, i = work[n - 1]
            heads_free[(n - 1) % 2] = heads_turned(normed_at, both[(n - 1) % 2], dstn, dstr, i * P)
        if n < len(work):
            normed_at = head_norm(ready, both[n % 2], g, rope_tile)
            fill.pop(0)()
            if n < 2:
                fill.pop(0)()
    k_ready = [core.dve.last, core.act.last]

    p_sb, PT = (ctx[:, i, :].rearrange("p (b c) -> p b c", b=2) for i in range(2))
    att, den = tile("att", [P, NT, 512]), tile("den", [P, NT, MLA_H])
    scale = QK ** -0.5
    prepare, ml = mlstm_prepare(core, K, ml_tiles, convw, qk_lat, k_ctx, pads, gates, h2, hT, sq, ident)
    core.dve.wait(core.pe.last)
    p_free, pt_free, max_free = [None] * 2, [None] * 2, [None] * 2

    def attend(n):
        tt, h = divmod(n, MLA_H)
        q = slice(tt * P, tt * P + P)
        slot, bank, free = core.banks.take()
        core.matmul([k_ready, free], bank[:, :], qnT[:, h, q], knT[:, h, :], start=True, stop=False)
        t = core.matmul([], bank[:, :], qrT[:, h, q], krT[:, h, :], start=False, stop=True)
        m = small[:, 40 + 2 * (n % 2):42 + 2 * (n % 2)]
        core.dve([t, max_free[n % 2]], V.tensor_reduce, m[:, 0:1], bank[:, :], AX.X, MAX)
        s = core.ts([], m[:, 1:2], m[:, 0:1], -scale, MUL)
        s = core.f([s, p_free[n % 2]], p_sb[:, n % 2, :], bank[:, :], ACT.Exp, bias=m[:, 1:2], scale=scale,
                   accum_out=den[:, tt, h:h + 1])
        max_free[n % 2] = s
        core.banks.release(slot, s)
        return s

    def attended(n, ready):
        tt, h = divmod(n, MLA_H)
        slot, bank, t = turned(core, [ready], [p_sb[:, n % 2, c * P:c * P + P] for c in range(TILES)], ident)
        p_free[n % 2] = t
        s = core.act([t, pt_free[n % 2]], nc.scalar.copy, PT[:, n % 2, :], bank[:, :])
        core.banks.release(slot, s)
        for c in range(TILES):
            t = core.matmul([s], core.held[tt][:, h * P:h * P + P], PT[:, n % 2, c * P:c * P + P], vm[:, c, h, :],
                            start=c == 0, stop=c == TILES - 1)
        pt_free[n % 2] = t
        return t

    def attention_out(tt, ready):
        core.dve([core.act.last], V.reciprocal, den[:, tt, :], den[:, tt, :])
        s = core.tt([ready], att[:, tt, :].rearrange("p (h d) -> p h d", h=MLA_H),
                    core.held[tt][:, :].rearrange("p (h d) -> p h d", h=MLA_H),
                    wide(den[:, tt, :].unsqueeze(2), [P, MLA_H, MLA_V]), MUL)
        slot, bank, t = turned(core, [s], [att[:, tt, c * P:c * P + P] for c in range(4)], ident)
        s = core.dve([t], V.tensor_copy, mixT[:, 0:4, tt * P:tt * P + P], bank[:, :].rearrange("p (c t) -> p c t", c=4))
        core.banks.release(slot, s)

    heads_all = NT * MLA_H
    ready = attend(0)
    for n in range(heads_all):
        following = attend(n + 1) if n + 1 < heads_all else None
        if n % 2 == 0:
            next_late()
            weighted()
        for step in prepare[n]:
            step()
        t = attended(n, ready)
        ready = following
        if n % MLA_H == MLA_H - 1:
            attention_out(n // MLA_H, t)
    assert len(prepare) == heads_all
    mla.close()
    core.meet()
    def mix_out(i, ready):
        view, landed = stream.next()
        for k in range(4):
            for tt in range(NT):
                for h in range(2):
                    t = core.matmul([ready, landed], core.held[2 * tt + h][:, :], mixT[:, 4 * i + k, tt * P:tt * P + P],
                                    view[:, k, h * 512:h * 512 + 512], start=i + k == 0, stop=i == 1 and k == 3, mark=k == 3)
        stream.done(t)

    fill = [[], [next_late, weighted], [], [next_late, weighted], [], [next_late], [next_late],
            [lambda: mix_out(0, [core.dve.last])]]
    with ExitStack() as own:
        mlstm(core, K, lambda n, shape, dt=F32: sb(core, own, n, shape, dt), ml, fill, vec, R_GML, v_ext, o_gate,
              mixT, small, ident)
    core.meet()
    tile = whole
    core.ts([], scale2, mod[:, 32:40, 0], 1.0, ADD)
    core.tt([], scale2, scale2, vec[:, R_G2:R_G2 + 8], MUL)

    mix_out(1, [core.dve.last, core.act.last])
    t = core.pe.last
    for tt in range(NT):
        for h in range(2):
            c = slice(h * 512, h * 512 + 512)
            core.tt([t], sq[:, c], core.held[2 * tt + h][:, :], gt1[:, c], MUL)
            s = core.tt([], x[:, tt, c], x[:, tt, c], sq[:, c], ADD)
    core.act.wait(s)
    s = normed(core, [s], x, xn, sq, small)
    h2_ready = scaled_transposed(core, [s], xn, hT, 0, scale2, mod[:, 24:32, 0], ident)
    for tt in range(NT):
        for half in range(2):
            slot, bank, t = turned(core, [h2_ready], [hT[:, 4 * half + k, tt * P:tt * P + P] for k in range(4)], ident)
            s = core.copy([t], h2[:, tt, half * 512:half * 512 + 512], bank[:, :])
            core.banks.release(slot, s)
    core.rings.remove(ring)
    core.rings.remove(sums)


def mlstm_prepare(core, K, tiles, convw, qk_lat, k_ctx, pads, gates, rows_at, sums_at, sq, ident):
    nc = core.nc
    V = nc.vector
    ST = 2 * NT
    tmp, gcol, ecol = (tiles[n] for n in ("tmp", "gcol", "ecol"))
    rows = rows_at.rearrange("p t d -> p (t d)")[0:ML_H, :].rearrange("p (a s) -> p a s", a=4)
    E = rows[:, 2:4, :]
    flat = sums_at.rearrange("p k t -> p (k t)")
    F, G, M = (flat[0:ML_H, i * 4 * T:(i + 1) * 4 * T].rearrange("p (a s) -> p a s", a=2) for i in range(3))
    kT = flat[:, 12 * T:16 * T].rearrange("p (c s) -> p c s", c=2)
    raw, sig = sq[:, 0:T], sq[:, T:2 * T]
    qT = sq[:, 2 * T:4 * T].rearrange("p (c s) -> p c s", c=2)
    st = {"qT": qT, "kT": kT, "M": M, "gcol": gcol, "ecol": ecol}

    def convolve(c):
        src = qk_lat[:, c, :] if c < 4 else k_ctx[:, c - 4, :]
        wc = c if c < 4 else c - 2
        core.ts([pads], raw, src[:, 0:T], convw[:, wc, 0:1], MUL)
        core.stt([], raw, src[:, 1:T + 1], convw[:, wc, 1:2], raw, MUL, ADD)
        st["raw_ready"] = core.stt([], raw, src[:, 2:T + 2], convw[:, wc, 2:3], raw, MUL, ADD)

    def silu(c):
        core.f([st["raw_ready"]], sig, raw, ACT.Sigmoid)
        if c < 2:
            core.stt([core.act.last], qT[:, c, :], raw, ML_QK ** -0.5, sig, MUL, MUL)
        else:
            at = T if c < 4 else 0
            core.tt([core.act.last], kT[:, c - 2 if c < 4 else c - 4, at:at + T], raw, sig, MUL)
        st["qk_ready"] = core.dve.last

    f = gates[:, :, 8:16]

    def log_gates():
        st["abs_ready"] = core.stt([], tmp[:, 0], f, -1.0, f, MUL, MAX)

    def log_gates_end():
        core.f([st["abs_ready"]], tmp[:, 1], tmp[:, 0], ACT.Exp, scale=-1.0)
        log1p_unit(core, [core.act.last], tmp[:, 2], tmp[:, 1], tmp[:, 3], tmp[:, 4], tmp[:, 5])
        core.ts([], f, f, 0.0, MIN)
        st["gates_ready"] = core.tt([], f, f, tmp[:, 2], SUB)

    def gates_turned(td):
        slot, bank, t = turned(core, [st["gates_ready"]], [gates[:, i, td * 4:td * 4 + 4] for i in range(ST)], ident)
        core.banks.release(slot, core.dve([t], V.tensor_copy, rows[:, td, :], bank[0:ML_H, :]))

    one = wide(K["ones"][0:ML_H, 0:1], [ML_H, T])

    def sums(d):
        def order(ap, part):
            a, b = part * T, part * T + T
            if d == 0:
                return ap[:, a:b]
            return ap[:, a:b][:, ::-1]

        def last(ap, part):
            at = part * T + (T - 1 if d == 0 else 0)
            return ap[:, at:at + 1]

        fd, idd = rows[:, 2 + d, :], rows[:, d, :]
        core.dve([], V.tensor_tensor_scan, order(F[:, d, :], 0), one, order(fd, 0), 0.0, MUL, ADD)
        core.dve([], V.tensor_tensor_scan, order(F[:, d, :], 1), one, order(fd, 1), last(F[:, d, :], 0), MUL, ADD)
        core.tt([], G[:, d, :], idd, F[:, d, :], SUB)
        g = G[:, d, :]
        core.dve([], V.tensor_tensor_scan, order(M[:, d, :], 0), order(g, 0), order(g, 0), 0.0, MAX, MAX)
        core.dve([], V.tensor_tensor_scan, order(M[:, d, :], 1), order(g, 1), order(g, 1), last(M[:, d, :], 0), MAX, MAX)

    def stabilisers():
        st["m_ready"] = core.tt([], E, F, M, ADD)

    def stabilisers_end():
        st["rows_ready"] = core.f([st["m_ready"]], E, E, ACT.Exp, scale=-1.0)

    def columns(d):
        slot, bank, free = core.banks.take()
        for i in range(ST):
            t = core.pe([st["rows_ready"], free], nc.tensor.transpose, bank[:, i * 4:i * 4 + 4],
                        G[:, d, i * P:i * P + P], ident[0:ML_H, 0:ML_H])
        for i in range(NT):
            t = core.pe([], nc.tensor.transpose, bank[:, 16 + i * 4:20 + i * 4],
                        E[:, d, T + i * P:T + i * P + P], ident[0:ML_H, 0:ML_H])
        core.dve([t], V.tensor_copy, gcol[:, d], bank[:, 0:16].rearrange("p (i h) -> p i h", h=ML_H))
        s = core.dve([], V.tensor_copy, ecol[:, :, :, d], bank[:, 16:24].rearrange("p (i h) -> p i h", h=ML_H))
        core.banks.release(slot, s)
        st["cols_ready"] = s

    conv, silu_of = ([lambda c=c, step=step: step(c) for c in range(6)] for step in (convolve, silu))
    groups = [
        [log_gates, conv[0]],
        [log_gates_end, silu_of[0], conv[1]],
        [*(lambda td=td: gates_turned(td) for td in range(4)), silu_of[1], conv[2]],
        [silu_of[2], lambda: sums(0)],
        [lambda: sums(1), stabilisers],
        [stabilisers_end, conv[3]],
        [silu_of[3], conv[4], lambda: columns(0)],
        [silu_of[4], conv[5], lambda: columns(1), silu_of[5]]]
    return groups, st


def mlstm(core, K, tile, st, fill, vec, g_row, v_ext, o_gate, mixT, small, ident):
    nc = core.nc
    V = nc.vector
    ST = 2 * NT
    qT, kT, M, gcol, ecol = (st[n] for n in ("qT", "kT", "M", "gcol", "ecol"))
    nm, nmm = tile("ml_nm", [P, 2, NT, P]), tile("ml_nmm", [P, 2, NT, P])
    W = tile("ml_W", [P, 2, ST, T])
    hn = tile("ml_hn", [P, NT, ML_H, 2, ML_V + 1])
    w_free, score_free = [None] * 2, [None] * 2
    whole_pair = [(2, 1), (3, 0)]

    def products(h):
        half = slice((h % 2) * ML_QK, (h % 2) * ML_QK + ML_QK)
        for part in range(2):
            bank = core.held[2 * (h % 2) + part]
            for e in range(2):
                at = (2 * part + e) * P
                t = core.matmul([st["qk_ready"], score_free[h % 2]], bank[:, e * T:e * T + T],
                                kT[half, h // 2, at:at + P], qT[half, h // 2, :])
        return t

    def decays(n):
        (h, d), b = divmod(n, 2), n % 2
        slot, bank, free = core.banks.take()
        t = core.matmul([st["rows_ready"], free], bank[:, 0:T], K["select"][0:ML_H, h * P:h * P + P], M[:, d, T:2 * T])
        s = core.ts([t, w_free[b]], nm[:, b], bank[:, 0:T].rearrange("p (i t) -> p i t", i=NT), -1.0, MUL)
        core.banks.release(slot, s)
        mask = K["upper"] if d == 0 else K["lower"]
        s = core.tt([], nmm[:, b], nm[:, b], wide(mask.unsqueeze(1), [P, NT, P]), ADD)
        flat = nm[:, b].rearrange("p i t -> p (i t)")
        for e in range(2):
            core.f([s, st["cols_ready"], w_free[b]], W[:, b, e, :], flat, ACT.Exp, bias=gcol[:, d, e, h:h + 1])
        for i in range(NT):
            core.f([], W[:, b, 2 + i, i * P:i * P + P], nmm[:, b, i, :], ACT.Exp, bias=gcol[:, d, 2 + i, h:h + 1])
        src, dst = whole_pair[d]
        return core.f([], W[:, b, src, dst * P:dst * P + P], nm[:, b, dst, :], ACT.Exp, bias=gcol[:, d, src, h:h + 1])

    def outputs(n, decays_ready, scores_ready):
        (h, d), b = divmod(n, 2), n % 2
        score = [core.held[2 * (h % 2) + part] for part in range(2)]
        core.tt([decays_ready, scores_ready], W[:, b, 0:2, :], W[:, b, 0:2, :],
                score[0][:, :].rearrange("p (e t) -> p e t", e=2), MUL)
        pairs = [(2, 0), (3, 1), whole_pair[d]]
        for src, i in pairs:
            c = slice(i * P, i * P + P)
            s = core.tt([], W[:, b, src, c], W[:, b, src, c],
                        score[1][:, (src - 2) * T + i * P:(src - 2) * T + i * P + P], MUL)
        if d == 1:
            score_free[h % 2] = s
        slot, bank, free = core.banks.take()
        for i in range(NT):
            use = [0, 1] + [src for src, j in sorted(pairs) if j == i]
            for src in use:
                t = core.matmul([s, free], bank[:, i * (ML_V + 1):(i + 1) * (ML_V + 1)], W[:, b, src, i * P:i * P + P],
                                v_ext[:, src, h, :], start=src == use[0], stop=src == use[-1])
        w_free[b] = t
        s = core.act([t], nc.scalar.copy, hn[:, :, h, d, :], bank[:, 0:NT * (ML_V + 1)].rearrange("p (i v) -> p i v", i=NT))
        core.banks.release(slot, s)

    scores_ready = {0: products(0)}
    ready = decays(0)
    for n in range(2 * ML_H):
        if n % 2 and n + 1 < 2 * ML_H:
            scores_ready[n // 2 + 1] = products(n // 2 + 1)
        following = decays(n + 1) if n + 1 < 2 * ML_H else None
        if n < 2 * ML_H - 1:
            for step in fill[n]:
                step()
        outputs(n, ready, scores_ready[n // 2])
        ready = following
    for step in fill[-1]:
        step()

    den = tile("ml_den", [P, NT * ML_H, 2])
    num = hn.rearrange("p i h d v -> p (i h) d v")
    raw_den = num[:, :, :, ML_V]
    core.ts([core.act.last], den, raw_den, -1.0, MUL)
    core.tt([], den, den, raw_den, MAX)
    core.tt([], den, den, ecol.rearrange("p i h d -> p (i h) d"), MAX)
    core.dve([], V.reciprocal, den, den)
    hs, ht = (W[:, b].rearrange("p s t -> p (s t)").rearrange("p (i v) -> p i v", v=ML_V) for b in range(2))
    shape = [P, NT * ML_H, ML_V]
    core.tt([core.pe.last], hs, num[:, :, 0, 0:ML_V], wide(den[:, :, 0:1], shape), MUL)
    core.tt([], ht, num[:, :, 1, 0:ML_V], wide(den[:, :, 1:2], shape), MUL)
    core.tt([], hs, hs, ht, ADD)
    core.tt([], ht, hs, hs, MUL)
    core.dve([], V.tensor_reduce, small[:, 0:8], ht, AX.X, ADD)
    s = inv_rms(core, [], small[:, 16:24], small[:, 0:8], ML_V, small[:, 8:16])
    core.tt([s], hs, hs, wide(small[:, 16:24].unsqueeze(2), shape), MUL)
    s = core.tt([], hs, hs, o_gate.rearrange("p i (h v) -> p (i h) v", h=ML_H), MUL)
    for i in range(NT):
        slot, bank, t = turned(core, [s], [hs[:, i * ML_H + h, :] for h in range(ML_H)], ident)
        for h in range(ML_H):
            s2 = core.ts([t], mixT[:, 4 + h, i * P:i * P + P], bank[:, h * P:h * P + P],
                         vec[:, g_row + h:g_row + h + 1], MUL)
        core.banks.release(slot, s2)


def experts(core, A, K, x, gt2, h2, hT, out, stack):
    nc = core.nc
    V = nc.vector
    ident = K["ident"]
    BUFS, BATCH = TOPK, 4
    BATCHES = NT * TOPK // BATCH

    def tile(name, shape, dt=F32):
        return sb(core, stack, "e_" + name, shape, dt)

    rows_uv = [tile(f"uv{j}", [P, 2 * D]) for j in range(BUFS)]
    idx = [tile(f"idx{j}", [P, 1], U32) for j in range(BUFS)]
    diag = [tile(f"diag{j}", [P, P]) for j in range(BUFS)]
    dot, act, w = tile("dot", [P, BUFS]), tile("act", [P, BUFS]), tile("w", [P, BUFS])
    chosen, weight = tile("chosen", [P, NT, SLOTS], U32), tile("weight", [P, NT, SLOTS])
    w_pq, keys, keysT = tile("w_pq", [P, KT, 2 * P]), tile("keys", [P, 2, P]), tile("keysT", [P, 2, P])
    qT, scores = tile("qT", [P, 2, T]), tile("scores", [P, NT, 2, N_KEYS])
    rest = tile("rest", [P, TOPK * TOPK])
    sv, si, sif = tile("sv", [P, NT, 2, TOPK]), tile("si", [P, NT, 2, TOPK], U32), tile("sif", [P, NT, 2, TOPK])
    cand, hot = tile("cand", [P, NT, TOPK * TOPK]), tile("hot", [P, NT, TOPK, TOPK])
    best, pos = tile("best", [P, NT, TOPK]), tile("pos", [P, NT, TOPK], U32)
    part, partf, e01 = tile("part", [P, NT, TOPK], U32), tile("partf", [P, NT, TOPK]), tile("e01", [P, 2, NT, TOPK])
    gap, norm = tile("gap", [P, NT, TOPK]), tile("norm", [P, NT])

    sem = nc.alloc_semaphore
    landed, free = ([sem(f"{name}{j}") for j in range(BUFS)] for name in ("uv_in", "uv_free"))
    idx_set = [sem(f"idx_set{j}") for j in range(BUFS)]
    seen, dots_done, gelu_done, diags_done = (
        sem(n) for n in ("indices_seen", "dots_done", "gelu_done", "diags_done"))
    w_in, keys_in, keys_turned, queries_done, scores_done, keysT_set, qT_set, scores_set, scores_seen, best_set, exp_set, routed = (
        sem(n) for n in ("w_pq_in", "keys_in", "keys_turned", "queries_done", "scores_done", "keysT_set",
                         "qT_set", "scores_set", "scores_seen", "best_set", "exp_set", "routed"))
    steps = Lane(nc, nc.vector, "steps", True)
    acc = [core.held[0:2], core.held[2:4]]
    bank_k, bank_q, bank_s = core.banks.items[0:3]
    table = A["experts"]

    def after(engine, sem, heads):
        if not isinstance(heads, int) or heads > 0:
            engine.wait_ge(sem, heads)

    def load_head(head):
        w_cols = A["w_pq_2"][:, :, bass.ds(head * 2 * P, 2 * P)]
        after(nc.sync, keys_turned, head)
        nc.sync.dma_start(keys, A["sub_keys_2"][:, bass.ds(head, 1)].rearrange("o h a k d -> k (o h a) d")).then_inc(keys_in, 16)
        after(nc.sync, queries_done, head)
        nc.sync.dma_start(w_pq, w_cols.rearrange("o (k p) n -> p (o k) n", p=P)).then_inc(w_in, 16)

    def product_keys(head):
        def keys_step():
            nc.tensor.wait_ge(keys_in, head * 16 + 16)
            for a in range(2):
                t = nc.tensor.transpose(bank_k[:, a * P:a * P + P], keys[:, a, :], ident)
            t.then_inc(keys_turned, 1)
            nc.scalar.wait_ge(keys_turned, head + 1)
            nc.scalar.copy(keysT, bank_k[:, 0:2 * P].rearrange("p (a k) -> p a k", a=2)).then_inc(keysT_set, 1)
            nc.tensor.wait_ge(w_in, head * 16 + 16)
            queries(0)

        def queries(a):
            for k in range(KT):
                t = nc.tensor.matmul(bank_q[:, a * T:a * T + T], w_pq[:, k, a * P:a * P + P], hT[:, k, 0:T],
                                     start=k == 0, stop=k == KT - 1)
            return t

        def queries_step():
            queries(1).then_inc(queries_done, 1)
            nc.scalar.wait_ge(queries_done, head + 1)
            nc.scalar.copy(qT, bank_q[:, :].rearrange("p (a t) -> p a t", a=2)).then_inc(qT_set, 1)

        def scores_step():
            nc.tensor.wait_ge(keysT_set, head + 1)
            nc.tensor.wait_ge(qT_set, head + 1)
            for tt in range(NT):
                for a in range(2):
                    t = nc.tensor.matmul(bank_s[:, (2 * tt + a) * P:(2 * tt + a) * P + P],
                                         qT[:, a, tt * P:tt * P + P], keysT[:, a, :], start=True, stop=True)
            t.then_inc(scores_done, 1)
            nc.scalar.wait_ge(scores_done, head + 1)
            after(nc.scalar, routed, head)
            nc.scalar.copy(scores, bank_s[:, :].rearrange("p (t a k) -> p t a k", t=NT, a=2)).then_inc(scores_set, 1)

        return [keys_step, queries_step, scores_step]

    def top16(values, scratch, out_v, out_i):
        steps([], V.max, out_v[:, 0:8], values)
        steps([], V.max_index, out_i[:, 0:8], out_v[:, 0:8], values)
        steps([], V.match_replace, scratch, out_v[:, 0:8], values, -3e38)
        steps([], V.max, out_v[:, 8:16], scratch)
        steps([], V.max_index, out_i[:, 8:16], out_v[:, 8:16], scratch)

    def route(head):
        shape = [P, NT, TOPK, TOPK]
        col = bass.ds(head * TOPK, TOPK)

        def halves(tt):
            if tt == 0:
                nc.vector.wait_ge(scores_set, head + 1)
                nc.vector.sem_inc(scores_seen, 1)
            for a in range(2):
                top16(scores[:, tt, a, :], rest[:, 0:N_KEYS], sv[:, tt, a, :], si[:, tt, a, :])

        def candidates():
            steps([], V.tensor_copy, sif, si)
            steps([], V.tensor_tensor, cand.rearrange("p t (i j) -> p t i j", i=TOPK),
                  wide(sv[:, :, 0, :].unsqueeze(3), shape), wide(sv[:, :, 1, :].unsqueeze(2), shape), ADD)
            for tt in range(NT):
                top16(cand[:, tt, :], rest, best[:, tt, :], pos[:, tt, :])
            steps([], V.tensor_tensor, gap, best, wide(best[:, :, 0:1], [P, NT, TOPK]), SUB)
            nc.vector.wait_ge(*steps.last)
            nc.vector.sem_inc(best_set, 1)
            nc.scalar.wait_ge(best_set, head + 1)
            nc.scalar.activation(best, gap, ACT.Exp).then_inc(exp_set, 1)

        def places():
            iota = wide(K["iota"].unsqueeze(1).unsqueeze(1), shape)
            for a, (op, by) in enumerate(((ALU.logical_shift_right, 4), (ALU.bitwise_and, 15))):
                steps([], V.tensor_scalar, part, pos, by, None, op)
                steps([], V.tensor_copy, partf, part)
                steps([], V.tensor_tensor, hot, wide(partf.unsqueeze(3), shape), iota, ALU.is_equal)
                steps([], V.tensor_tensor, hot, hot, wide(sif[:, :, a, :].unsqueeze(2), shape), MUL)
                steps([], V.tensor_reduce, e01[:, a], hot, AX.X, ADD)

        def weights():
            steps([], V.scalar_tensor_tensor, e01[:, 0], e01[:, 0], float(N_KEYS), e01[:, 1], MUL, ADD)
            steps([], V.tensor_copy, chosen[:, :, col], e01[:, 0])
            nc.vector.wait_ge(exp_set, head + 1)
            steps([], V.tensor_reduce, norm, best, AX.X, ADD)
            steps([], V.reciprocal, norm, norm)
            steps([], V.tensor_tensor, weight[:, :, col], best, wide(norm.unsqueeze(2), [P, NT, TOPK]), MUL)
            nc.vector.wait_ge(*steps.last)
            nc.vector.sem_inc(routed, 1)

        return [lambda: halves(0), lambda: halves(1), candidates, places, weights]

    def rewind():
        nc.vector.wait_ge(*steps.last)
        nc.vector.sem_clear(steps.sem)
        steps.clear()

    def gather(turn):
        nc.gpsimd.wait_ge(routed, turn + 1)
        for n in range(NT * TOPK):
            tt, j = divmod(n, BUFS)
            use = turn * NT + tt
            nc.gpsimd.wait_ge(free[j], use + 1)
            nc.gpsimd.tensor_copy(idx[j], chosen[:, tt, bass.ds(turn * TOPK + j, 1)]).then_inc(idx_set[j], 1)
            nc.gpsimd.wait_ge(idx_set[j], use + 1)
            nc.gpsimd.sem_inc(seen, 1)
            nc.gpsimd.indirect_dma_start(out=rows_uv[j], out_offset=None, in_=table,
                                         in_offset=bass.IndirectOffsetOnAxis(ap=idx[j], axis=0)).then_inc(landed[j], 16)

    def dots(turn, b):
        tt, j0 = divmod(b * BATCH, BUFS)
        for j in range(j0, j0 + BATCH):
            nc.vector.wait_ge(landed[j], turn * 32 + (tt * 16 + 16))
            u = rows_uv[j][:, 0:D]
            ins = nc.vector.tensor_tensor_reduce(u, u, h2[:, tt, :], 1.0, 0.0, MUL, ADD, dot[:, j:j + 1])
        ins.then_inc(dots_done, 1)
        nc.scalar.wait_ge(dots_done, turn * BATCHES + (b + 1))
        nc.scalar.activation(act[:, j0:j0 + BATCH], dot[:, j0:j0 + BATCH], ACT.Gelu).then_inc(gelu_done, 1)

    def add(turn, b):
        tt, j0 = divmod(b * BATCH, BUFS)
        cols = slice(j0, j0 + BATCH)
        nc.vector.wait_ge(gelu_done, turn * BATCHES + (b + 1))
        steps([], V.tensor_tensor, w[:, cols], act[:, cols], weight[:, tt, bass.ds(turn * TOPK + j0, BATCH)], MUL)
        nc.vector.wait_ge(*steps.last)
        for j in range(j0, j0 + BATCH):
            ins = nc.vector.tensor_scalar(diag[j], ident, w[:, j:j + 1], None, MUL)
        ins.then_inc(diags_done, 1)
        nc.tensor.wait_ge(diags_done, turn * BATCHES + (b + 1))
        for j in range(j0, j0 + BATCH):
            for h in range(2):
                ins = nc.tensor.matmul(acc[tt][h], diag[j], rows_uv[j][:, D + h * 512:D + h * 512 + 512],
                                       start=False, stop=False, skip_group_check=True)
            ins.then_inc(free[j], 1)

    def experts_of(turn, between):
        for b in range(BATCHES):
            dots(turn, b)
            for step in between[b]:
                step()
            if b:
                add(turn, b - 1)
        add(turn, BATCHES - 1)
        rewind()

    for tt in range(NT):
        for h in range(2):
            core.matmul([], acc[tt][h], K["zeros"], h2[:, tt, h * 512:h * 512 + 512], start=True, stop=False,
                        mark=False)
    for j in range(BUFS):
        nc.tensor.sem_inc(free[j], 1)
    for head in range(2):
        load_head(head)
        for step in product_keys(head) + route(head):
            step()
        rewind()
    with nc.Fori(0, PEER_H - 2) as turn:
        head = turn + 2
        load_head(head)
        gather(turn)
        pk, rt = product_keys(head), route(head)
        experts_of(turn, [pk[0:1], pk[1:2], pk[2:3], rt[0:1], rt[1:2], rt[2:3], rt[3:4], rt[4:5]])
    with nc.Fori(PEER_H - 2, PEER_H) as turn:
        gather(turn)
        experts_of(turn, [[]] * BATCHES)
    stored = nc.alloc_semaphore("stored")
    for tt in range(NT):
        for h in range(2):
            t = core.matmul([], acc[tt][h], K["zeros"], h2[:, tt, h * 512:h * 512 + 512], start=False, stop=True)
    for tt in range(NT):
        for h in range(2):
            c = slice(h * 512, h * 512 + 512)
            core.tt([t], h2[:, tt, c], acc[tt][h], gt2[:, c], MUL)
            s = core.tt([], x[:, tt, c], x[:, tt, c], h2[:, tt, c], ADD)
        core.sp.wait(s)
        nc.sync.dma_start(out[tt * P:tt * P + P, :], x[:, tt, :]).then_inc(stored, 16)
    nc.sync.wait_ge(stored, 16 * NT)


def program(nc, A, out):
    core = Core(nc)
    _, where = constants()
    x = nc.alloc_sbuf_tensor("x_sb", [P, NT, D], F32)[:]
    table = nc.alloc_sbuf_tensor("constants", [P, max(b for _, b in where.values())], F32)[:]
    K = {name: table[:, a:b] for name, (a, b) in where.items()}
    zeros = where["zeros"][0]
    K["mask2"] = table[:, zeros:zeros + 2 * P]
    K["ready"] = core.load("constants", table, A["constants"])
    x_in = core.load("x", x, A["x"].rearrange("b (t p) d -> p (b t) d", p=P))
    core.sp.wait(x_in, K["ready"])
    first_block(core, A, K, x)
    second_block(core, A, K, x, out)


_USED = ["x", "positions", "norm_g", "w_in", "b_gate", "cmp_pos", "cmp_w1", "cmp_w2", "lru_conv_w",
         "lru_conv_b", "lru_w_a", "lru_b_a", "lru_w_i", "lru_b_i", "lru_lam", "conv_dw_w",
         "conv_dw_b", "conv_ln_g", "conv_ln_b", "conv_w_pw2", "w_out", "final_g", "c_2", "ctx_2",
         "c_ctx_2", "w_ada_2", "b_ada_2", "g_norm1_2", "w_in_2", "g_cq_2", "w_uq_2", "g_ckv_2",
         "w_ukv_2", "g_qn_2", "g_kn_2", "conv_qk_2", "b_igate_2", "b_fgate_2", "g_mlstm_2",
         "w_out_2", "g_norm2_2", "w_pq_2", "sub_keys_2", "expert_u_2", "expert_v_2"]


def kernel(**inputs):
    import concourse.bacc as bacc
    from concourse.bass_utils import run_bass_kernel_spmd

    nc = bacc.Bacc("TRN2", target_bir_lowering=False, num_devices=1)
    arrays, A = {}, {}
    rows = np.concatenate([inputs["expert_u_2"][0], inputs["expert_v_2"][0]], axis=1)
    for name, a in [("constants", constants()[0]), ("experts", rows)] + [(n, inputs[n]) for n in _USED]:
        a = np.ascontiguousarray(a)
        arrays[f"in_{name}_dram"] = a
        A[name] = nc.dram_tensor(f"in_{name}_dram", a.shape, mybir.dt.from_np(a.dtype), kind="ExternalInput").ap()
    out = nc.dram_tensor("out_0_dram", (T, D), F32, kind="ExternalOutput").ap()
    program(nc, A, out)
    r = run_bass_kernel_spmd(nc, [arrays], core_ids=[0])
    return r.results[0]["out_0_dram"].reshape(1, T, D)
```

```python
from contextlib import ExitStack

import numpy as np
import concourse.bass as bass
from concourse import mybir

F32 = mybir.dt.float32
I32 = mybir.dt.int32
U32 = mybir.dt.uint32
ALU = mybir.AluOpType
ACT = mybir.ActivationFunctionType
AX = mybir.AxisListType
MUL, ADD, SUB, MAX, MIN = ALU.mult, ALU.add, ALU.subtract, ALU.max, ALU.min

P = 128
T = 256
NT = T // P
D = 1024
KT = D // P
DEPTH = 2
EPS = 1e-6
NEG = -1e30

HEADS, KV, HD = 8, 2, 64
REP = HEADS // KV
WIDE = 512
FT = WIDE // P
NCMP, CMP_PAD, L_CMP, S_CMP, CMP_HID = 15, 16, 32, 16, 256
LRU_C = 8.0
LRU_TAPS, DW_TAPS = 4, 31
BRANCHES = 3
TAPS_AT_ONCE = 5
C_Q, C_KVC, C_KVW, C_ZN = 0, 512, 1024, 1304
C_ULRU, C_ZLRU, C_GA, C_GB, C_ZC = 1816, 2328, 2840, 3352, 3864

MLA_H, NOPE, ROPE2, MLA_V = 4, 128, 64, 128
QK = NOPE + ROPE2
Q_RANK, KV_RANK = 256, 128
ML_H, ML_QK, ML_V = 4, 64, 128
MLA_COLS = Q_RANK + KV_RANK + ROPE2
B_QK = MLA_COLS
B_V = B_QK + 2 * ML_H * ML_QK
B_O = B_V + ML_H * ML_V
B_G = B_O + ML_H * ML_V
PEER_H, N_KEYS, TOPK = 8, 128, 16
SLOTS = PEER_H * TOPK

ROW_DW, ROW_LC, ROW_LCB, ROW_BA, ROW_BI, ROW_LAM, ROW_DWB, ROW_LNG, ROW_LNB, N_ROWS = (
    0, 31, 35, 36, 37, 38, 39, 40, 41, 42)


def constants():
    p, f = np.arange(P)[:, None], np.arange(P)[None, :]
    t = np.arange(T).reshape(NT, P)
    n = np.arange(CMP_PAD)
    parts = {}
    parts["ident"] = np.eye(P)
    parts["zeros"] = np.zeros((P, P))
    parts["lower"] = np.where(f <= p, 0.0, NEG)
    parts["upper"] = np.where(f >= p, 0.0, NEG)
    ok = (n[None, None] < NCMP) & (n[None, None] * S_CMP + L_CMP - 1 <= t.T[:, :, None])
    parts["cmp_neg"] = np.where(ok, 0.0, NEG).reshape(P, -1)
    parts["cmp_one"] = ok.astype(float).reshape(P, -1)
    parts["blocks"] = (np.arange(P)[:, None] // CMP_PAD == np.arange(HEADS)[None]).astype(float)
    inv = (np.float32(10000.0) ** (-np.arange(0, HD, 2, dtype=np.float32) / np.float32(HD)))
    parts["inv_freq"] = np.broadcast_to(inv, (P, HD // 2))
    half = ROPE2 // 4
    inv2 = np.float32(10000.0) ** (-np.arange(half, dtype=np.float32) * np.float32(2.0 / (2 * half)))
    ang = np.stack([(t // 64).T, (t % 64).T], -1).astype(np.float32)[..., None] * inv2
    parts["cos2"] = np.cos(ang).reshape(P, -1)
    parts["sin2"] = np.sin(ang).reshape(P, -1)
    sel = np.zeros((P, ML_H, P))
    sel[np.arange(ML_H), np.arange(ML_H)] = 1.0
    parts["select"] = sel.reshape(P, -1)
    parts["iota"] = np.broadcast_to(np.arange(TOPK), (P, TOPK))
    parts["ones"] = np.ones((P, P))
    at, where = 0, {}
    for name, a in parts.items():
        where[name] = (at, at + a.shape[1])
        at += a.shape[1]
    return np.concatenate(list(parts.values()), 1).astype(np.float32), where


class Lane:

    def __init__(self, nc, engine, name, chained):
        self.engine, self.sem, self.chained = engine, nc.alloc_semaphore(name), chained
        self.count, self.seen = 0, {}

    def wait(self, *tokens):
        for token in tokens:
            if isinstance(token, list):
                self.wait(*token)
            elif token is not None and self.seen.get(token[0].name, 0) < token[1]:
                self.engine.wait_ge(token[0], token[1])
                self.seen[token[0].name] = token[1]

    @property
    def last(self):
        return (self.sem, self.count) if self.count else None

    def __call__(self, tokens, issue, *args, mark=True, behind=None, **kw):
        self.wait(*tokens)
        if self.chained:
            self.wait(behind or self.last)
        ins = issue(*args, **kw)
        if mark:
            ins.then_inc(self.sem, 1)
            self.count += 1
        return self.last

    def clear(self):
        self.count, self.seen = 0, {}


class Arrivals:

    def __init__(self, nc, name):
        self.nc, self.sem, self.count = nc, nc.alloc_semaphore(name), 0

    def load(self, lane, tokens, out, in_, **kw):
        lane.wait(*tokens)
        lane.engine.dma_start(out, in_, **kw).then_inc(self.sem, 16)
        self.count += 16
        return (self.sem, self.count)

    def clear(self):
        self.count = 0


class Ring:

    def __init__(self, items):
        self.items = items
        self.clear()

    def take(self):
        n = len(self.items)
        self.at = next(i % n for i in range(self.at + 1, self.at + 1 + n) if not self.taken[i % n])
        self.taken[self.at] = True
        return self.at, self.items[self.at], self.free[self.at]

    def release(self, slot, token):
        self.free[slot], self.taken[slot] = token, False

    def clear(self):
        n = len(self.items)
        self.free, self.taken, self.at = [None] * n, [False] * n, -1


class WeightStream:

    def __init__(self, core, ring, plan, at_once=None):
        self.core, self.ring, self.plan, self.ready = core, ring, list(plan), []
        for _ in range(at_once or len(ring.items)):
            self.fetch()

    def fill(self):
        while len(self.ready) < len(self.ring.items):
            self.fetch()

    def fetch(self):
        if self.plan:
            src, k, n = self.plan.pop(0)
            slot, buf, free = self.ring.take()
            view = buf[:, 0:k * n].rearrange("p (k n) -> p k n", k=k)
            self.ready.append((slot, view, self.core.load(f"weights{slot}", view, src, [free])))

    def next(self):
        return self.ready[0][1:]

    def done(self, token):
        self.drop(self.hold(), token)

    def hold(self):
        return self.ready.pop(0)

    def drop(self, held, token):
        self.ring.release(held[0], token)
        self.fetch()


class Core:

    def __init__(self, nc):
        self.nc = nc
        self.dve = Lane(nc, nc.vector, "dve_done", True)
        self.act = Lane(nc, nc.scalar, "act_done", True)
        self.pool = Lane(nc, nc.gpsimd, "pool_done", True)
        self.pe = Lane(nc, nc.tensor, "pe_done", False)
        self.sp = Lane(nc, nc.sync, "sp_done", False)
        self.lanes = [self.dve, self.act, self.pool, self.pe, self.sp]
        self.streams, self.rings = {}, []
        self.flip = 0
        banks = [nc.alloc_psum_tensor(f"bank{i}", [P, 512], F32)[:] for i in range(8)]
        self.banks = self.ring([b for b in banks[:4]])
        self.held = banks[4:]

    def ring(self, items):
        r = Ring(items)
        self.rings.append(r)
        return r

    def stream(self, name):
        if name not in self.streams:
            self.streams[name] = Arrivals(self.nc, "in_" + name)
        return self.streams[name]

    def load(self, name, out, in_, tokens=(), lane=None, **kw):
        return self.stream(name).load(lane or self.sp, tokens, out, in_, **kw)

    def meet(self):
        done = [lane.last for lane in self.lanes]
        for lane in self.lanes:
            lane.wait(*done)

    def restart(self):
        for s in self.streams.values():
            self.sp.wait((s.sem, s.count) if s.count else None)
        self.nc.all_engine_barrier()
        for s in [*self.lanes, *self.streams.values()]:
            self.nc.gpsimd.sem_clear(s.sem)
        self.nc.all_engine_barrier()
        for s in [*self.lanes, *self.streams.values(), *self.rings]:
            s.clear()

    def matmul(self, tokens, out, lhsT, rhs, start=True, stop=True, mark=None, **kw):
        return self.pe(tokens, self.nc.tensor.matmul, out, lhsT, rhs, start=start, stop=stop,
                       mark=stop if mark is None else mark, **kw)

    def copy(self, tokens, out, in_):
        self.flip ^= 1
        if self.flip:
            return self.dve(tokens, self.nc.vector.tensor_copy, out, in_)
        return self.act(tokens, self.nc.scalar.copy, out, in_)

    def tt(self, tokens, out, a, b, op):
        return self.dve(tokens, self.nc.vector.tensor_tensor, out, a, b, op)

    def ts(self, tokens, out, a, s1, op0, s2=None, op1=None):
        if s2 is None:
            return self.dve(tokens, self.nc.vector.tensor_scalar, out, a, s1, None, op0)
        return self.dve(tokens, self.nc.vector.tensor_scalar, out, a, s1, s2, op0, op1)

    def stt(self, tokens, out, a, s, b, op0, op1, **kw):
        return self.dve(tokens, self.nc.vector.scalar_tensor_tensor, out, a, s, b, op0, op1, **kw)

    def f(self, tokens, out, a, func, **kw):
        return self.act(tokens, self.nc.scalar.activation, out, a, func, **kw)


def wide(ap, shape):
    return ap.to_broadcast(shape)


def sb(core, stack, name, shape, dt=F32):
    return stack.enter_context(core.nc.sbuf_tensor(name, shape, dt))[:]


def inv_rms(core, tokens, out, sums, width, scratch):
    core.ts(tokens, scratch, sums, 1.0 / width, MUL, EPS, ADD)
    t = core.dve([], core.nc.vector.reciprocal, scratch, scratch)
    return core.f([t], out, scratch, ACT.Sqrt)


def normed(core, ready, x, xn, sq, small, tiles=range(NT)):
    a, b = tiles[0], tiles[-1] + 1
    for tt in tiles:
        s = core.f(ready, sq, x[:, tt, :], ACT.Square, accum_out=small[:, tt:tt + 1])
    s = inv_rms(core, [s], small[:, 4 + a:4 + b], small[:, a:b], D, small[:, 2 + a:2 + b])
    for tt in tiles:
        s = core.ts([s], xn[:, tt, :], x[:, tt, :], small[:, 4 + tt:5 + tt], MUL)
    return s


def scaled_transposed(core, ready, xn, hT, col, scale, shift, ident):
    for k in range(KT):
        slot, bank, free = core.banks.take()
        for tt in range(NT):
            t = core.pe([ready, free], core.nc.tensor.transpose, bank[:, tt * P:tt * P + P],
                        xn[:, tt, k * P:k * P + P], ident)
        if shift is None:
            t = core.ts([t], hT[:, k, col:col + T], bank[:, 0:T], scale[:, k:k + 1], MUL)
        else:
            t = core.ts([t], hT[:, k, col:col + T], bank[:, 0:T], scale[:, k:k + 1], MUL,
                        shift[:, k:k + 1], ADD)
        core.banks.release(slot, t)
    return t


def log1p_unit(core, tokens, out, z, s, s2, acc):
    core.ts(tokens, s, z, 2.0, ADD)
    core.dve([], core.nc.vector.reciprocal, s, s)
    core.tt([], s, s, z, MUL)
    core.tt([], s2, s, s, MUL)
    core.ts([], acc, s2, 1.0 / 17, MUL, 1.0 / 15, ADD)
    for odd in (13, 11, 9, 7, 5, 3, 1):
        core.tt([], acc, acc, s2, MUL)
        core.ts([], acc, acc, 1.0 / odd, ADD)
    core.tt([], acc, acc, s, MUL)
    return core.ts([], out, acc, 2.0, MUL)


def rope_angles(core, ready, pos, inv_freq, cos, sin, ang, turns):
    two_pi, magic = 2 * np.pi, 1.5 * 2.0**23
    part1 = 6.28125
    part2 = float(np.float32(np.round((two_pi - part1) * 2**21) / 2**21))
    part3 = two_pi - part1 - part2
    edge = 3.1415925
    for tt in range(NT):
        core.ts(ready, ang[:, tt, :], inv_freq, pos[:, tt:tt + 1], MUL)
    core.ts([], turns, ang, 1.0 / two_pi, MUL)
    core.ts([], turns, turns, magic, ADD)
    core.ts([], turns, turns, magic, SUB)
    for part in (part1, part2, part3):
        core.stt([], ang, turns, -part, ang, MUL, ADD)
    s = core.ts([], ang, ang, edge, MIN, -edge, MAX)
    core.f([s], sin, ang, ACT.Sin)
    core.stt([], turns, ang, -1.0, ang, MUL, MAX)
    s = core.ts([], turns, turns, -1.0, MUL, np.pi / 2, ADD)
    return core.f([s], cos, turns, ACT.Sin)


def first_block(core, A, K, x):
    nc = core.nc
    with ExitStack() as stack:
        def tile(name, shape, dt=F32):
            return sb(core, stack, name, shape, dt)

        w = core.ring([tile(f"weights{i}", [P, 4096]) for i in range(4)])
        tiles = {}
        for name, shape in (
                ("hT", [P, KT, T]), ("xn", [P, NT, D]), ("sq", [P, D]), ("small", [P, 8]),
                ("rows", [N_ROWS, WIDE]), ("vec", [P, FT, N_ROWS]), ("sp8", [P, FT]), ("sc", [P, 24]),
                ("grows", [KT, P]), ("gT", [P, KT]), ("b_gate", [P, 24]),
                ("cos", [P, NT, 32]), ("sin", [P, NT, 32]), ("ang", [P, NT, 32]), ("turns", [P, NT, 32]),
                ("posf", [P, NT]),
                ("ubuf", [P, FT, DW_TAPS - 1 + T]), ("conv", [P, FT, T]), ("fa", [P, FT, T]),
                ("fb", [P, FT, T]), ("fc", [P, FT, T]), ("fd", [P, FT, T]),
                ("lbuf", [P, FT, LRU_TAPS - 1 + T]), ("xc", [P, FT, T]),
                ("qr", [P, NT, WIDE]), ("kr", [P, 3, NT, P]), ("vr", [P, 3, NT, P]),
                ("r1", [P, WIDE // 2]), ("r2", [P, WIDE // 2]),
                ("qT", [P, FT, T]), ("kT", [P, 2, T]), ("pair", [P, 2, KV, T]), ("cT", [P, 2, T]),
                ("pos_rows", [16, 2, P]), ("posT", [P, 2, 16]), ("blk", [P, 2, 16, KV * CMP_PAD]),
                ("hidT", [P, 2, 2, KV * CMP_PAD]), ("hid_rep", [P, 2, HEADS, CMP_PAD]), ("sig32", [P, 32]),
                ("w2", [P, 2, 2, HD]), ("kcT", [P, CMP_PAD]), ("vcb", [P, HEADS, HD]),
                ("gates", [P, NT, 24]), ("zn", [P, NT, WIDE]), ("mixT", [P, 12, T]),
                ("S", [P, 4, T]), ("mx", [P, 4]), ("sums", [P, NT, 3, HEADS]),
                ("pc", [P, HEADS, CMP_PAD]), ("mc", [P, HEADS]), ("PT", [P, 3, 512]),
                ("y", [P, WIDE]), ("yt", [P, WIDE]), ("coef", [P, 3, HEADS]), ("bd", [P, 2, FT, P])):
            tiles[name] = tile(name, shape)
        posi = tile("posi", [P, NT], I32)
        core.dve([], nc.vector.memset, tiles["bd"][:], 0.0)
        core.dve([], nc.vector.memset, tiles["ubuf"][:], 0.0)
        core.dve([], nc.vector.memset, tiles["lbuf"][:], 0.0)
        core.dve([], nc.vector.memset, tiles["blk"][:], 0.0)
        s = core.load("pos", posi[:], A["positions"].rearrange("b (t p) -> p (b t)", p=P),
                      allow_slow_non_contiguous=True)
        s = core.dve([s, K["ready"]], nc.vector.tensor_copy, tiles["posf"][:], posi[:])
        rope_angles(core, [s], tiles["posf"], K["inv_freq"], tiles["cos"][:], tiles["sin"][:],
                    tiles["ang"], tiles["turns"][:])
        products = tiles["xn"].rearrange("p t (h c n) -> p (t h) c n", h=2, n=T)
        tap_ring = core.ring([products[:, i] for i in range(4)])
        core.restart()
        with nc.Fori(0, DEPTH) as layer:
            first_layer(core, A, K, x, w, tap_ring, tiles, layer)
            core.restart()
        core.rings.remove(w)
        core.rings.remove(tap_ring)


def first_layer(core, A, K, x, w, tap_ring, tl, layer):
    nc = core.nc
    V = nc.vector
    one = bass.ds(layer, 1)
    ident = K["ident"]
    hT, vec, mixT = tl["hT"], tl["vec"], tl["mixT"]

    def rows_of(ap):
        return ap.rearrange("o (k p) n -> p (o k) n", p=P)

    gain_in = core.load("gain", tl["grows"][:], A["norm_g"][one, :].rearrange("o (k p) -> (o k) p", p=P))
    slot, bank, free = core.banks.take()
    t = core.pe([gain_in], nc.tensor.transpose, bank[:, 0:KT], tl["grows"][:], ident[0:KT, 0:KT])
    gain_ready = core.dve([t], V.tensor_copy, tl["gT"][:], bank[:, 0:KT])
    core.banks.release(slot, gain_ready)

    stream = WeightStream(core, w, [
        *((rows_of(A["w_in"][one, :, c0:c0 + n]), KT, n) for c0, n in (
            (C_GB, WIDE), (C_GA, WIDE), (C_ULRU, WIDE), (C_Q, WIDE), (C_KVC, WIDE),
            (C_KVW, C_ZN - C_KVW), (C_ZN, WIDE), (C_ZLRU, WIDE))),
        *((rows_of(A["cmp_w1"][one, b]), 16, CMP_HID) for b in range(2)),
        (rows_of(A["w_in"][one, :, C_ZC:C_ZC + WIDE]), KT, WIDE),
        (rows_of(A["conv_w_pw2"][one]), FT, WIDE),
        *((rows_of(A["w_out"][one, i * 512:i * 512 + 512, :]), 4, D) for i in (1, 2, 0))], at_once=1)

    rows = tl["rows"]
    core.load("rows", rows[ROW_DW:ROW_LC, :], A["conv_dw_w"][one].rearrange("o k c -> (o k) c"))
    core.load("rows", rows[ROW_LC:ROW_LCB, :], A["lru_conv_w"][one].rearrange("o k c -> (o k) c"))
    for r, name in ((ROW_LCB, "lru_conv_b"), (ROW_BA, "lru_b_a"), (ROW_BI, "lru_b_i"),
                    (ROW_LAM, "lru_lam"), (ROW_DWB, "conv_dw_b"), (ROW_LNG, "conv_ln_g"),
                    (ROW_LNB, "conv_ln_b")):
        rows_in = core.load("rows", rows[r:r + 1, :], A[name][one, :])

    core.load("misc", tl["b_gate"][:], A["b_gate"][one, :].to_broadcast([P, 24]))
    core.load("misc", tl["pos_rows"][:], A["cmp_pos"][one].rearrange("o b (j e) d -> j (o b) (e d)", e=2))
    misc_in = core.load("misc", tl["w2"][:], A["cmp_w2"][one].rearrange("o b (k p) d -> p (o b) k d", p=P))

    stream.fill()
    bd = tl["bd"]
    for i, name in enumerate(("lru_w_a", "lru_w_i")):
        for par in range(2):
            bd_in = core.load("bd", bd[par * HD:par * HD + HD, i, :, par * HD:par * HD + HD],
                              A[name][one, par:HEADS:2].rearrange("o h i j -> i (o h) j"))
    xn_ready = normed(core, [], x, tl["xn"], tl["sq"][:], tl["small"])

    h_ready = scaled_transposed(core, [xn_ready, gain_ready], tl["xn"], hT, 0, tl["gT"], None, ident)

    slot, bank, free = core.banks.take()
    for c in range(FT):
        t = core.pe([rows_in, free], nc.tensor.transpose, bank[:, c * N_ROWS:(c + 1) * N_ROWS],
                    rows[:, c * P:c * P + P], ident[0:N_ROWS, 0:N_ROWS])
    vec_ready = core.dve([t], V.tensor_copy, vec[:], bank[:, 0:FT * N_ROWS].rearrange("p (c r) -> p c r", c=FT))
    core.banks.release(slot, vec_ready)

    lam = vec[:, :, ROW_LAM]
    sp8, sc = tl["sp8"], tl["sc"]
    s = core.stt([], sc[:, 0:4], lam, -1.0, lam, MUL, MAX)
    s = core.f([s], sc[:, 4:8], sc[:, 0:4], ACT.Exp, scale=-1.0)
    log1p_unit(core, [s], sc[:, 8:12], sc[:, 4:8], sc[:, 12:16], sc[:, 16:20], sc[:, 20:24])
    core.ts([], sc[:, 0:4], lam, -1.0, MUL, 0.0, MAX)
    core.tt([], sp8[:], sc[:, 0:4], sc[:, 8:12], ADD)
    half, neg = sc[:, 0:4], sc[:, 4:8]
    core.ts([], half, sp8[:], LRU_C / 2, MUL)
    sp_ready = core.ts([], neg, sp8[:], -LRU_C, MUL)

    def feature_steps(use, pieces=0):
        def step(c):
            view, landed = stream.next()
            slot, bank, free = core.banks.take()
            for e in range(2):
                for k in range(KT):
                    t = core.matmul([landed, h_ready, free], bank[:, e * T:e * T + T],
                                    view[:, k, (c + e) * P:(c + e) * P + P], hT[:, k, :],
                                    start=k == 0, stop=k == KT - 1)
            core.banks.release(slot, use(c, bank[:, :].rearrange("p (e t) -> p e t", e=2), t))
            spare(pieces)
            if c + 2 == FT:
                stream.done(t)

        return [lambda c=c: step(c) for c in range(0, FT, 2)]

    def by_feature(use, pieces=0):
        for step in feature_steps(use, pieces):
            step()

    def by_token(n, use, pieces):
        view, landed = stream.next()
        for tt in range(NT):
            slot, bank, free = core.banks.take()
            for k in range(KT):
                t = core.matmul([landed, h_ready, free], bank[:, 0:n], hT[:, k, tt * P:tt * P + P],
                                view[:, k, :], start=k == 0, stop=k == KT - 1)
            core.banks.release(slot, use(tt, bank, t))
            spare(pieces)
        stream.done(t)

    fa, fb, fc, fd, conv, xc = tl["fa"], tl["fb"], tl["fc"], tl["fd"], tl["conv"], tl["xc"]
    ubuf, lbuf = tl["ubuf"], tl["lbuf"]

    later, tap_left = [], []

    def spare(pieces):
        for _ in range(min(pieces, len(later))):
            later.pop(0)()
        for _ in range(min(TAPS_AT_ONCE, len(tap_left))):
            tap(tap_left.pop(0))

    def taps(out, src, tiles, row_w, row_b, first, end):
        s = {c: core.dve.last for c in tiles}
        for j in range(first, end):
            for c in tiles:
                if j == 0:
                    s[c] = core.ts([], out[:, c, :], src[:, c, 0:T], vec[:, c, row_w:row_w + 1], MUL,
                                   vec[:, c, row_b:row_b + 1], ADD)
                else:
                    s[c] = core.stt([], out[:, c, :], src[:, c, j:j + T], vec[:, c, row_w + j:row_w + j + 1],
                                    out[:, c, :], MUL, ADD, behind=s[c])
        return core.dve.last

    def tap(j):
        slot, product, free = tap_ring.take()
        for c in range(FT // 2):
            row = ROW_DW + j
            if j == 0:
                s = core.f([free], product[:, c, :], ubuf[:, c, 0:T], ACT.Identity,
                           bias=vec[:, c, ROW_DWB:ROW_DWB + 1], scale=vec[:, c, row:row + 1])
            else:
                s = core.f([free], product[:, c, :], ubuf[:, c, j:j + T], ACT.Copy, scale=vec[:, c, row:row + 1])
        if j == 0:
            t = core.pool([s], nc.gpsimd.tensor_copy, conv[:, 0:2, :], product)
        else:
            t = core.pool([s], nc.gpsimd.tensor_tensor, conv[:, 0:2, :], conv[:, 0:2, :], product, ADD)
        tap_ring.release(slot, t)

    by_feature(lambda c, b, t: core.f([t], fb[:, c:c + 2, :], b, ACT.Sigmoid))
    sig_ready = core.act.last
    def use_a(c, b, t):
        s = core.tt([t, sig_ready], ubuf[:, c:c + 2, DW_TAPS - 1:], b, fb[:, c:c + 2, :], MUL)
        if c == 0:
            core.act.wait(s)
            tap_left.extend(range(DW_TAPS))
        return s

    by_feature(use_a)
    for first in range(0, DW_TAPS, 4):
        later.append(lambda first=first: taps(conv, ubuf, range(FT // 2, FT), ROW_DW, ROW_DWB, first,
                                              min(first + 4, DW_TAPS)))
    by_feature(lambda c, b, t: core.f([t], lbuf[:, c:c + 2, LRU_TAPS - 1:], b, ACT.Copy), 2)
    u_ready = core.act.last
    core.dve.wait(u_ready)
    xc_ready = taps(xc, lbuf, range(FT), ROW_LC, ROW_LCB, 0, LRU_TAPS)

    cos, sin, r1, r2, qr, kr, vr = (tl[n] for n in ("cos", "sin", "r1", "r2", "qr", "kr", "vr"))

    def rotate(tt, t, out, src, g, i):
        n = g * i * 32
        shape = [P, g, i, 32]
        c4 = wide(cos[:, tt, :].unsqueeze(1).unsqueeze(1), shape)
        s4 = wide(sin[:, tt, :].unsqueeze(1).unsqueeze(1), shape)
        v1 = r1[:, 0:n].rearrange("p (g i d) -> p g i d", g=g, i=i)
        v2 = r2[:, 0:n].rearrange("p (g i d) -> p g i d", g=g, i=i)
        a, b = src[:, :, :, 0:32], src[:, :, :, 32:64]
        core.tt([t], v1, a, c4, MUL)
        core.tt([], v2, b, s4, MUL)
        core.tt([], out[:, :, :, 0:32], v1, v2, SUB)
        core.tt([], v1, b, c4, MUL)
        core.tt([], v2, a, s4, MUL)
        return core.tt([], out[:, :, :, 32:64], v1, v2, ADD)

    def use_q(tt, bank, t):
        return rotate(tt, t, qr[:, tt, :].rearrange("p (i g d) -> p g i d", g=KV, d=HD),
                      bank[:, :].rearrange("p (g i d) -> p g i d", g=KV, d=HD), KV, REP)

    def use_k(tt, bank, t):
        s = []
        for i, (kc, b) in enumerate(((0, 0), (256, 1))):
            s.append(rotate(tt, t, kr[:, b, tt, :].rearrange("p (g i d) -> p g i d", g=KV, d=HD),
                            bank[:, kc:kc + P].rearrange("p (g i d) -> p g i d", g=KV, d=HD), KV, 1))
            s.append(core.dve([t], V.tensor_copy, vr[:, b, tt, :], bank[:, kc + P:kc + 2 * P]))
        return s

    gates = tl["gates"]

    def use_w(tt, bank, t):
        s1 = rotate(tt, t, kr[:, 2, tt, :].rearrange("p (g i d) -> p g i d", g=KV, d=HD),
                    bank[:, 0:P].rearrange("p (g i d) -> p g i d", g=KV, d=HD), KV, 1)
        s2 = core.dve([t], V.tensor_copy, vr[:, 2, tt, :], bank[:, P:2 * P])
        s1 = core.tt([t, misc_in], gates[:, tt, :], bank[:, 256:280], tl["b_gate"][:], ADD)
        return [s1, s2]

    by_token(WIDE, use_q, 0)
    slot, bank, free = core.banks.take()
    for b in range(2):
        t = core.pe([misc_in, free], nc.tensor.transpose, bank[:, b * 16:b * 16 + 16],
                    tl["pos_rows"][:, b, :], ident[0:16, 0:16])
    s = core.dve([t], V.tensor_copy, tl["posT"][:], bank[:, 0:32].rearrange("p (b j) -> p b j", b=2))
    core.banks.release(slot, s)
    for i, (dst, row) in enumerate(((fa, ROW_BA), (fc, ROW_BI))):
        for c in range(0, FT, 2):
            slot, bank, free = core.banks.take()
            for e in range(2):
                t = core.matmul([xc_ready, bd_in, free], bank[:, e * T:e * T + T], bd[:, i, c + e, :],
                                xc[:, c + e, :])
            for e in range(2):
                s = core.f([t], dst[:, c + e, :], bank[:, e * T:e * T + T], ACT.Sigmoid,
                           bias=vec[:, c + e, row:row + 1])
            core.banks.release(slot, s)

    for c in range(FT):
        core.f([sp_ready], fd[:, c, :], fa[:, c, :], ACT.Tanh, scale=half[:, c:c + 1])
    for c in range(FT):
        core.f([], fa[:, c, :], fa[:, c, :], ACT.Exp, scale=neg[:, c:c + 1])
    lru_in = core.f([], fd[:], fd[:], ACT.Sqrt)

    def lru_input():
        core.tt([lru_in], fc[:], fc[:], xc[:], MUL)
        core.stt([], fc[:], fa[:], 1.0, fc[:], ADD, MUL)
        core.tt([], fd[:], fd[:], fc[:], MUL)

    def lru_scan():
        for c in range(FT):
            core.dve([], V.tensor_tensor_scan, fc[:, c, :], fa[:, c, :], fd[:, c, :], 0.0, MUL, ADD)

    later[:0] = [lru_input, lru_scan]

    by_token(WIDE, use_k, 1)
    by_token(C_ZN - C_KVW, use_w, 1)
    s = core.f([core.dve.last], gates[:], gates[:], ACT.Sigmoid)
    qkv_ready = [s, core.dve.last]
    zn = tl["zn"]

    def use_z(tt, bank, t):
        s = core.f([t], zn[:, tt, :], bank[:, :], ACT.Sigmoid)
        return core.tt([s], zn[:, tt, :], zn[:, tt, :], bank[:, :], MUL)

    by_token(WIDE, use_z, 2)

    qT, kT, cT, pair = tl["qT"], tl["kT"], tl["cT"], tl["pair"]
    for c in range(0, FT, 2):
        slot, bank, free = core.banks.take()
        for e in range(2):
            for tt in range(NT):
                t = core.pe([qkv_ready, free], nc.tensor.transpose,
                            bank[:, e * T + tt * P:e * T + tt * P + P],
                            qr[:, tt, (c + e) * P:(c + e) * P + P], ident)
        s = core.act([t], nc.scalar.copy, qT[:, c:c + 2, :], bank[:, :].rearrange("p (e t) -> p e t", e=2))
        core.banks.release(slot, s)
    q_ready = [core.dve.last, core.act.last]
    for dst, srcs in ((kT, (kr[:, 1], kr[:, 2])), (cT, (kr[:, 0], vr[:, 0]))):
        slot, bank, free = core.banks.take()
        for e, src in enumerate(srcs):
            for tt in range(NT):
                t = core.pe([free], nc.tensor.transpose, bank[:, e * T + tt * P:e * T + tt * P + P],
                            src[:, tt, :], ident)
        s = core.act([t], nc.scalar.copy, dst[:], bank[:, :].rearrange("p (e t) -> p e t", e=2))
        core.banks.release(slot, s)
    k_ready = [core.dve.last, core.act.last]
    for g in range(KV):
        src = cT[g * HD:g * HD + HD, :, :]
        core.load("pair", pair[0:HD, :, g, :], src, [k_ready])
        pair_in = core.load("pair", pair[HD:P, :, g, 0:T - 1], src[:, :, 1:T])

    def gate_lru(c, b, t):
        s = core.f([t], fb[:, c:c + 2, :], b, ACT.Sigmoid)
        core.tt([s], fb[:, c:c + 2, :], fb[:, c:c + 2, :], b, MUL)
        return core.tt([], mixT[:, 4 + c:6 + c, :], fb[:, c:c + 2, :], fc[:, c:c + 2, :], MUL)


    blk, posT, hidT, w2 = tl["blk"], tl["posT"], tl["hidT"], tl["w2"]
    for b in range(2):
        for g in range(KV):
            ap = pair[:, b, g, :]
            src = bass.AP(ap.tensor, ap.offset, [ap.ap[0], [2, 8], [S_CMP, NCMP]])
            src2 = bass.AP(ap.tensor, ap.offset + 16, [ap.ap[0], [2, 8], [S_CMP, NCMP]])
            for half, sr in ((0, src), (1, src2)):
                dst = blk[:, b, half * 8:half * 8 + 8, g * CMP_PAD:g * CMP_PAD + NCMP]
                blk_ready = core.tt([pair_in, misc_in], dst, sr,
                            wide(posT[:, b, half * 8:half * 8 + 8].unsqueeze(2), [P, 8, NCMP]), ADD)

    def compress(b):
        view, landed = stream.next()
        slot, bank, free = core.banks.take()
        for m in range(2):
            for k in range(16):
                t = core.matmul([blk_ready, landed, free], bank[:, m * 32:m * 32 + 32],
                                view[:, k, m * P:m * P + P], blk[:, b, k, :], start=k == 0, stop=k == 15)
        stream.done(t)
        for m in range(2):
            s = core.f([t], tl["sig32"][:], bank[:, m * 32:m * 32 + 32], ACT.Sigmoid)
            s = core.tt([s], hidT[:, b, m, :], bank[:, m * 32:m * 32 + 32], tl["sig32"][:], MUL)
            core.act.wait(s)
        core.banks.release(slot, s)
        return s

    ones = K["ones"]
    mean, var = fa[:, 0, :], fa[:, 1, :]
    zc = tl["xc"]

    def gate_conv(c, b, t):
        s = core.f([t, core.dve.last], zc[:, c:c + 2, :], b, ACT.Sigmoid)
        s = core.tt([s], zc[:, c:c + 2, :], zc[:, c:c + 2, :], b, MUL)
        if c == 0:
            squares_ready.append(centred())
        else:
            layer_norm_end(squares_ready[0])
        return s

    squares_ready = []

    def centred():
        assert not later and not tap_left
        slot, bank, free = core.banks.take()
        for c in range(FT):
            t = core.matmul([core.dve.last, core.pool.last, free], bank[:, 0:T], ones, conv[:, c, :],
                            start=c == 0, stop=c == FT - 1)
        core.ts([t], mean, bank[:, 0:T], 1.0 / WIDE, MUL)
        core.banks.release(slot, core.dve.last)
        s = core.tt([], conv[:], conv[:], wide(mean.unsqueeze(1), [P, FT, T]), SUB)
        s = core.f([s], fd[:], conv[:], ACT.Square)
        return s

    def layer_norm_end(squares_ready):
        slot, bank, free = core.banks.take()
        for c in range(FT):
            t = core.matmul([squares_ready, free], bank[:, 0:T], ones, fd[:, c, :], start=c == 0, stop=c == FT - 1)
        s = inv_rms(core, [t], var, bank[:, 0:T], WIDE, fa[:, 2, :])
        core.banks.release(slot, s)
        core.tt([s], conv[:], conv[:], wide(var.unsqueeze(1), [P, FT, T]), MUL)
        for c in range(FT):
            s = core.ts([], conv[:, c, :], conv[:, c, :], vec[:, c, ROW_LNG:ROW_LNG + 1], MUL,
                        vec[:, c, ROW_LNB:ROW_LNB + 1], ADD)
        s = core.f([s], fd[:], conv[:], ACT.Sigmoid)
        act_ready.append(core.tt([s], fd[:], fd[:], conv[:], MUL))

    act_ready = []

    def pointwise(c):
        pw2, pw_in = stream.next()
        slot, bank, free = core.banks.take()
        for e in range(2):
            for k in range(FT):
                t = core.matmul([*act_ready, pw_in, free], bank[:, e * T:e * T + T],
                                pw2[:, k, (c + e) * P:(c + e) * P + P], fd[:, k, :],
                                start=k == 0, stop=k == FT - 1)
        s = core.tt([t], mixT[:, 8 + c:10 + c, :], bank[:, :].rearrange("p (e t) -> p e t", e=2),
                    zc[:, c:c + 2, :], MUL)
        core.banks.release(slot, s)
        if c + 2 == FT:
            stream.done(t)
            parts_ready.append(s)

    parts_ready = []
    cmp_ready = []

    def compressed_keys_values():
        rep, s = tl["hid_rep"], core.dve.last
        slot, bank, free = core.banks.take()
        for g in range(KV):
            for m in range(2):
                t = core.matmul([s, free], bank[g * HD:g * HD + HD, 0:CMP_PAD], w2[:, 0, m, :],
                                hidT[:, 0, m, g * CMP_PAD:g * CMP_PAD + CMP_PAD], start=m == 0, stop=m == 1)
        core.banks.release(slot, core.dve([t], V.tensor_copy, tl["kcT"][:], bank[:, 0:CMP_PAD]))
        for m in range(2):
            for g in range(KV):
                s = core.dve([], V.tensor_copy, rep[:, m, g * REP:g * REP + REP, :],
                             wide(hidT[:, 1, m, g * CMP_PAD:g * CMP_PAD + CMP_PAD].unsqueeze(1), [P, REP, CMP_PAD]))
        slot, bank, free = core.banks.take()
        for m in range(2):
            t = core.matmul([s, free], bank[:, 0:HD], rep[:, m, :, :].rearrange("p h n -> p (h n)"),
                            w2[:, 1, m, :], start=m == 0, stop=m == 1)
        s = core.tt([t], tl["vcb"][:], wide(bank[:, 0:HD].unsqueeze(1), [P, HEADS, HD]),
                    wide(K["blocks"].unsqueeze(2), [P, HEADS, HD]), MUL)
        core.banks.release(slot, s)
        cmp_ready.append(s)

    S, mx, PT, sums, coef = tl["S"], tl["mx"], tl["PT"], tl["sums"], tl["coef"]
    O = core.held
    pc, mc, y, yt = tl["pc"], tl["mc"], tl["y"], tl["yt"]
    free_of = {"y": None, "O": None, "S0": None, "S1": None, "PT0": None, "PT1": None, "PT2": None}

    def compressed_scores(qt, unit):
        at = slice(qt * CMP_PAD, qt * CMP_PAD + CMP_PAD)
        for g in range(KV):
            slot, bank, free = core.banks.take()
            for i in range(REP):
                t = core.matmul([q_ready, *cmp_ready, free], bank[:, i * CMP_PAD:(i + 1) * CMP_PAD],
                                qT[g * HD:g * HD + HD, i, qt * P:qt * P + P], tl["kcT"][g * HD:g * HD + HD, :])
            s = core.stt([t], pc[:, g * REP:g * REP + REP, :],
                         bank[:, 0:REP * CMP_PAD].rearrange("p (h n) -> p h n", h=REP), HD ** -0.5,
                         wide(K["cmp_neg"][:, at].unsqueeze(1), [P, REP, CMP_PAD]), MUL, ADD)
            core.banks.release(slot, s)
        core.dve([], V.tensor_reduce, mc[:], pc[:], AX.X, MAX)
        s = core.tt([], pc[:], pc[:], wide(mc[:].unsqueeze(2), [P, HEADS, CMP_PAD]), SUB)
        s = core.f([s], pc[:], pc[:], ACT.Exp)
        core.dve([s], V.tensor_reduce, sums[:, qt, 0, :], pc[:], AX.X, ADD)
        return core.tt([], pc[:], pc[:], wide(K["cmp_one"][:, at].unsqueeze(1), [P, HEADS, CMP_PAD]), MUL)

    def compressed_turned(qt, unit, ready):
        slot, bank, free = core.banks.take()
        t = core.pe([ready, free], nc.tensor.transpose, bank[:, 0:P], pc[:].rearrange("p h n -> p (h n)"), ident)
        s = core.dve([t, free_of[f"PT{unit % 3}"]], V.tensor_copy, PT[:, unit % 3, 0:P], bank[:, 0:P])
        core.banks.release(slot, s)
        return s

    def compressed_values(qt, unit, ready):
        t = core.matmul([ready, free_of["O"]], O[0][:, :], PT[:, unit % 3, 0:P],
                        tl["vcb"][:].rearrange("p h d -> p (h d)"))
        free_of[f"PT{unit % 3}"] = t
        return t

    def head_scores(qt, unit, i, g):
        nk, b0 = (qt + 1) * P, 2 * (unit % 2)
        mask = K["mask2"][:, (NT - 1 - qt) * P:NT * P]
        slot, bank, free = core.banks.take()
        for b in range(2):
            t = core.matmul([k_ready, free], bank[:, b * T:b * T + nk],
                            qT[g * HD:g * HD + HD, i, qt * P:qt * P + P], kT[g * HD:g * HD + HD, b, 0:nk])
        for b in range(2):
            s = core.dve([t, free_of[f"S{unit % 2}"]], V.tensor_tensor_reduce, S[:, b0 + b, 0:nk],
                         bank[:, b * T:b * T + nk], mask, -(HD ** -0.5), 3e38, ADD, MIN, mx[:, b0 + b:b0 + b + 1])
        core.banks.release(slot, s)
        for b in range(2):
            s = core.f([s], S[:, b0 + b, 0:nk], S[:, b0 + b, 0:nk], ACT.Exp, bias=mx[:, b0 + b:b0 + b + 1], scale=-1.0,
                       accum_out=sums[:, qt, 1 + b, g * REP + i:g * REP + i + 1])
        return s

    def head_turned(qt, unit, i, g, ready):
        slot, bank, free = core.banks.take()
        for b in range(2):
            for kt in range(qt + 1):
                at = (b * (qt + 1) + kt) * P
                t = core.pe([ready, free], nc.tensor.transpose, bank[:, at:at + P],
                            S[:, 2 * (unit % 2) + b, kt * P:kt * P + P], ident)
        free_of[f"S{unit % 2}"] = t
        n = 2 * (qt + 1) * P
        s = core.copy([t, free_of[f"PT{unit % 3}"]], PT[:, unit % 3, 0:n], bank[:, 0:n])
        core.banks.release(slot, s)
        return s

    def head_values(qt, unit, i, g, ready):
        h = g * REP + i
        for b in range(2):
            for kt in range(qt + 1):
                at = (b * (qt + 1) + kt) * P
                t = core.matmul([ready, free_of["O"]], O[1 + b][:, h * HD:h * HD + HD], PT[:, unit % 3, at:at + P],
                                vr[:, 1 + b, kt, g * HD:g * HD + HD], start=kt == 0, stop=kt == qt)
        free_of[f"PT{unit % 3}"] = t
        return t

    def gated(qt, t):
        core.dve([core.act.last], V.reciprocal, coef[:], sums[:, qt])
        core.tt([], coef[:], coef[:], gates[:, qt, :].rearrange("p (h b) -> p b h", b=BRANCHES), MUL)
        for b in range(BRANCHES):
            dst, o = ((y if b == 0 else yt)[:, :], O[b][:, :])
            core.tt([t, free_of["y"]], *(ap.rearrange("p (h d) -> p h d", h=HEADS) for ap in (dst, o)),
                    wide(coef[:, b, :].unsqueeze(2), [P, HEADS, HD]), MUL)
            if b:
                core.tt([], y[:], y[:], yt[:], ADD)
        free_of["O"] = core.dve.last
        return core.tt([], y[:], y[:], zn[:, qt, :], MUL)

    def mixed(qt, ready):
        slot, bank, free = core.banks.take()
        for c in range(FT):
            t = core.pe([ready, free], nc.tensor.transpose, bank[:, c * P:c * P + P], y[:, c * P:c * P + P], ident)
        free_of["y"] = t
        s = core.dve([t], V.tensor_copy, mixT[:, 0:FT, qt * P:qt * P + P],
                     bank[:, :].rearrange("p (c t) -> p c t", c=FT))
        core.banks.release(slot, s)
        return s

    units = []
    for qt in range(NT):
        units += [(head_scores, head_turned, head_values, qt, i, g) for i in range(REP) for g in range(KV)]
        units.insert(len(units) - 2 * REP + 5, (compressed_scores, compressed_turned, compressed_values, qt))
    per_tile = len(units) // NT
    scored, copied = {}, {}
    lru_gate, conv_gate = feature_steps(gate_lru, 3), feature_steps(gate_conv)
    for step in (*lru_gate, lambda: compress(0), lambda: compress(1), compressed_keys_values):
        step()
    rest = {1: conv_gate[0], 2: conv_gate[1], 10: lambda: pointwise(0), 11: lambda: pointwise(2)}
    for step in range(len(units) + 2):
        if step < len(units):
            first, _, _, qt, *head = units[step]
            scored[step] = first(qt, step, *head)
        if step in rest:
            rest[step]()
        if 1 <= step <= len(units):
            _, second, _, qt, *head = units[step - 1]
            copied[step - 1] = second(qt, step - 1, *head, scored[step - 1])
        if step >= 2:
            _, _, third, qt, *head = units[step - 2]
            t = third(qt, step - 2, *head, copied[step - 2])
        if step == per_tile + 1:
            y_ready = gated(0, t)
        if step == per_tile + 3:
            mixed(0, y_ready)
    y_ready = gated(1, t)
    taken = [core.banks.take() for _ in range(3)]
    sums_out = [bank for _, bank, _ in taken] + [core.held[3]]
    free = [token for _, _, token in taken]
    summed = {}
    s = parts_ready[0]
    for i in (1, 2, 0):
        if i == 0:
            s = mixed(1, y_ready)
        view, landed = stream.next()
        steps = [(k, tt) for tt in range(NT) for k in range(4)]
        if i:
            steps = sorted(steps)
        for k, tt in steps:
            for n in range(2):
                t = core.matmul([s, landed, *free], sums_out[2 * tt + n][:, :], mixT[:, 4 * i + k, tt * P:tt * P + P],
                                view[:, k, n * 512:n * 512 + 512], start=i == 1 and k == 0,
                                stop=i == 0 and k == 3, mark=k == 3)
            summed[tt] = t
        stream.done(t)
    for tt in range(NT):
        for n in range(2):
            part = x[:, tt, n * 512:n * 512 + 512]
            s = core.tt([summed[tt]], part, sums_out[2 * tt + n][:, :], part, ADD)
    return s


def group_steps(core, w_stream, tokens, n_out, width, lhs, rhs, use, k_tiles):
    def step(o):
        view, landed = w_stream.next()
        slot, bank, free = core.banks.take()
        for k in range(k_tiles):
            a = lhs(view, o, k)
            t = core.matmul([landed, free, *tokens], bank[0:a.shape[-1], 0:width], a, rhs(view, o, k),
                            start=k == 0, stop=k == k_tiles - 1)
        core.banks.release(slot, use(o, bank, t))
        if o == n_out - 1:
            w_stream.done(t)

    return [lambda o=o: step(o) for o in range(n_out)]


def matmul_groups(*args):
    for step in group_steps(*args):
        step()


def turned(core, tokens, srcs, ident, rows=P):
    slot, bank, free = core.banks.take()
    for i, src in enumerate(srcs):
        n = src.shape[-1]
        t = core.pe([*tokens, free], core.nc.tensor.transpose, bank[0:n, i * P:i * P + rows], src,
                    ident[0:rows, 0:rows])
    return slot, bank, t


def second_block(core, A, K, x, out):
    with ExitStack() as outer:
        def keep(name, shape, dt=F32):
            return sb(core, outer, "second_" + name, shape, dt)

        gt2, h2 = keep("gt2", [P, D]), keep("h2", [P, NT, D])
        hT = keep("hT", [P, KT, 2 * T])
        with ExitStack() as stack:
            mixers(core, A, K, x, gt2, h2, hT, stack)
            core.restart()
        with ExitStack() as stack:
            experts(core, A, K, x, gt2, h2, hT, out, stack)


def mixers(core, A, K, x, gt2, h2, hT, stack):
    nc = core.nc
    V = nc.vector
    ident = K["ident"]

    def tile(name, shape, dt=F32):
        return sb(core, stack, "m_" + name, shape, dt)

    def rows_of(ap):
        return ap.rearrange("o (k p) n -> p (o k) n", p=P)

    R_C, R_CC, R_G1, R_G2, R_ADA, R_GCQ, R_GKV, R_GML, R_END = 0, 8, 16, 24, 32, 80, 82, 83, 87
    rows = tile("rows", [R_END, P])
    for r, name, k in ((R_C, "c_2", 8), (R_G1, "g_norm1_2", 8), (R_G2, "g_norm2_2", 8),
                       (R_ADA, "b_ada_2", 48), (R_GCQ, "g_cq_2", 2), (R_GKV, "g_ckv_2", 1),
                       (R_GML, "g_mlstm_2", 4)):
        core.load("m_rows", rows[r:r + k, :], A[name].rearrange("o (k p) -> (o k) p", p=P))
    core.load("m_rows", rows[R_CC:R_G1, :], A["c_ctx_2"].rearrange("(k p) -> k p", p=P))
    conv_rows = tile("conv_rows", [3, 512])
    rows_in = core.load("m_rows", conv_rows, A["conv_qk_2"].rearrange("o k c -> (o k) c"))
    gt1, fin_g = tile("gt1", [P, D]), tile("fin_g", [P, D])
    fin_in = core.load("fin_g", fin_g, A["final_g"].rearrange("(o n) -> o n", o=1).to_broadcast([P, D]))
    ring = core.ring([tile(f"w{i}", [P, 4096]) for i in range(3)])
    ada = lambda c: (rows_of(A["w_ada_2"][:, :, c * 512:c * 512 + 512]), KT, 512)
    w_in = lambda a, b: (rows_of(A["w_in_2"][:, :, a:b]), KT, b - a)
    stream = WeightStream(core, ring, [
        *(ada(c) for c in (0, 1, 2, 3)), w_in(0, B_QK), w_in(B_QK, B_V), w_in(B_G, B_G + 16),
        (rows_of(A["w_uq_2"]), 2, MLA_H * QK), (rows_of(A["w_ukv_2"]), 1, MLA_H * (NOPE + MLA_V)),
        w_in(B_V, B_O), w_in(B_O, B_G), *(ada(c) for c in range(4, 12)),
        *((rows_of(A["w_out_2"][:, i * 512:i * 512 + 512, :]), 4, D) for i in range(2))])
    ctx = tile("ctx", [P, NT, D])
    ctx_in = core.load("ctx", ctx, A["ctx_2"].rearrange("b (t p) d -> p (b t) d", p=P))
    b_if = tile("b_if", [P, 16])
    g_q, g_k = tile("g_q", [P, QK]), tile("g_k", [P, QK])
    core.load("m_small", b_if[:, 0:8], A["b_igate_2"].rearrange("o a b -> o (a b)").to_broadcast([P, 8]))
    core.load("m_small", b_if[:, 8:16], A["b_fgate_2"].rearrange("o a b -> o (a b)").to_broadcast([P, 8]))
    core.load("m_small", g_q, A["g_qn_2"].to_broadcast([P, QK]))
    core.load("m_small", g_k, A["g_kn_2"].to_broadcast([P, QK]))
    for dst, col in ((gt1, 2 * D), (gt2, 5 * D)):
        small_in = core.load("m_small", dst, A["b_ada_2"][:, col:col + D].to_broadcast([P, D]))

    vec = tile("vec", [P, R_END])
    convw = tile("convw", [P, 4, 3])
    slot, bank, t = turned(core, [rows_in], [rows], ident, R_END)
    core.banks.release(slot, core.dve([t], V.tensor_copy, vec, bank[:, 0:R_END]))
    slot, bank, t = turned(core, [rows_in], [conv_rows[:, c * P:c * P + P] for c in range(4)], ident, 3)
    vec_ready = core.dve([t], V.tensor_copy, convw, bank[:, :].rearrange("p (c r) -> p c r", c=4)[:, :, 0:3])
    core.banks.release(slot, vec_ready)

    small, sq = tile("small", [P, 64]), tile("sq", [P, D])
    for tt in range(NT):
        s = core.f([], sq, x[:, tt, :], ACT.Square, accum_out=small[:, tt:tt + 1])
    s = inv_rms(core, [s], small[:, 4:6], small[:, 0:2], D, small[:, 2:4])
    for tt in range(NT):
        x_ready = core.stt([s, fin_in], x[:, tt, :], x[:, tt, :], small[:, 4 + tt:5 + tt], fin_g, MUL, MUL)

    sT, cond = tile("sT", [P, KT, 2]), vec[:, 0:16].rearrange("p (a k) -> p k a", a=2)
    s = core.f([vec_ready], sT, cond, ACT.Sigmoid)
    core.tt([s], sT, sT, cond, MUL)
    s_ready = core.dve.last
    sums = core.ring([tile(f"sum{i}", [P, 512]) for i in range(2)])

    mod, mod_rows, rows_free = tile("mod", [P, 48, 2]), tile("mod_rows", [2, 512]), None

    def modulation(c):
        def use(o, bank, t):
            nonlocal rows_free
            s = core.act([t, rows_free], nc.scalar.copy, mod_rows, bank[0:2, :])
            slot, turn, free = core.banks.take()
            for n in range(4):
                t = core.pe([s, free], nc.tensor.transpose, turn[:, 2 * n:2 * n + 2], mod_rows[:, n * P:n * P + P],
                            ident[0:2, 0:2])
            rows_free = t
            bias = wide(vec[:, R_ADA + 4 * c:R_ADA + 4 * c + 4].unsqueeze(2), [P, 4, 2])
            core.banks.release(slot, core.tt([t], mod[:, 4 * c:4 * c + 4, :],
                                             turn[:, 0:8].rearrange("p (n a) -> p n a", a=2), bias, ADD))
            return s

        matmul_groups(core, stream, [s_ready], 1, 512, lambda v, o, k: sT[:, k, :], lambda v, o, k: v[:, k, :],
                      use, KT)
        return core.dve.last

    def weighted(o=None):
        view, landed = stream.next()
        slot, total, free = sums.take()
        add = lambda out, a, b: core.pool([], nc.gpsimd.tensor_tensor, out, a, b, ADD)
        core.pool([landed, s_ready], nc.gpsimd.tensor_tensor, view, view, wide(sT[:, :, 0:1], [P, KT, 512]), MUL)
        add(view[:, 0:4, :], view[:, 0:4, :], view[:, 4:8, :])
        add(view[:, 0:2, :], view[:, 0:2, :], view[:, 2:4, :])
        core.pool.wait(free)
        t = add(total, view[:, 0, :], view[:, 1, :])
        stream.done(t)
        totals.append((slot, total, t))

    totals = []

    def gate_row(dst, half):
        slot, total, ready = totals.pop(0)
        cols = slice(half * 512, half * 512 + 512)
        at, bank, free = core.banks.take()
        t = core.matmul([ready, free], bank[:, :], K["ones"], total)
        sums.release(slot, t)
        core.banks.release(at, core.tt([t, small_in], dst[:, cols], bank[:, :], dst[:, cols], ADD))

    def late_modulation(c):
        slot, total, ready = totals.pop(0)
        at, bank, free = core.banks.take()
        for n in range(4):
            t = core.matmul([ready, free], bank[:, n:n + 1], total[:, n * P:n * P + P], K["ones"][:, 0:1])
        sums.release(slot, t)
        core.banks.release(at, core.tt([t], mod[:, 4 * c:4 * c + 4, 0], bank[:, 0:4],
                                       vec[:, R_ADA + 4 * c:R_ADA + 4 * c + 4], ADD))

    late = [*(lambda h=h: gate_row(gt1, h) for h in range(2)), *(lambda c=c: late_modulation(c) for c in (6, 7, 8, 9)),
            *(lambda h=h: gate_row(gt2, h) for h in range(2))]

    def next_late():
        late.pop(0)()

    modulation(0)
    modulation(1)
    xn = h2
    normed(core, [ctx_in, core.dve.last], ctx, ctx, sq, small)
    core.act.wait(core.dve.last)
    normed(core, [x_ready], x, xn, sq, small)
    modulation(2)
    modulation(3)
    scale1, scale2 = tile("scale1", [P, 2, KT]), tile("scale2", [P, KT])
    for a in range(2):
        core.ts([], scale1[:, a, :], mod[:, 8:16, a], 1.0, ADD)
        s = core.tt([], scale1[:, a, :], scale1[:, a, :], vec[:, R_G1:R_G1 + 8], MUL)

    scaled_transposed(core, [s], ctx, hT, 0, scale1[:, 1, :], mod[:, 0:8, 1], ident)
    h_ready = scaled_transposed(core, [s], xn, hT, T, scale1[:, 0, :], mod[:, 0:8, 0], ident)
    TILES = 2 * NT

    cq, ckv = tile("cq", [P, NT, Q_RANK]), tile("ckv", [P, TILES, KV_RANK + ROPE2])
    v_ext = tile("v_ext", [P, TILES, ML_H, ML_V + 1])
    o_gate = tile("o_gate", [P, NT, ML_H * ML_V])
    gates = tile("gates", [P, TILES, 16])
    core.dve([], V.memset, v_ext[:, :, :, ML_V:ML_V + 1], 1.0)

    def token(tile_at):
        return lambda v, o, k: hT[:, k, (tile_at + o) * P:(tile_at + o) * P + P]

    def use_mla(o, bank, t):
        if o >= NT:
            core.dve([t], V.tensor_copy, cq[:, o - NT, :], bank[:, 0:Q_RANK])
        return core.dve([t], V.tensor_copy, ckv[:, o, :], bank[:, Q_RANK:B_QK])

    matmul_groups(core, stream, [h_ready], TILES, B_QK, token(0), lambda v, o, k: v[:, k, :], use_mla, KT)

    mixT = tile("mixT", [P, KT, T])
    whole, mla = tile, ExitStack()
    ml_tiles = {n: tile("ml_" + n, shape) for n, shape in (
        ("tmp", [P, 6, TILES, 8]), ("gcol", [P, 2, TILES, ML_H]), ("ecol", [P, NT, ML_H, 2]))}

    def tile(name, shape, dt=F32):
        return sb(core, mla, "mla_" + name, shape, dt)

    qnT, qrT = tile("qnT", [P, MLA_H, T]), tile("qrT", [ROPE2, MLA_H, T])
    knT, krT = tile("knT", [P, MLA_H, 2 * T]), tile("krT", [ROPE2, MLA_H, 2 * T])
    vm = tile("vm", [P, TILES, MLA_H, MLA_V])
    cqT, ckvT = tile("cqT", [P, 2, T]), tile("ckvT", [P, 2 * T])
    heads, sq4 = tile("heads", [P, MLA_H, QK]), tile("sq4", [P, MLA_H, QK])
    r1, r2 = tile("r1", [P, MLA_H, 2, 16]), tile("r2", [P, MLA_H, 2, 16])

    def rank_norm(src, n_tiles, width, at):
        sums, root, inv = (small[:, at + i * 4:at + i * 4 + n_tiles] for i in range(3))
        for i in range(n_tiles):
            s = core.f([core.dve.last], sq[:, 0:width], src[:, i, 0:width], ACT.Square, accum_out=sums[:, i:i + 1])
        s = inv_rms(core, [s], inv, sums, width, root)
        for i in range(n_tiles):
            s = core.ts([s], src[:, i, 0:width], src[:, i, 0:width], inv[:, i:i + 1], MUL)
        return s

    def rank_turned(ready, src, n_tiles, width, dst_of, g_row):
        for i in range(n_tiles):
            slot, bank, t = turned(core, [ready], [src[:, i, k * P:k * P + P] for k in range(width // P)], ident)
            for k in range(width // P):
                s = core.ts([t], dst_of(k, i), bank[:, k * P:k * P + P], vec[:, g_row + k:g_row + k + 1], MUL)
            core.banks.release(slot, s)
        return s

    rank_norm(cq, NT, Q_RANK, 0)
    ranks_ready = rank_norm(ckv, TILES, KV_RANK, 12)

    qk_lat, k_ctx = tile("qk_lat", [P, 4, T + 2]), tile("k_ctx", [P, 2, T + 2])
    core.dve([], V.memset, qk_lat, 0.0)
    pads = core.dve([], V.memset, k_ctx, 0.0)

    def use_qk(o, bank, t):
        if o < 4:
            return core.dve([t], V.tensor_copy, qk_lat[:, o, 1:T + 1], bank[:, 0:T])
        return core.dve([t], V.tensor_copy, k_ctx[:, o - 4, 1:T + 1], bank[:, 0:T])

    matmul_groups(core, stream, [h_ready], 6, T,
                  lambda v, o, k: v[:, k, (o if o < 4 else o - 2) * P:(o if o < 4 else o - 2) * P + P],
                  lambda v, o, k: hT[:, k, T:2 * T] if o < 4 else hT[:, k, 0:T], use_qk, KT)
    matmul_groups(core, stream, [h_ready], TILES, 16, token(0), lambda v, o, k: v[:, k, :],
                  lambda o, bank, t: core.tt([t, small_in], gates[:, o, :], bank[:, 0:16], b_if, ADD), KT)

    rank_turned(ranks_ready, cq, NT, Q_RANK, lambda k, i: cqT[:, k, i * P:i * P + P], R_GCQ)
    cq_ready = rank_turned(ranks_ready, ckv, TILES, KV_RANK, lambda k, i: ckvT[:, i * P:i * P + P], R_GKV)

    def head_norm(ready, heads, g, rope_tile):
        for h in range(MLA_H):
            s = core.f([ready], sq4[:, h, :], heads[:, h, :], ACT.Square, accum_out=small[:, 24 + h:25 + h])
        s = inv_rms(core, [s], small[:, 32:36], small[:, 24:28], QK, small[:, 28:32])
        core.tt([s, small_in], heads, heads, wide(small[:, 32:36].unsqueeze(2), [P, MLA_H, QK]), MUL)
        core.tt([], heads, heads, wide(g.unsqueeze(1), [P, MLA_H, QK]), MUL)
        if rope_tile is not None:
            r = heads[:, :, NOPE:QK].rearrange("p h (a e d) -> p h a e d", a=2, e=2)
            a, b = r[:, :, :, 0, :], r[:, :, :, 1, :]
            shape = [P, MLA_H, 2, 16]
            c, n = (wide(K[name][:, rope_tile * 32:rope_tile * 32 + 32].rearrange("p (a d) -> p a d", a=2)
                         .unsqueeze(1), shape) for name in ("cos2", "sin2"))
            core.tt([], r1, a, n, MUL)
            core.tt([], r2, b, n, MUL)
            core.tt([], a, a, c, MUL)
            core.tt([], a, a, r2, SUB)
            core.tt([], b, b, c, MUL)
            core.tt([], b, b, r1, ADD)
        return core.dve.last

    def heads_turned(ready, heads, dstn, dstr, col):
        slot, bank, t = turned(core, [ready], [heads[:, h, 0:NOPE] for h in range(MLA_H)], ident)
        s = core.copy([t], dstn[:, :, col:col + P], bank[:, :].rearrange("p (h t) -> p h t", h=MLA_H))
        core.banks.release(slot, s)
        slot, bank, t = turned(core, [], [heads[:, h, NOPE:QK] for h in range(MLA_H)], ident)
        s = core.copy([t], dstr[:, :, col:col + P], bank[0:ROPE2, :].rearrange("p (h t) -> p h t", h=MLA_H))
        core.banks.release(slot, s)
        return t

    w_uq, w_ukv = stream.hold(), stream.hold()
    values = group_steps(core, stream, [h_ready], TILES, 512, token(0), lambda v, o, k: v[:, k, :],
                         lambda o, bank, t: core.f([t], v_ext[:, o, :, 0:ML_V],
                                                   bank[:, :].rearrange("p (h d) -> p h d", h=ML_H), ACT.Copy), KT)
    output_gates = group_steps(core, stream, [h_ready], NT, 512, token(NT), lambda v, o, k: v[:, k, :],
                               lambda o, bank, t: core.f([t], o_gate[:, o, :], bank[:, :], ACT.Sigmoid), KT)
    fill = [values[0:1], values[1:3], values[3:4], output_gates[0:1], [], [output_gates[1], weighted, weighted]]

    def queries(i, heads, free_heads):
        _, view, landed = w_uq
        for half in range(2):
            slot, bank, free = core.banks.take()
            for k in range(2):
                t = core.matmul([landed, cq_ready, free], bank[:, 0:2 * QK], cqT[:, k, i * P:i * P + P],
                                view[:, k, half * 2 * QK:half * 2 * QK + 2 * QK], start=k == 0, stop=k == 1)
            s = core.act([t, free_heads], nc.scalar.copy, heads[:, 2 * half:2 * half + 2, :],
                         bank[:, 0:2 * QK].rearrange("p (h d) -> p h d", h=2))
            core.banks.release(slot, s)
        if i == NT - 1:
            stream.drop(w_uq, t)
        return s

    def keys_values(i, heads, free_heads):
        _, view, landed = w_ukv
        for half in range(2):
            slot, bank, free = core.banks.take()
            t = core.matmul([landed, cq_ready, free], bank[:, :], ckvT[:, i * P:i * P + P],
                            view[:, 0, half * 512:half * 512 + 512])
            b4 = bank[:, :].rearrange("p (h e d) -> p h e d", h=2, e=2)
            core.act([t, free_heads], nc.scalar.copy, heads[:, 2 * half:2 * half + 2, 0:NOPE], b4[:, :, 0, :])
            s = core.act([], nc.scalar.copy, vm[:, i, 2 * half:2 * half + 2, :], b4[:, :, 1, :])
            core.banks.release(slot, s)
        if i == TILES - 1:
            stream.drop(w_ukv, t)
        return core.act([core.dve.last], nc.scalar.copy, heads[:, :, NOPE:QK],
                        wide(ckv[:, i, KV_RANK:KV_RANK + ROPE2].unsqueeze(1), [P, MLA_H, ROPE2]))

    both = [heads, ctx[:, 0, 0:MLA_H * QK].rearrange("p (h d) -> p h d", h=MLA_H)]
    work = [(queries, g_q, i, qnT, qrT, i) for i in range(NT)] + [
        (keys_values, g_k, i - NT if i >= NT else None, knT, krT, i) for i in range(TILES)]
    heads_free, normed_at = [None, None], None
    for n in range(len(work) + 1):
        if n < len(work):
            product, g, rope_tile, _, _, i = work[n]
            ready = product(i, both[n % 2], heads_free[n % 2])
        if n:
            _, _, _, dstn, dstr, i = work[n - 1]
            heads_free[(n - 1) % 2] = heads_turned(normed_at, both[(n - 1) % 2], dstn, dstr, i * P)
        if n < len(work):
            normed_at = head_norm(ready, both[n % 2], g, rope_tile)
            for step in fill[n]:
                step()
    k_ready = [core.dve.last, core.act.last]

    p_sb, PT = (ctx[:, i, :].rearrange("p (b c) -> p b c", b=2) for i in range(2))
    att, den = tile("att", [P, NT, 512]), tile("den", [P, NT, MLA_H])
    scale = QK ** -0.5
    prepare, ml = mlstm_prepare(core, K, ml_tiles, convw, qk_lat, k_ctx, pads, gates, h2, hT, sq, ident)
    core.dve.wait(core.pe.last)
    p_free, pt_free, max_free = [None] * 2, [None] * 2, [None] * 2

    def attend(n):
        tt, h = divmod(n, MLA_H)
        q = slice(tt * P, tt * P + P)
        slot, bank, free = core.banks.take()
        core.matmul([k_ready, free], bank[:, :], qnT[:, h, q], knT[:, h, :], start=True, stop=False)
        t = core.matmul([], bank[:, :], qrT[:, h, q], krT[:, h, :], start=False, stop=True)
        m = small[:, 40 + 2 * (n % 2):42 + 2 * (n % 2)]
        core.dve([t, max_free[n % 2]], V.tensor_reduce, m[:, 0:1], bank[:, :], AX.X, MAX)
        s = core.ts([], m[:, 1:2], m[:, 0:1], -scale, MUL)
        s = core.f([s, p_free[n % 2]], p_sb[:, n % 2, :], bank[:, :], ACT.Exp, bias=m[:, 1:2], scale=scale,
                   accum_out=den[:, tt, h:h + 1])
        max_free[n % 2] = s
        core.banks.release(slot, s)
        return s

    def attended(n, ready):
        tt, h = divmod(n, MLA_H)
        slot, bank, t = turned(core, [ready], [p_sb[:, n % 2, c * P:c * P + P] for c in range(TILES)], ident)
        p_free[n % 2] = t
        s = core.act([t, pt_free[n % 2]], nc.scalar.copy, PT[:, n % 2, :], bank[:, :])
        core.banks.release(slot, s)
        for c in range(TILES):
            t = core.matmul([s], core.held[tt][:, h * P:h * P + P], PT[:, n % 2, c * P:c * P + P], vm[:, c, h, :],
                            start=c == 0, stop=c == TILES - 1)
        pt_free[n % 2] = t
        return t

    def attention_out(tt, ready):
        core.dve([core.act.last], V.reciprocal, den[:, tt, :], den[:, tt, :])
        s = core.tt([ready], att[:, tt, :].rearrange("p (h d) -> p h d", h=MLA_H),
                    core.held[tt][:, :].rearrange("p (h d) -> p h d", h=MLA_H),
                    wide(den[:, tt, :].unsqueeze(2), [P, MLA_H, MLA_V]), MUL)
        slot, bank, t = turned(core, [s], [att[:, tt, c * P:c * P + P] for c in range(4)], ident)
        s = core.dve([t], V.tensor_copy, mixT[:, 0:4, tt * P:tt * P + P], bank[:, :].rearrange("p (c t) -> p c t", c=4))
        core.banks.release(slot, s)

    heads_all = NT * MLA_H
    ready = attend(0)
    for n in range(heads_all):
        following = attend(n + 1) if n + 1 < heads_all else None
        if n % 2 == 0:
            next_late()
            weighted()
        for step in prepare[n]:
            step()
        t = attended(n, ready)
        ready = following
        if n % MLA_H == MLA_H - 1:
            attention_out(n // MLA_H, t)
    assert len(prepare) == heads_all
    mla.close()
    core.meet()
    def mix_out(i, tt, ready):
        view, landed = stream.next()
        for k in range(4):
            for h in range(2):
                t = core.matmul([ready, landed], core.held[2 * tt + h][:, :], mixT[:, 4 * i + k, tt * P:tt * P + P],
                                view[:, k, h * 512:h * 512 + 512], start=i + k == 0,
                                stop=i == 1 and k == 3, mark=k == 3)
        mixed[tt] = t
        if tt == NT - 1:
            stream.done(t)

    mixed = {}
    fill = [[], [next_late, weighted], [], [next_late, weighted], [], [next_late], [next_late],
            [lambda tt=tt: mix_out(0, tt, core.dve.last) for tt in range(NT)]]
    with ExitStack() as own:
        mlstm(core, K, lambda n, shape, dt=F32: sb(core, own, n, shape, dt), ml, fill, vec, R_GML, v_ext, o_gate,
              mixT, small, ident, lambda tt, ready: mix_out(1, tt, ready))
    tile = whole
    core.ts([], scale2, mod[:, 32:40, 0], 1.0, ADD)
    core.tt([], scale2, scale2, vec[:, R_G2:R_G2 + 8], MUL)

    for tt in range(NT):
        for h in range(2):
            c = slice(h * 512, h * 512 + 512)
            core.tt([mixed[tt]], xn[:, tt, c], core.held[2 * tt + h][:, :], gt1[:, c], MUL)
            s = core.tt([], x[:, tt, c], x[:, tt, c], xn[:, tt, c], ADD)
        s = normed(core, [s], x, xn, sq, small, [tt])
    scaled_transposed(core, [s], xn, hT, 0, scale2, mod[:, 24:32, 0], ident)
    core.rings.remove(ring)
    core.rings.remove(sums)


def mlstm_prepare(core, K, tiles, convw, qk_lat, k_ctx, pads, gates, rows_at, sums_at, sq, ident):
    nc = core.nc
    V = nc.vector
    ST = 2 * NT
    tmp, gcol, ecol = (tiles[n] for n in ("tmp", "gcol", "ecol"))
    rows = rows_at.rearrange("p t d -> p (t d)")[0:ML_H, :].rearrange("p (a s) -> p a s", a=4)
    E = rows[:, 2:4, :]
    flat = sums_at.rearrange("p k t -> p (k t)")
    F, G, M = (flat[0:ML_H, i * 4 * T:(i + 1) * 4 * T].rearrange("p (a s) -> p a s", a=2) for i in range(3))
    kT = flat[:, 12 * T:16 * T].rearrange("p (c s) -> p c s", c=2)
    raw, sig = sq[:, 0:T], sq[:, T:2 * T]
    qT = sq[:, 2 * T:4 * T].rearrange("p (c s) -> p c s", c=2)
    st = {"qT": qT, "kT": kT, "M": M, "gcol": gcol, "ecol": ecol}

    def convolve(c):
        src = qk_lat[:, c, :] if c < 4 else k_ctx[:, c - 4, :]
        wc = c if c < 4 else c - 2
        core.ts([pads], raw, src[:, 0:T], convw[:, wc, 0:1], MUL)
        core.stt([], raw, src[:, 1:T + 1], convw[:, wc, 1:2], raw, MUL, ADD)
        st["raw_ready"] = core.stt([], raw, src[:, 2:T + 2], convw[:, wc, 2:3], raw, MUL, ADD)

    def silu(c):
        core.f([st["raw_ready"]], sig, raw, ACT.Sigmoid)
        if c < 2:
            core.stt([core.act.last], qT[:, c, :], raw, ML_QK ** -0.5, sig, MUL, MUL)
        else:
            at = T if c < 4 else 0
            core.tt([core.act.last], kT[:, c - 2 if c < 4 else c - 4, at:at + T], raw, sig, MUL)
        st["qk_ready"] = core.dve.last

    f = gates[:, :, 8:16]

    def log_gates():
        st["abs_ready"] = core.stt([], tmp[:, 0], f, -1.0, f, MUL, MAX)

    def log_gates_end():
        core.f([st["abs_ready"]], tmp[:, 1], tmp[:, 0], ACT.Exp, scale=-1.0)
        log1p_unit(core, [core.act.last], tmp[:, 2], tmp[:, 1], tmp[:, 3], tmp[:, 4], tmp[:, 5])
        core.ts([], f, f, 0.0, MIN)
        st["gates_ready"] = core.tt([], f, f, tmp[:, 2], SUB)

    def gates_turned(td):
        slot, bank, t = turned(core, [st["gates_ready"]], [gates[:, i, td * 4:td * 4 + 4] for i in range(ST)], ident)
        core.banks.release(slot, core.dve([t], V.tensor_copy, rows[:, td, :], bank[0:ML_H, :]))

    one = wide(K["ones"][0:ML_H, 0:1], [ML_H, T])

    def sums(d):
        def order(ap, part):
            a, b = part * T, part * T + T
            if d == 0:
                return ap[:, a:b]
            return ap[:, a:b][:, ::-1]

        def last(ap, part):
            at = part * T + (T - 1 if d == 0 else 0)
            return ap[:, at:at + 1]

        fd, idd = rows[:, 2 + d, :], rows[:, d, :]
        core.dve([], V.tensor_tensor_scan, order(F[:, d, :], 0), one, order(fd, 0), 0.0, MUL, ADD)
        core.dve([], V.tensor_tensor_scan, order(F[:, d, :], 1), one, order(fd, 1), last(F[:, d, :], 0), MUL, ADD)
        core.tt([], G[:, d, :], idd, F[:, d, :], SUB)
        g = G[:, d, :]
        core.dve([], V.tensor_tensor_scan, order(M[:, d, :], 0), order(g, 0), order(g, 0), 0.0, MAX, MAX)
        core.dve([], V.tensor_tensor_scan, order(M[:, d, :], 1), order(g, 1), order(g, 1), last(M[:, d, :], 0),
                 MAX, MAX)

    def stabilisers():
        st["m_ready"] = core.tt([], E, F, M, ADD)

    def stabilisers_end():
        st["rows_ready"] = core.f([st["m_ready"]], E, E, ACT.Exp, scale=-1.0)

    def columns(d):
        slot, bank, free = core.banks.take()
        for i in range(ST):
            t = core.pe([st["rows_ready"], free], nc.tensor.transpose, bank[:, i * 4:i * 4 + 4],
                        G[:, d, i * P:i * P + P], ident[0:ML_H, 0:ML_H])
        for i in range(NT):
            t = core.pe([], nc.tensor.transpose, bank[:, 16 + i * 4:20 + i * 4],
                        E[:, d, T + i * P:T + i * P + P], ident[0:ML_H, 0:ML_H])
        core.dve([t], V.tensor_copy, gcol[:, d], bank[:, 0:16].rearrange("p (i h) -> p i h", h=ML_H))
        s = core.dve([], V.tensor_copy, ecol[:, :, :, d], bank[:, 16:24].rearrange("p (i h) -> p i h", h=ML_H))
        core.banks.release(slot, s)
        st["cols_ready"] = s

    conv, silu_of = ([lambda c=c, step=step: step(c) for c in range(6)] for step in (convolve, silu))
    groups = [
        [log_gates, conv[0]],
        [log_gates_end, silu_of[0], conv[1]],
        [*(lambda td=td: gates_turned(td) for td in range(4)), silu_of[1], conv[2]],
        [silu_of[2], lambda: sums(0)],
        [lambda: sums(1), stabilisers],
        [stabilisers_end, conv[3]],
        [silu_of[3], conv[4], lambda: columns(0)],
        [silu_of[4], conv[5], lambda: columns(1), silu_of[5]]]
    return groups, st


def mlstm(core, K, tile, st, fill, vec, g_row, v_ext, o_gate, mixT, small, ident, use):
    nc = core.nc
    V = nc.vector
    ST = 2 * NT
    qT, kT, M, gcol, ecol = (st[n] for n in ("qT", "kT", "M", "gcol", "ecol"))
    nm, nmm = tile("ml_nm", [P, 2, NT, P]), tile("ml_nmm", [P, 2, NT, P])
    W = tile("ml_W", [P, 2, ST, T])
    hn = tile("ml_hn", [P, NT, ML_H, 2, ML_V + 1])
    w_free, score_free, level_free = [None] * 2, [None] * 2, [None] * 2
    whole_pair = [(2, 1), (3, 0)]

    def products(h):
        half = slice((h % 2) * ML_QK, (h % 2) * ML_QK + ML_QK)
        for part in range(2):
            bank = core.held[2 * (h % 2) + part]
            for e in range(2):
                at = (2 * part + e) * P
                t = core.matmul([st["qk_ready"], score_free[h % 2]], bank[:, e * T:e * T + T],
                                kT[half, h // 2, at:at + P], qT[half, h // 2, :])
        return t

    def levels(n):
        (h, d), b = divmod(n, 2), n % 2
        slot, bank, free = core.banks.take()
        t = core.matmul([st["rows_ready"], free], bank[:, 0:T], K["select"][0:ML_H, h * P:h * P + P], M[:, d, T:2 * T])
        s = core.ts([t, level_free[b]], nm[:, b], bank[:, 0:T].rearrange("p (i t) -> p i t", i=NT), -1.0, MUL)
        core.banks.release(slot, s)
        mask = K["upper"] if d == 0 else K["lower"]
        return core.tt([], nmm[:, b], nm[:, b], wide(mask.unsqueeze(1), [P, NT, P]), ADD)

    def decays(n, levels_ready):
        (h, d), b = divmod(n, 2), n % 2
        flat = nm[:, b].rearrange("p i t -> p (i t)")
        for e in range(2):
            core.f([levels_ready, st["cols_ready"], w_free[b]], W[:, b, e, :], flat, ACT.Exp,
                   bias=gcol[:, d, e, h:h + 1])
        for i in range(NT):
            core.f([], W[:, b, 2 + i, i * P:i * P + P], nmm[:, b, i, :], ACT.Exp, bias=gcol[:, d, 2 + i, h:h + 1])
        src, dst = whole_pair[d]
        level_free[b] = core.f([], W[:, b, src, dst * P:dst * P + P], nm[:, b, dst, :], ACT.Exp,
                               bias=gcol[:, d, src, h:h + 1])
        return level_free[b]

    def outputs(n, decays_ready, scores_ready):
        (h, d), b = divmod(n, 2), n % 2
        score = [core.held[2 * (h % 2) + part] for part in range(2)]
        core.tt([decays_ready, scores_ready], W[:, b, 0:2, :], W[:, b, 0:2, :],
                score[0][:, :].rearrange("p (e t) -> p e t", e=2), MUL)
        pairs = [(2, 0), (3, 1), whole_pair[d]]
        for src, i in pairs:
            c = slice(i * P, i * P + P)
            s = core.tt([], W[:, b, src, c], W[:, b, src, c],
                        score[1][:, (src - 2) * T + i * P:(src - 2) * T + i * P + P], MUL)
        if d == 1:
            score_free[h % 2] = s
        slot, bank, free = core.banks.take()
        for i in range(NT):
            use = [0, 1] + [src for src, j in sorted(pairs) if j == i]
            for src in use:
                t = core.matmul([s, free], bank[:, i * (ML_V + 1):(i + 1) * (ML_V + 1)], W[:, b, src, i * P:i * P + P],
                                v_ext[:, src, h, :], start=src == use[0], stop=src == use[-1])
        w_free[b] = t
        s = core.act([t], nc.scalar.copy, hn[:, :, h, d, :],
                     bank[:, 0:NT * (ML_V + 1)].rearrange("p (i v) -> p i v", i=NT))
        core.banks.release(slot, s)

    count = 2 * ML_H
    scores_ready = {0: products(0)}
    levels_ready = [levels(n) for n in range(2)]
    ready = decays(0, levels_ready[0])
    for n in range(count):
        if n % 2 and n + 1 < count:
            scores_ready[n // 2 + 1] = products(n // 2 + 1)
        if n + 2 < count:
            levels_ready.append(levels(n + 2))
        following = decays(n + 1, levels_ready[n + 1]) if n + 1 < count else None
        if n < count - 1:
            for step in fill[n]:
                step()
        outputs(n, ready, scores_ready[n // 2])
        ready = following
    for step in fill[-1]:
        step()

    den = tile("ml_den", [P, NT, ML_H, 2])
    hs, ht = (W[:, b].rearrange("p s t -> p (s t)").rearrange("p (i h v) -> p i h v", h=ML_H, v=ML_V) for b in range(2))
    shape = [P, ML_H, ML_V]
    core.dve.wait(core.act.last, core.pe.last)
    for i in range(NT):
        num, raw_den, d, a, b = hn[:, i], hn[:, i, :, :, ML_V], den[:, i], hs[:, i], ht[:, i]
        at = slice(i * ML_H, i * ML_H + ML_H)
        sums, root, inv = small[:, 0:8][:, at], small[:, 8:16][:, at], small[:, 16:24][:, at]
        core.stt([], d, raw_den, -1.0, raw_den, MUL, MAX)
        core.tt([], d, d, ecol[:, i], MAX)
        core.dve([], V.reciprocal, d, d)
        core.tt([], a, num[:, :, 0, 0:ML_V], wide(d[:, :, 0:1], shape), MUL)
        core.tt([], b, num[:, :, 1, 0:ML_V], wide(d[:, :, 1:2], shape), MUL)
        core.tt([], a, a, b, ADD)
        core.tt([], b, a, a, MUL)
        core.dve([], V.tensor_reduce, sums, b, AX.X, ADD)
        s = inv_rms(core, [], inv, sums, ML_V, root)
        core.tt([s], a, a, wide(inv.unsqueeze(2), shape), MUL)
        s = core.tt([], a, a, o_gate[:, i].rearrange("p (h v) -> p h v", h=ML_H), MUL)
        if i:
            use(i - 1, outputs_ready)
        slot, bank, t = turned(core, [s], [a[:, h, :] for h in range(ML_H)], ident)
        for h in range(ML_H):
            outputs_ready = core.ts([t], mixT[:, 4 + h, i * P:i * P + P], bank[:, h * P:h * P + P],
                        vec[:, g_row + h:g_row + h + 1], MUL)
        core.banks.release(slot, outputs_ready)
    use(NT - 1, outputs_ready)


def experts(core, A, K, x, gt2, h2, hT, out, stack):
    nc = core.nc
    V = nc.vector
    ident = K["ident"]
    BUFS, BATCH = TOPK, 4
    BATCHES = NT * TOPK // BATCH

    def tile(name, shape, dt=F32):
        return sb(core, stack, "e_" + name, shape, dt)

    rows_uv = [tile(f"uv{j}", [P, 2 * D]) for j in range(BUFS)]
    idx = [tile(f"idx{j}", [P, 1], U32) for j in range(BUFS)]
    diag = [tile(f"diag{j}", [P, P]) for j in range(BUFS)]
    dot, act, w = tile("dot", [P, BUFS]), tile("act", [P, BUFS]), tile("w", [P, BUFS])
    chosen, weight = tile("chosen", [P, NT, SLOTS], U32), tile("weight", [P, NT, SLOTS])
    w_pq, keys, keysT = tile("w_pq", [P, KT, 2 * P]), tile("keys", [P, 2, P]), tile("keysT", [P, 2, P])
    qT, scores = tile("qT", [P, 2, T]), tile("scores", [P, NT, 2, N_KEYS])
    rest = tile("rest", [P, TOPK * TOPK])
    sv, si, sif = tile("sv", [P, NT, 2, TOPK]), tile("si", [P, NT, 2, TOPK], U32), tile("sif", [P, NT, 2, TOPK])
    cand, hot = tile("cand", [P, NT, TOPK * TOPK]), tile("hot", [P, NT, TOPK, TOPK])
    best, pos = tile("best", [P, NT, TOPK]), tile("pos", [P, NT, TOPK], U32)
    part, partf, e01 = tile("part", [P, NT, TOPK], U32), tile("partf", [P, NT, TOPK]), tile("e01", [P, 2, NT, TOPK])
    gap, norm = tile("gap", [P, NT, TOPK]), tile("norm", [P, NT])

    sem = nc.alloc_semaphore
    landed, free = ([sem(f"{name}{j}") for j in range(BUFS)] for name in ("uv_in", "uv_free"))
    idx_set = [sem(f"idx_set{j}") for j in range(BUFS)]
    seen, dots_done, gelu_done, diags_done = (
        sem(n) for n in ("indices_seen", "dots_done", "gelu_done", "diags_done"))
    (w_in, keys_in, keys_turned, queries_done, scores_done, keysT_set, qT_set, scores_set, scores_seen,
     best_set, exp_set, routed) = (
        sem(n) for n in ("w_pq_in", "keys_in", "keys_turned", "queries_done", "scores_done", "keysT_set",
                         "qT_set", "scores_set", "scores_seen", "best_set", "exp_set", "routed"))
    steps = Lane(nc, nc.vector, "steps", True)
    acc = [core.held[0:2], core.held[2:4]]
    bank_k, bank_q, bank_s = core.banks.items[0:3]
    table = A["experts"]

    def after(engine, sem, heads):
        if not isinstance(heads, int) or heads > 0:
            engine.wait_ge(sem, heads)

    def load_head(head):
        w_cols = A["w_pq_2"][:, :, bass.ds(head * 2 * P, 2 * P)]
        after(nc.sync, keys_turned, head)
        keys_of = A["sub_keys_2"][:, bass.ds(head, 1)]
        nc.sync.dma_start(keys, keys_of.rearrange("o h a k d -> k (o h a) d")).then_inc(keys_in, 16)
        after(nc.sync, queries_done, head)
        nc.sync.dma_start(w_pq, w_cols.rearrange("o (k p) n -> p (o k) n", p=P)).then_inc(w_in, 16)

    def product_keys(head):
        def keys_step():
            nc.tensor.wait_ge(keys_in, head * 16 + 16)
            for a in range(2):
                t = nc.tensor.transpose(bank_k[:, a * P:a * P + P], keys[:, a, :], ident)
            t.then_inc(keys_turned, 1)
            nc.scalar.wait_ge(keys_turned, head + 1)
            nc.scalar.copy(keysT, bank_k[:, 0:2 * P].rearrange("p (a k) -> p a k", a=2)).then_inc(keysT_set, 1)
            nc.tensor.wait_ge(w_in, head * 16 + 16)
            queries(0)

        def queries(a):
            for k in range(KT):
                t = nc.tensor.matmul(bank_q[:, a * T:a * T + T], w_pq[:, k, a * P:a * P + P], hT[:, k, 0:T],
                                     start=k == 0, stop=k == KT - 1)
            return t

        def queries_step():
            queries(1).then_inc(queries_done, 1)
            nc.scalar.wait_ge(queries_done, head + 1)
            nc.scalar.copy(qT, bank_q[:, :].rearrange("p (a t) -> p a t", a=2)).then_inc(qT_set, 1)

        def scores_step():
            nc.tensor.wait_ge(keysT_set, head + 1)
            nc.tensor.wait_ge(qT_set, head + 1)
            for tt in range(NT):
                for a in range(2):
                    t = nc.tensor.matmul(bank_s[:, (2 * tt + a) * P:(2 * tt + a) * P + P],
                                         qT[:, a, tt * P:tt * P + P], keysT[:, a, :], start=True, stop=True)
            t.then_inc(scores_done, 1)
            nc.scalar.wait_ge(scores_done, head + 1)
            after(nc.scalar, routed, head * NT)
            nc.scalar.copy(scores, bank_s[:, :].rearrange("p (t a k) -> p t a k", t=NT, a=2)).then_inc(scores_set, 1)

        return [keys_step, queries_step, scores_step]

    def top16(values, scratch, out_v, out_i):
        steps([], V.max, out_v[:, 0:8], values)
        steps([], V.max_index, out_i[:, 0:8], out_v[:, 0:8], values)
        steps([], V.match_replace, scratch, out_v[:, 0:8], values, -3e38)
        steps([], V.max, out_v[:, 8:16], scratch)
        steps([], V.max_index, out_i[:, 8:16], out_v[:, 8:16], scratch)

    def route(head):
        shape = [P, TOPK, TOPK]
        col = bass.ds(head * TOPK, TOPK)

        def halves(tt):
            if tt == 0:
                nc.vector.wait_ge(scores_set, head + 1)
                nc.vector.sem_inc(scores_seen, 1)
            for a in range(2):
                top16(scores[:, tt, a, :], rest[:, 0:N_KEYS], sv[:, tt, a, :], si[:, tt, a, :])

        def candidates(tt):
            steps([], V.tensor_copy, sif[:, tt], si[:, tt])
            steps([], V.tensor_tensor, cand[:, tt].rearrange("p (i j) -> p i j", i=TOPK),
                  wide(sv[:, tt, 0, :].unsqueeze(2), shape), wide(sv[:, tt, 1, :].unsqueeze(1), shape), ADD)
            top16(cand[:, tt, :], rest, best[:, tt, :], pos[:, tt, :])
            steps([], V.tensor_tensor, gap[:, tt], best[:, tt], wide(best[:, tt, 0:1], [P, TOPK]), SUB)
            nc.vector.wait_ge(*steps.last)
            nc.vector.sem_inc(best_set, 1)
            nc.scalar.wait_ge(best_set, head * NT + (tt + 1))
            nc.scalar.activation(best[:, tt], gap[:, tt], ACT.Exp).then_inc(exp_set, 1)

        def places(tt):
            for a, (op, by) in enumerate(((ALU.logical_shift_right, 4), (ALU.bitwise_and, 15))):
                steps([], V.tensor_scalar, part[:, tt], pos[:, tt], by, None, op)
                steps([], V.tensor_copy, partf[:, tt], part[:, tt])
                steps([], V.tensor_tensor, hot[:, tt], wide(partf[:, tt].unsqueeze(2), shape),
                      wide(K["iota"].unsqueeze(1), shape), ALU.is_equal)
                steps([], V.tensor_tensor, hot[:, tt], hot[:, tt], wide(sif[:, tt, a, :].unsqueeze(1), shape), MUL)
                steps([], V.tensor_reduce, e01[:, a, tt], hot[:, tt], AX.X, ADD)
            steps([], V.scalar_tensor_tensor, e01[:, 0, tt], e01[:, 0, tt], float(N_KEYS), e01[:, 1, tt], MUL, ADD)
            steps([], V.tensor_copy, chosen[:, tt, col], e01[:, 0, tt])
            nc.vector.wait_ge(exp_set, head * NT + (tt + 1))
            steps([], V.tensor_reduce, norm[:, tt:tt + 1], best[:, tt], AX.X, ADD)
            steps([], V.reciprocal, norm[:, tt:tt + 1], norm[:, tt:tt + 1])
            steps([], V.tensor_scalar, weight[:, tt, col], best[:, tt], norm[:, tt:tt + 1], None, MUL)
            nc.vector.wait_ge(*steps.last)
            nc.vector.sem_inc(routed, 1)

        return [lambda step=step, tt=tt: step(tt) for tt in range(NT) for step in (halves, candidates, places)]

    def rewind():
        nc.vector.wait_ge(*steps.last)
        nc.vector.sem_clear(steps.sem)
        steps.clear()

    def gather(turn):
        for n in range(NT * TOPK):
            tt, j = divmod(n, BUFS)
            if j == 0:
                nc.gpsimd.wait_ge(routed, turn * NT + (tt + 1))
            use = turn * NT + tt
            nc.gpsimd.wait_ge(free[j], use + 1)
            nc.gpsimd.tensor_copy(idx[j], chosen[:, tt, bass.ds(turn * TOPK + j, 1)]).then_inc(idx_set[j], 1)
            nc.gpsimd.wait_ge(idx_set[j], use + 1)
            nc.gpsimd.sem_inc(seen, 1)
            nc.gpsimd.indirect_dma_start(out=rows_uv[j], out_offset=None, in_=table,
                                         in_offset=bass.IndirectOffsetOnAxis(ap=idx[j], axis=0)).then_inc(landed[j], 16)

    def dots(turn, b):
        tt, j0 = divmod(b * BATCH, BUFS)
        for j in range(j0, j0 + BATCH):
            nc.vector.wait_ge(landed[j], turn * 32 + (tt * 16 + 16))
            u = rows_uv[j][:, 0:D]
            ins = nc.vector.tensor_tensor_reduce(u, u, h2[:, tt, :], 1.0, 0.0, MUL, ADD, dot[:, j:j + 1])
        ins.then_inc(dots_done, 1)
        nc.scalar.wait_ge(dots_done, turn * BATCHES + (b + 1))
        nc.scalar.activation(act[:, j0:j0 + BATCH], dot[:, j0:j0 + BATCH], ACT.Gelu).then_inc(gelu_done, 1)

    def add(turn, b):
        tt, j0 = divmod(b * BATCH, BUFS)
        cols = slice(j0, j0 + BATCH)
        nc.vector.wait_ge(gelu_done, turn * BATCHES + (b + 1))
        steps([], V.tensor_tensor, w[:, cols], act[:, cols], weight[:, tt, bass.ds(turn * TOPK + j0, BATCH)], MUL)
        nc.vector.wait_ge(*steps.last)
        for j in range(j0, j0 + BATCH):
            ins = nc.vector.tensor_scalar(diag[j], ident, w[:, j:j + 1], None, MUL)
        ins.then_inc(diags_done, 1)
        nc.tensor.wait_ge(diags_done, turn * BATCHES + (b + 1))
        for j in range(j0, j0 + BATCH):
            for h in range(2):
                ins = nc.tensor.matmul(acc[tt][h], diag[j], rows_uv[j][:, D + h * 512:D + h * 512 + 512],
                                       start=False, stop=False, skip_group_check=True)
            ins.then_inc(free[j], 1)

    def experts_of(turn, between, behind=1):
        for b in range(BATCHES):
            dots(turn, b)
            for step in between[b]:
                step()
            if b >= behind:
                add(turn, b - behind)
        for b in range(BATCHES - behind, BATCHES):
            add(turn, b)
        rewind()

    for j in range(BUFS):
        nc.tensor.sem_inc(free[j], 1)
    load_head(0)
    for step in product_keys(0):
        step()
    turned_back = Ring(core.held)
    for tt in range(NT):
        for half in range(2):
            slot, bank, read = turned_back.take()
            for k in range(4):
                t = core.pe([read], nc.tensor.transpose, bank[:, k * P:k * P + P],
                            hT[:, 4 * half + k, tt * P:tt * P + P], ident)
            s = core.act([t], nc.scalar.copy, h2[:, tt, half * 512:half * 512 + 512], bank[:, :])
            turned_back.release(slot, s)
    core.dve.wait(s)
    for step in route(0):
        step()
    rewind()
    load_head(1)
    for step in product_keys(1) + route(1):
        step()
    rewind()
    for tt in range(NT):
        for h in range(2):
            core.matmul([s], acc[tt][h], K["zeros"], h2[:, tt, h * 512:h * 512 + 512], start=True, stop=False,
                        mark=False)
    with nc.Fori(0, PEER_H - 2) as turn:
        head = turn + 2
        load_head(head)
        gather(turn)
        pk, rt = product_keys(head), route(head)
        experts_of(turn, [pk[0:1], pk[1:2], pk[2:3], rt[0:1], rt[1:2], rt[2:3], rt[3:4], rt[4:6]])
    gather(PEER_H - 2)
    experts_of(PEER_H - 2, [[]] * BATCHES)
    stored = nc.alloc_semaphore("stored")

    def finish(tt):
        for h in range(2):
            t = core.matmul([], acc[tt][h], K["zeros"], h2[:, tt, h * 512:h * 512 + 512], start=False, stop=True)
        for h in range(2):
            c = slice(h * 512, h * 512 + 512)
            core.tt([t], h2[:, tt, c], acc[tt][h], gt2[:, c], MUL)
            s = core.tt([], x[:, tt, c], x[:, tt, c], h2[:, tt, c], ADD)
        core.sp.wait(s)
        nc.sync.dma_start(out[tt * P:tt * P + P, :], x[:, tt, :]).then_inc(stored, 16)

    gather(PEER_H - 1)
    between = [[]] * BATCHES
    between[BATCHES // NT] = [lambda: finish(0)]
    experts_of(PEER_H - 1, between, behind=0)
    finish(1)
    nc.sync.wait_ge(stored, 16 * NT)


def program(nc, A, out):
    core = Core(nc)
    _, where = constants()
    x = nc.alloc_sbuf_tensor("x_sb", [P, NT, D], F32)[:]
    table = nc.alloc_sbuf_tensor("constants", [P, max(b for _, b in where.values())], F32)[:]
    K = {name: table[:, a:b] for name, (a, b) in where.items()}
    zeros = where["zeros"][0]
    K["mask2"] = table[:, zeros:zeros + 2 * P]
    K["ready"] = core.load("constants", table, A["constants"])
    x_in = core.load("x", x, A["x"].rearrange("b (t p) d -> p (b t) d", p=P))
    core.sp.wait(x_in, K["ready"])
    first_block(core, A, K, x)
    second_block(core, A, K, x, out)


_USED = ["x", "positions", "norm_g", "w_in", "b_gate", "cmp_pos", "cmp_w1", "cmp_w2", "lru_conv_w",
         "lru_conv_b", "lru_w_a", "lru_b_a", "lru_w_i", "lru_b_i", "lru_lam", "conv_dw_w",
         "conv_dw_b", "conv_ln_g", "conv_ln_b", "conv_w_pw2", "w_out", "final_g", "c_2", "ctx_2",
         "c_ctx_2", "w_ada_2", "b_ada_2", "g_norm1_2", "w_in_2", "g_cq_2", "w_uq_2", "g_ckv_2",
         "w_ukv_2", "g_qn_2", "g_kn_2", "conv_qk_2", "b_igate_2", "b_fgate_2", "g_mlstm_2",
         "w_out_2", "g_norm2_2", "w_pq_2", "sub_keys_2", "expert_u_2", "expert_v_2"]


def kernel(**inputs):
    import concourse.bacc as bacc
    from concourse.bass_utils import run_bass_kernel_spmd

    nc = bacc.Bacc("TRN2", target_bir_lowering=False, num_devices=1)
    arrays, A = {}, {}
    rows = np.concatenate([inputs["expert_u_2"][0], inputs["expert_v_2"][0]], axis=1)
    for name, a in [("constants", constants()[0]), ("experts", rows)] + [(n, inputs[n]) for n in _USED]:
        a = np.ascontiguousarray(a)
        arrays[f"in_{name}_dram"] = a
        A[name] = nc.dram_tensor(f"in_{name}_dram", a.shape, mybir.dt.from_np(a.dtype), kind="ExternalInput").ap()
    out = nc.dram_tensor("out_0_dram", (T, D), F32, kind="ExternalOutput").ap()
    program(nc, A, out)
    r = run_bass_kernel_spmd(nc, [arrays], core_ids=[0])
    return r.results[0]["out_0_dram"].reshape(1, T, D)
```
